# Optimizing a Trainium2 kernel written in Bass

```python
import math
import jax, jax.numpy as jnp
from jax import lax
import numpy as np

D_MODEL = 1024
BATCH = 1
SEQ = 128
DEPTH = 1
DEC_BATCH = 1
DEC_SEQ = 1024
PAST_LEN = 128

GRID_W = 64
N_HEADS = 8
QK_NOPE_DIM = 64
QK_ROPE_DIM = 32
V_HEAD_DIM = 64
QK_DIM = QK_NOPE_DIM + QK_ROPE_DIM
Q_LORA_RANK = 256
KV_LORA_RANK = 128
MLA_WIDTH = N_HEADS * V_HEAD_DIM
POOL_WIDTH = D_MODEL - MLA_WIDTH
POOL_WINDOWS = (2, 4, 8, 16)
N_POOL_GROUPS = len(POOL_WINDOWS)
POOL_GROUP = POOL_WIDTH // N_POOL_GROUPS
IN_COLS = Q_LORA_RANK + KV_LORA_RANK + QK_ROPE_DIM + POOL_WIDTH
D_FF = 4 * D_MODEL
Q_BLOCK = 128
ROPE_THETA = 10000.0
AXIS_ROPE = QK_ROPE_DIM // 2
N_FREQ = AXIS_ROPE // 2
EPS = 1e-6
ATTN_SCALE = 1.0 / math.sqrt(QK_DIM)

kernel_name = "hybrid_mla_pool_dit_step"

def rmsnorm(x, g):
    xf = x.astype(jnp.float32)
    y = xf * lax.rsqrt(jnp.mean(xf * xf, axis=-1, keepdims=True) + EPS)
    return (y * g.astype(jnp.float32)).astype(x.dtype)

def grid_rope_tables(n_tokens, dtype):
    rows = n_tokens // GRID_W
    row = jnp.repeat(jnp.arange(rows, dtype=jnp.float32), GRID_W)
    col = jnp.tile(jnp.arange(GRID_W, dtype=jnp.float32), rows)
    inv_freq = 1.0 / (ROPE_THETA ** (jnp.arange(N_FREQ, dtype=jnp.float32) * 2.0 / AXIS_ROPE))
    ang = jnp.stack([row[:, None] * inv_freq, col[:, None] * inv_freq], axis=1)
    return jnp.cos(ang).astype(dtype), jnp.sin(ang).astype(dtype)

def axial_rope(x, cos, sin):
    x2 = x.reshape(x.shape[:-1] + (2, 2, N_FREQ))
    a, b = x2[..., 0, :], x2[..., 1, :]
    out = jnp.stack([a * cos - b * sin, b * cos + a * sin], axis=-2)
    return out.reshape(x.shape)

def mla_attend(q_nope, q_rope, k_nope, k_rope, v):
    B, S = q_nope.shape[:2]
    nblk = S // Q_BLOCK
    qn = jnp.moveaxis(q_nope.reshape(B, nblk, Q_BLOCK, N_HEADS, QK_NOPE_DIM), 1, 0)
    qr = jnp.moveaxis(q_rope.reshape(B, nblk, Q_BLOCK, N_HEADS, QK_ROPE_DIM), 1, 0)

    def block(args):
        qn_b, qr_b = args
        s = (jnp.einsum('bqhd,bkhd->bhqk', qn_b, k_nope)
             + jnp.einsum('bqhr,bkr->bhqk', qr_b, k_rope)) * ATTN_SCALE
        p = jax.nn.softmax(s.astype(jnp.float32), axis=-1).astype(v.dtype)
        return jnp.einsum('bhqk,bkhd->bqhd', p, v)

    out = lax.map(block, (qn, qr))
    return jnp.moveaxis(out, 0, 1).reshape(B, S, MLA_WIDTH)

def pool_mix(u, w_pool, pool_scale):
    B, S, _ = u.shape
    uf = u.astype(jnp.float32)
    cs = jnp.concatenate([jnp.zeros((B, 1, POOL_WIDTH), jnp.float32), jnp.cumsum(uf, axis=1)], axis=1)
    t = jnp.arange(S)
    outs = []
    for g, w in enumerate(POOL_WINDOWS):
        lo = jnp.clip(t - w // 2, 0, S)
        hi = jnp.clip(t + w // 2, 0, S)
        seg = cs[..., g * POOL_GROUP:(g + 1) * POOL_GROUP]
        mean = (seg[:, hi] - seg[:, lo]) / (hi - lo).astype(jnp.float32)[:, None]
        outs.append(mean - uf[..., g * POOL_GROUP:(g + 1) * POOL_GROUP])
    pooled = jnp.stack(outs, axis=2).astype(u.dtype)
    mixed = jnp.einsum('bsgc,gcd->bsgd', pooled, w_pool).reshape(B, S, POOL_WIDTH)
    return mixed * pool_scale

def trunk_layer(x, mod, p, rope, ctx):
    (norm1, w_in, q_norm, w_qb, kv_norm, w_kvb, w_pool, pool_scale, w_o, norm2, w1, w2) = p
    shift1, scale1, gate1, shift2, scale2, gate2 = jnp.split(mod, 6, axis=-1)
    B, S, _ = x.shape
    h = rmsnorm(x, norm1) * (1 + scale1) + shift1
    proj = h @ w_in
    q_a, kv_a, k_r, u = jnp.split(
        proj, [Q_LORA_RANK, Q_LORA_RANK + KV_LORA_RANK, Q_LORA_RANK + KV_LORA_RANK + QK_ROPE_DIM], axis=-1)
    q = (rmsnorm(q_a, q_norm) @ w_qb).reshape(B, S, N_HEADS, QK_DIM)
    q_nope, q_rope = q[..., :QK_NOPE_DIM], q[..., QK_NOPE_DIM:]
    ckv = rmsnorm(kv_a, kv_norm)
    k_rope = k_r
    if rope is not None:
        cos, sin = rope
        q_rope = axial_rope(q_rope, cos[:, None], sin[:, None])
        k_rope = axial_rope(k_rope, cos, sin)
    keys_ckv, keys_kr = ckv, k_rope
    if ctx is not None:
        ctx_ckv, ctx_kr = ctx
        keys_ckv = jnp.concatenate([keys_ckv, ctx_ckv], axis=1)
        keys_kr = jnp.concatenate([keys_kr, ctx_kr], axis=1)
    K = keys_ckv.shape[1]
    kv = (keys_ckv @ w_kvb).reshape(B, K, N_HEADS, QK_NOPE_DIM + V_HEAD_DIM)
    k_nope, v = kv[..., :QK_NOPE_DIM], kv[..., QK_NOPE_DIM:]
    attn = mla_attend(q_nope, q_rope, k_nope, keys_kr, v)
    pooled = pool_mix(u, w_pool, pool_scale)
    x = x + gate1 * (jnp.concatenate([attn, pooled], axis=-1) @ w_o)
    h2 = rmsnorm(x, norm2) * (1 + scale2) + shift2
    x = x + gate2 * (jnp.square(jax.nn.relu(h2 @ w1)) @ w2)
    return x, ckv, k_rope

def setup_inputs(seed: int = 0) -> dict:
    key = jax.random.key(seed)
    ks = jax.random.split(key, 24)
    f = jnp.float32
    nrm = lambda k, shape, s: jax.random.normal(k, shape, f) * s
    return {
        'x_prompt': nrm(ks[0], (BATCH, SEQ, D_MODEL), 1.0),
        'x_sample': nrm(ks[1], (DEC_BATCH, DEC_SEQ, D_MODEL), 1.0),
        'cache_ckv': nrm(ks[2], (DEC_BATCH, DEPTH, PAST_LEN, KV_LORA_RANK), 1.0),
        'cache_krope': nrm(ks[3], (DEC_BATCH, DEPTH, PAST_LEN, QK_ROPE_DIM), 1.0),
        'c': nrm(ks[4], (DEC_BATCH, D_MODEL), 1.0),
        'c_ctx': nrm(ks[5], (D_MODEL,), 1.0),
        'w_ada': nrm(ks[6], (DEPTH, D_MODEL, 6 * D_MODEL), 0.5 * D_MODEL ** -0.5),
        'b_ada': nrm(ks[7], (DEPTH, 6 * D_MODEL), 0.1),
        'norm1': 1.0 + nrm(ks[8], (DEPTH, D_MODEL), 0.05),
        'w_in': nrm(ks[9], (DEPTH, D_MODEL, IN_COLS), D_MODEL ** -0.5),
        'q_norm': 1.0 + nrm(ks[10], (DEPTH, Q_LORA_RANK), 0.05),
        'w_qb': nrm(ks[11], (DEPTH, Q_LORA_RANK, N_HEADS * QK_DIM), Q_LORA_RANK ** -0.5),
        'kv_norm': 1.0 + nrm(ks[12], (DEPTH, KV_LORA_RANK), 0.05),
        'w_kvb': nrm(ks[13], (DEPTH, KV_LORA_RANK, N_HEADS * (QK_NOPE_DIM + V_HEAD_DIM)), KV_LORA_RANK ** -0.5),
        'w_pool': nrm(ks[14], (DEPTH, N_POOL_GROUPS, POOL_GROUP, POOL_GROUP), POOL_GROUP ** -0.5),
        'pool_scale': 1.0 + nrm(ks[15], (DEPTH, POOL_WIDTH), 0.05),
        'w_o': nrm(ks[16], (DEPTH, D_MODEL, D_MODEL), D_MODEL ** -0.5),
        'norm2': 1.0 + nrm(ks[17], (DEPTH, D_MODEL), 0.05),
        'w1': nrm(ks[18], (DEPTH, D_MODEL, D_FF), D_MODEL ** -0.5),
        'w2': nrm(ks[19], (DEPTH, D_FF, D_MODEL), D_FF ** -0.5),
        'final_norm': 1.0 + nrm(ks[20], (D_MODEL,), 0.05),
    }

def reference(x_prompt, x_sample, cache_ckv, cache_krope, c, c_ctx, w_ada, b_ada, norm1, w_in,
              q_norm, w_qb, kv_norm, w_kvb, w_pool, pool_scale, w_o, norm2, w1, w2, final_norm):
    n_lat = x_sample.shape[1]
    rope = grid_rope_tables(n_lat, x_sample.dtype)
    silu_c = jax.nn.silu(c)
    silu_ctx = jax.nn.silu(c_ctx)
    xc, xl = x_prompt, x_sample
    new_ckv, new_krope = [], []
    for l in range(DEPTH):
        p = (norm1[l], w_in[l], q_norm[l], w_qb[l], kv_norm[l], w_kvb[l], w_pool[l], pool_scale[l],
             w_o[l], norm2[l], w1[l], w2[l])
        mod_ctx = (silu_ctx @ w_ada[l] + b_ada[l])[None, None, :]
        mod_lat = (silu_c @ w_ada[l] + b_ada[l])[:, None, :]
        xc, ckv, krope = trunk_layer(xc, mod_ctx, p, None, None)
        new_ckv.append(ckv)
        new_krope.append(krope)
        xl, _, _ = trunk_layer(xl, mod_lat, p, rope, (cache_ckv[:, l], cache_krope[:, l]))
    y_prompt = rmsnorm(xc, final_norm)
    y_sample = rmsnorm(xl, final_norm)
    state_ckv = jnp.stack(new_ckv, axis=1)
    state_krope = jnp.stack(new_krope, axis=1)
    return (y_prompt, y_sample, state_ckv, state_krope)


_drawn_inputs = setup_inputs


def setup_inputs(seed=0):
    import zlib

    import numpy as np

    out = dict(_drawn_inputs(seed))
    spreads = {}
    factors = {'cache_ckv': 8.0, 'cache_krope': 8.0, 'q_norm': 8.0, 'pool_scale': 5.434, 'norm2': 3.567}
    for name, (base, spread) in spreads.items():
        noise = np.random.default_rng([zlib.crc32(name.encode()), seed]).standard_normal(out[name].shape)
        drawn = base * np.exp(spread * noise) if base else spread * noise
        out[name] = __import__('jax').numpy.asarray(drawn.astype(out[name].dtype))
    for name, factor in factors.items():
        out[name] = (out[name] * factor).astype(out[name].dtype)
    return out
```

```python
from contextlib import ExitStack

import concourse.bass as bass
import numpy as np
from concourse import mybir

F32 = mybir.dt.float32
F32R = mybir.dt.float32r
BF16 = mybir.dt.bfloat16
ACT = mybir.ActivationFunctionType
ALU = mybir.AluOpType
AX_X = mybir.AxisListType.X

P = 128
D = 1024
DC = D // P
LAT = 1024
LT = LAT // P
T = LT + 1
CTX = LT
CACHE = LT + 1
NTOK = T * P
NKEY = LAT + 2 * P
LKEY = LAT + P
H = 8
NOPE, ROPE, VD = 64, 32, 64
QK = NOPE + ROPE
QL, KVL = 256, 128
POOLW = 512
G = 4
WINDOWS = (2, 4, 8, 16)
EDGE = max(WINDOWS) // 2
PA = QL + KVL + 2 * ROPE
INC = PA + POOLW
FC = 4 * D // P
BLK = 3
NB = T // BLK
BN = BLK * P
EPS = 1e-6
SCALE = 1.0 / float(np.sqrt(QK))
GRID_W = 64
WH = 2 * P + NOPE
VC = 2 * VD + 2
ADA_BLOCKS = 6 * DC

C_C, C_BADA, C_N1, C_N2, C_QN, C_KVN, C_PS = 0, 16, 64, 72, 80, 82, 83
NCOL = 87
BANDS = 4 * G * P + 2 * G * EDGE


def key_col(t):
    return {CTX: LKEY, CACHE: LAT}.get(t, t * P)


class Kept:
    pass


def memory(nc, ctx, side="left"):
    def sb(name, shape, dt=F32):
        return ctx.enter_context(nc.sbuf_tensor(name, shape, dt, side=side))

    return sb


def signals(nc, ctx):
    def sem(name):
        return ctx.enter_context(nc.semaphore(name))

    return sem


def build(nc, a):
    with ExitStack() as whole:
        sb, sem = memory(nc, whole), signals(nc, whole)
        k = Kept()
        k.bank = [whole.enter_context(nc.psum_tensor(f"bank{i}", [P, 512], F32)) for i in range(8)]
        k.cols = sb("cols", [P, NCOL])
        k.ident = sb("ident", [P, P])
        k.identr = sb("identr", [P, P], F32R)
        k.nhalf = sb("nhalf", [P, 2])
        k.mod = sb("mod", [P, ADA_BLOCKS, 2])
        k.silu = sb("silu", [P, 2, DC])
        k.junk = sb("junk", [P, D], BF16)
        k.stat = sb("stat", [P, T, 6])
        k.stat2 = sb("stat2", [P, T, 6])
        k.ada_loaded = [sem(f"ada_loaded{s}") for s in range(4)]
        k.ada_done = sem("ada_done")
        handed = ExitStack()
        sbr = memory(nc, handed, "right")
        k.mixT = sbr("mixT", [P, G, NTOK])
        with ExitStack() as ab:
            sb = memory(nc, ab)
            k.ada = sb("ada", [P, 4, D])
            k.qnT = [sb(f"qnT{x}", [P, 2, NTOK], F32R) for x in "hl"]
            k.ckvT = [sb(f"ckvT{x}", [P, NKEY], F32R) for x in "hl"]
            k.krT = sb("krT", [P, NKEY])
            project_phase(nc, a, k)
            k.attn = sbr("attn", [P, T, H * VD])
            attention_phase(nc, a, k)
        with ExitStack() as rest:
            sb = memory(nc, rest)
            k.x = sb("x", [P, T, D])
            k.gates = sb("gates", [P, 2, 2, D])
            k.gain2 = sb("gain2", [P, DC, 2])
            output_phase(nc, a, k)
            handed.close()
            mlp_phase(nc, a, k)


def project_phase(nc, a, k):
    with ExitStack() as ctx:
        sb, sem = memory(nc, ctx), signals(nc, ctx)
        bank = k.bank
        xin = sb("xin", [P, 2, D])
        win = [sb(f"win{x}", [P, DC, INC], F32R) for x in "hl"]
        gain1 = sb("gain1", [P, DC, 2])
        hf = sb("hf", [P, D])
        hT = [sb(f"hT{x}", [P, 2, D], F32R) for x in "hl"]
        us = [sb(f"us{x}", [P, 4, POOLW], F32R) for x in "hl"]
        pf = sb("pf", [P, PA])
        sm = sb("sm", [P, QL + KVL + ROPE])
        cin = sb("cin", [P, KVL + ROPE])
        rt = sb("rt", [P, 2, ROPE])
        ropek = sb("ropek", [P, 2, LT, ROPE])
        bandr = sb("bandr", [P, BANDS], F32R)
        invc = sb("invc", [P, 2, G * P])
        wp = [sb(f"wp{x}", [P, G * P], F32R) for x in "hl"]
        kvn = sb("kvn", [P, KVL])
        ckvo = sb("ckvo", [P, KVL])
        es = sb("es", [P, 2 * DC])
        junk2 = sb("junk2", [P, QL + KVL], BF16)
        with ExitStack() as early:
            wraw = memory(nc, early)("wraw", [P, 2, INC])
        pooled = sb("pooled", [P, G * P])
        pT = [sb(f"pT{x}", [P, G * P], F32R) for x in "hl"]

        small_loaded, tabs_loaded = sem("small_loaded"), sem("tabs_loaded")
        invc_loaded = [sem(f"invc_loaded{v}") for v in range(2)]
        x_loaded = [sem(f"x_loaded{s}") for s in range(2)]
        raw_loaded = [sem(f"raw_loaded{s}") for s in range(2)]
        raw_hi, raw_done = sem("raw_hi"), sem("raw_done")
        identr_done = sem("identr_done")
        const_done, silu_exp, silu_done, gain_done = sem("const_done"), sem("silu_exp"), sem("silu_done"), sem("gain_done")
        silu_den = sem("silu_den")
        x_sq, x_eps, x_rs, xn_ready = sem("x_sq"), sem("x_eps"), sem("x_rs"), sem("xn_ready")
        xT_ready, hf_ready, h_hi, h_ready = sem("xT_ready"), sem("hf_ready"), sem("h_hi"), sem("h_ready")
        proj_ready, pf_ready, u_hi, u_ready = sem("proj_ready"), sem("pf_ready"), sem("u_hi"), sem("u_ready")
        qk_sq, qk_eps, qk_rs, rope_mul, sm_ready = sem("qk_sq"), sem("qk_eps"), sem("qk_rs"), sem("rope_mul"), sem("sm_ready")
        smT_ready, sm_hi, sm_done = sem("smT_ready"), sem("sm_hi"), sem("sm_done")
        band_ready, pooled_f, pooled_hi, pooled_ready = sem("band_ready"), sem("pooled_f"), sem("pooled_hi"), sem("pooled_ready")
        mix_ready, mix_done = sem("mix_ready"), sem("mix_done")
        ckvo_done, stored = sem("ckvo_done"), sem("stored")

        staged = [(a["w_in"][c], INC, win[0][:, c, :], win[1][:, c, :]) for c in range(DC)]
        third = BANDS // 3
        staged += [(a["bands"][:, i * third:(i + 1) * third], third, bandr[:, i * third:(i + 1) * third], None) for i in range(3)]
        staged += [(a["w_pool"], G * P, wp[0][:, :], wp[1][:, :])]
        NS = len(staged)
        kind = lambda t: int(t == CTX)

        def main_band(t, g):
            variant = {0: 0, LT - 1: 2, CTX: 3}.get(t, 1)
            return bandr[:, (4 * g + variant) * P:(4 * g + variant + 1) * P]

        def side_band(g, after):
            at = 4 * G * P + (2 * g + after) * EDGE
            return bandr[:, at:at + EDGE]

        with nc.Block() as block:

            @block.sync
            def _(sp):
                sp.dma_start(k.cols[:], a["cols"]).then_inc(small_loaded, 16)
                sp.dma_start(k.ident[:], a["ident"]).then_inc(small_loaded, 16)
                for t in range(2):
                    sp.dma_start(xin[:, t, :], a["x"][t]).then_inc(x_loaded[t], 16)
                n = 0
                for b in range(2 * DC):
                    if b >= 4:
                        sp.wait_ge(k.ada_done, b - 3)
                    sp.dma_start(k.ada[:, b % 4, :], a["w_ada"][b]).then_inc(k.ada_loaded[b % 4], 16)
                    if b >= 3 and n < NS:
                        if n >= 2:
                            sp.wait_ge(raw_done, n - 1)
                        src, w, _, _ = staged[n]
                        sp.dma_start(wraw[:, n % 2, 0:w], src).then_inc(raw_loaded[n % 2], 16)
                        n += 1
                assert n == NS
                sp.dma_start(ropek[:].rearrange("p a b c -> p (a b c)"), a["ropek"]).then_inc(tabs_loaded, 16)
                sp.dma_start(kvn[:], a["kv_norm_row"]).then_inc(tabs_loaded, 16)
                sp.dma_start(cin[:], a["cache"]).then_inc(tabs_loaded, 16)
                for v in range(2):
                    sp.dma_start(invc[:, v, :], a["inv_count"][v]).then_inc(invc_loaded[v], 16)
                for t in range(2, T):
                    sp.wait_ge(xT_ready, t - 1)
                    sp.dma_start(xin[:, t % 2, :], a["x"][t]).then_inc(x_loaded[t % 2], 16)
                    if t == 6:
                        sp.wait_ge(pooled_f, 1)
                        sp.dma_start(invc[:, 0, :], a["inv_count"][2]).then_inc(invc_loaded[0], 16)
                sp.wait_ge(pooled_f, LT - 1)
                sp.dma_start(invc[:, 1, :], a["inv_count"][3]).then_inc(invc_loaded[1], 16)
                sp.wait_ge(pf_ready, T)
                sp.dma_start(a["new_krope"], pf[:, QL + KVL:QL + KVL + ROPE]).then_inc(stored, 16)
                sp.wait_ge(ckvo_done, 1)
                sp.dma_start(a["new_ckv"], ckvo[:]).then_inc(stored, 16)
                sp.wait_ge(stored, 32)

            def rs_qk(pool, t):
                pool.wait_ge(qk_sq, 2 * t + 2)
                pool.tensor_scalar(k.stat2[:, t, 2:4], k.stat2[:, t, 0:2], EPS, None, ALU.add).then_inc(qk_eps, 1)
                pool.wait_ge(qk_eps, t + 1)
                pool.tensor_tensor(k.stat2[:, t, 4:6], k.stat2[:, t, 2:4], k.nhalf[:, 0:2], ALU.pow).then_inc(qk_rs, 1)

            @block.gpsimd
            def _(pool):
                pool.memset(k.nhalf[:], -0.5).then_inc(const_done, 1)
                pool.wait_ge(const_done, 1)
                for t in range(T):
                    pool.wait_ge(x_sq, t + 1)
                    pool.tensor_scalar(k.stat[:, t, 1:2], k.stat[:, t, 0:1], EPS, None, ALU.add).then_inc(x_eps, 1)
                    pool.wait_ge(x_eps, t + 1)
                    pool.tensor_tensor(k.stat[:, t, 2:3], k.stat[:, t, 1:2], k.nhalf[:, 0:1], ALU.pow).then_inc(x_rs, 1)
                    if t >= 1:
                        rs_qk(pool, t - 1)
                rs_qk(pool, T - 1)

            @block.scalar
            def _(act):
                def square(t):
                    act.wait_ge(x_loaded[t % 2], 16 * (t // 2 + 1))
                    if t:
                        act.wait_ge(x_sq, t)
                    nc.scalar.activation(k.junk[:, :], xin[:, t % 2, :], ACT.Square, scale=1.0 / 32.0,
                                         accum_out=k.stat[:, t, 0:1]).then_inc(x_sq, 1)

                def modulate(t):
                    act.wait_ge(xT_ready, t + 1)
                    if t >= 1:
                        act.wait_ge(h_ready, t)
                    for c in range(DC):
                        op = nc.scalar.activation(hf[:, c * P:(c + 1) * P], bank[c // 4][:, (c % 4) * P:(c % 4 + 1) * P],
                                                  ACT.Identity, bias=k.mod[:, c, kind(t):kind(t) + 1],
                                                  scale=gain1[:, c, kind(t):kind(t) + 1])
                    op.then_inc(hf_ready, 1)

                def projected(t):
                    pa, pu = bank[2 + 2 * (t % 2)], bank[3 + 2 * (t % 2)]
                    act.wait_ge(proj_ready, t + 1)
                    if t >= 4:
                        act.wait_ge(band_ready, t - 2)
                    nc.scalar.activation(us[0][:, t % 4, :], pu[:, 0:POOLW], ACT.Copy).then_inc(u_hi, 1)
                    if t >= 1:
                        act.wait_ge(sm_ready, t)
                    nc.scalar.activation(pf[:, :], pa[:, 0:PA], ACT.Copy).then_inc(pf_ready, 1)
                    act.wait_ge(pf_ready, t + 1)
                    if t:
                        act.wait_ge(qk_sq, 2 * t)
                    nc.scalar.activation(junk2[:, 0:QL], pf[:, 0:QL], ACT.Square, scale=1.0 / 16.0,
                                         accum_out=k.stat2[:, t, 0:1]).then_inc(qk_sq, 1)
                    nc.scalar.activation(junk2[:, QL:QL + KVL], pf[:, QL:QL + KVL], ACT.Square, scale=float(KVL) ** -0.5,
                                         accum_out=k.stat2[:, t, 1:2]).then_inc(qk_sq, 1)

                def small_hi(t, n):
                    act.wait_ge(smT_ready, n + 1)
                    at = key_col(t)
                    s = bank[6]
                    if t != CACHE:
                        for c in range(2):
                            nc.scalar.activation(k.qnT[0][:, c, t * P:(t + 1) * P], s[:, c * P:(c + 1) * P], ACT.Copy,
                                                 scale=k.cols[:, C_QN + c:C_QN + c + 1])
                    gain = 1.0 if t == CACHE else k.cols[:, C_KVN:C_KVN + 1]
                    nc.scalar.activation(k.ckvT[0][:, at:at + P], s[:, 2 * P:3 * P], ACT.Copy, scale=gain)
                    nc.scalar.activation(k.krT[NOPE:QK, at:at + P], s[0:ROPE, 3 * P:4 * P], ACT.Copy).then_inc(sm_hi, 1)

                def split_hi(n):
                    _, w, hi, lo = staged[n]
                    if lo is None:
                        return
                    act.wait_ge(raw_loaded[n % 2], 16 * (n // 2 + 1))
                    nc.scalar.activation(hi, wraw[:, n % 2, 0:w], ACT.Copy).then_inc(raw_hi, 1)

                def pooled_high(t):
                    act.wait_ge(pooled_f, t + 1)
                    if t >= 1:
                        act.wait_ge(mix_ready, t)
                    nc.scalar.activation(pT[0][:, :], pooled[:, :], ACT.Copy).then_inc(pooled_hi, 1)

                def mixed(t):
                    act.wait_ge(mix_ready, t + 1)
                    for g in range(G):
                        op = nc.scalar.activation(k.mixT[:, g, t * P:(t + 1) * P], bank[7][:, g * P:(g + 1) * P], ACT.Copy,
                                                  scale=k.cols[:, C_PS + g:C_PS + g + 1])
                    op.then_inc(mix_done, 1)

                act.wait_ge(small_loaded, 32)
                nc.scalar.activation(es[:, :], k.cols[:, C_C:C_C + 2 * DC], ACT.Exp, scale=-1.0).then_inc(silu_exp, 1)
                square(0)
                square(1)
                for n in range(NS):
                    split_hi(n)
                act.wait_ge(gain_done, 4)
                modulate(0)
                for t in range(T + 3):
                    if 0 <= t - 3 < T:
                        mixed(t - 3)
                    if t + 2 < T:
                        square(t + 2)
                    if t + 1 < T:
                        modulate(t + 1)
                    if t < T:
                        projected(t)
                    if 0 <= t - 1 < T:
                        small_hi(t - 1, t - 1)
                    if t - 1 == T:
                        small_hi(CACHE, T)
                    if 0 <= t - 2 < T:
                        pooled_high(t - 2)

            @block.vector
            def _(dve):
                def split_lo(n):
                    _, w, hi, lo = staged[n]
                    if lo is None:
                        dve.wait_ge(raw_loaded[n % 2], 16 * (n // 2 + 1))
                        nc.vector.tensor_copy(hi, wraw[:, n % 2, 0:w]).then_inc(raw_done, 1)
                    else:
                        dve.wait_ge(raw_hi, sum(x[3] is not None for x in staged[:n + 1]))
                        nc.vector.tensor_tensor(lo, wraw[:, n % 2, 0:w], hi.bitcast(F32), ALU.subtract).then_inc(raw_done, 1)

                def normed(t):
                    dve.wait_ge(x_rs, t + 1)
                    nc.vector.tensor_scalar(xin[:, t % 2, :], xin[:, t % 2, :], k.stat[:, t, 2:3], None, ALU.mult).then_inc(xn_ready, 1)

                def h_split(t):
                    dve.wait_ge(hf_ready, t + 1)
                    if t >= 2:
                        dve.wait_ge(proj_ready, t - 1)
                    nc.vector.tensor_copy(hT[0][:, t % 2, :], hf[:, :]).then_inc(h_hi, 1)
                    dve.wait_ge(h_hi, t + 1)
                    nc.vector.tensor_tensor(hT[1][:, t % 2, :], hf[:, :], hT[0][:, t % 2, :].bitcast(F32),
                                            ALU.subtract).then_inc(h_ready, 1)

                def projected(t):
                    pu = bank[3 + 2 * (t % 2)]
                    dve.wait_ge(u_hi, t + 1)
                    nc.vector.tensor_tensor(us[1][:, t % 4, :], pu[:, 0:POOLW], us[0][:, t % 4, :].bitcast(F32),
                                            ALU.subtract).then_inc(u_ready, 1)
                    kv, kr, kw = QL, QL + KVL, QL + KVL + ROPE
                    dve.wait_ge(qk_rs, t + 1)
                    if t >= 1:
                        dve.wait_ge(smT_ready, t)
                    nc.vector.tensor_scalar(sm[:, 0:QL], pf[:, 0:QL], k.stat2[:, t, 4:5], None, ALU.mult)
                    if t == CTX:
                        nc.vector.tensor_scalar(sm[:, kv:kr], pf[:, kv:kr], k.stat2[:, t, 5:6], None,
                                                ALU.mult).then_inc(rope_mul, 1)
                        nc.vector.tensor_copy(sm[:, kr:kr + ROPE], pf[:, kr:kw]).then_inc(sm_ready, 1)
                        dve.wait_ge(rope_mul, LT + 1)
                        nc.vector.tensor_tensor(ckvo[:, :], sm[:, kv:kr], kvn[:, :], ALU.mult).then_inc(ckvo_done, 1)
                        return
                    nc.vector.tensor_scalar(sm[:, kv:kr], pf[:, kv:kr], k.stat2[:, t, 5:6], None, ALU.mult)
                    nc.vector.tensor_tensor(rt[:, 0, :], pf[:, kr:kw], ropek[:, 0, t, :], ALU.mult)
                    nc.vector.tensor_tensor(rt[:, 1, :], pf[:, kw:PA], ropek[:, 1, t, :], ALU.mult).then_inc(rope_mul, 1)
                    dve.wait_ge(rope_mul, t + 1)
                    nc.vector.tensor_tensor(sm[:, kr:kr + ROPE], rt[:, 0, :], rt[:, 1, :], ALU.add).then_inc(sm_ready, 1)

                def small_lo(t, n):
                    dve.wait_ge(sm_hi, n + 1)
                    at = key_col(t)
                    s = bank[6]
                    if t != CACHE:
                        for c in range(2):
                            cut = slice(t * P, (t + 1) * P)
                            nc.vector.scalar_tensor_tensor(k.qnT[1][:, c, cut], s[:, c * P:(c + 1) * P],
                                                           k.cols[:, C_QN + c:C_QN + c + 1],
                                                           k.qnT[0][:, c, cut].bitcast(F32), ALU.mult, ALU.subtract)
                    gain = 1.0 if t == CACHE else k.cols[:, C_KVN:C_KVN + 1]
                    nc.vector.scalar_tensor_tensor(k.ckvT[1][:, at:at + P], s[:, 2 * P:3 * P], gain,
                                                   k.ckvT[0][:, at:at + P].bitcast(F32), ALU.mult,
                                                   ALU.subtract).then_inc(sm_done, 1)

                def pooled_split(t):
                    variant = {0: 0, LT - 1: 2, CTX: 3}.get(t, 1)
                    dve.wait_ge(invc_loaded[variant % 2], 16 * (variant // 2 + 1))
                    dve.wait_ge(band_ready, t + 1)
                    nc.vector.tensor_tensor(pooled[:, :], bank[7][:, :], invc[:, variant % 2, :], ALU.mult).then_inc(pooled_f, 1)
                    dve.wait_ge(pooled_hi, t + 1)
                    nc.vector.tensor_tensor(pT[1][:, :], pooled[:, :], pT[0][:, :].bitcast(F32), ALU.subtract).then_inc(pooled_ready, 1)

                dve.wait_ge(small_loaded, 32)
                nc.vector.tensor_copy(k.identr[:, :], k.ident[:, :]).then_inc(identr_done, 1)
                dve.wait_ge(silu_exp, 1)
                nc.vector.tensor_scalar(es[:, :], es[:, :], 1.0, None, ALU.add).then_inc(silu_den, 1)
                dve.wait_ge(silu_den, 1)
                nc.vector.reciprocal(es[:, :], es[:, :]).then_inc(silu_den, 1)
                dve.wait_ge(silu_den, 2)
                nc.vector.tensor_tensor(k.silu[:].rearrange("p a b -> p (a b)"), k.cols[:, C_C:C_C + 2 * DC], es[:, :],
                                        ALU.mult).then_inc(silu_done, 1)
                normed(0)
                for n in range(NS):
                    split_lo(n)
                dve.wait_ge(k.ada_done, 2 * DC)
                for j in range(2):
                    nc.vector.tensor_tensor(k.mod[:, 0:2 * DC, j], bank[7][:, 0:4 * DC].rearrange("p (b j) -> p b j", j=2)[:, :, j],
                                            k.cols[:, C_BADA:C_BADA + 2 * DC], ALU.add).then_inc(gain_done, 1)
                dve.wait_ge(gain_done, 2)
                for j in range(2):
                    nc.vector.scalar_tensor_tensor(gain1[:, :, j], k.mod[:, DC:2 * DC, j], 1.0, k.cols[:, C_N1:C_N1 + DC],
                                                   ALU.add, ALU.mult).then_inc(gain_done, 1)
                dve.wait_ge(tabs_loaded, 48)
                h_split(0)
                for t in range(T + 3):
                    if t + 1 < T:
                        normed(t + 1)
                        h_split(t + 1)
                    if t < T:
                        projected(t)
                    if 0 <= t - 1 < T:
                        small_lo(t - 1, t - 1)
                    if t - 1 == T:
                        small_lo(CACHE, T)
                    if 0 <= t - 2 < T:
                        pooled_split(t - 2)

            @block.tensor
            def _(pe):
                def turn_x(t):
                    pe.wait_ge(xn_ready, t + 1)
                    if t >= 1:
                        pe.wait_ge(hf_ready, t)
                    for c in range(DC):
                        op = nc.tensor.transpose(bank[c // 4][:, (c % 4) * P:(c % 4 + 1) * P], xin[:, t % 2, c * P:(c + 1) * P], k.ident[:, :])
                    op.then_inc(xT_ready, 1)

                def project(t):
                    pa, pu = bank[2 + 2 * (t % 2)], bank[3 + 2 * (t % 2)]
                    pe.wait_ge(h_ready, t + 1)
                    if t >= 2:
                        pe.wait_ge(pf_ready, t - 1)
                        pe.wait_ge(u_ready, t - 1)
                    for c in range(DC):
                        for x, y in ((0, 0), (0, 1), (1, 0)):
                            w = hT[x][:, t % 2, c * P:(c + 1) * P]
                            first, last = c == 0 and (x, y) == (0, 0), c == DC - 1 and (x, y) == (1, 0)
                            nc.tensor.matmul(pa[:, 0:PA], w, win[y][:, c, 0:PA], start=first, stop=last)
                            op = nc.tensor.matmul(pu[:, 0:POOLW], w, win[y][:, c, PA:INC], start=first, stop=last)
                    op.then_inc(proj_ready, 1)

                def turn_small(t, n):
                    s = bank[6]
                    if n >= 1:
                        pe.wait_ge(sm_done, n)
                    if t == CACHE:
                        pe.wait_ge(tabs_loaded, 48)
                        nc.tensor.transpose(s[:, 2 * P:3 * P], cin[:, 0:KVL], k.ident[:, :])
                        nc.tensor.transpose(s[0:ROPE, 3 * P:4 * P], cin[:, KVL:KVL + ROPE], k.ident[:, :]).then_inc(smT_ready, 1)
                        return
                    pe.wait_ge(sm_ready, t + 1)
                    for c in range(3):
                        nc.tensor.transpose(s[:, c * P:(c + 1) * P], sm[:, c * P:(c + 1) * P], k.ident[:, :])
                    nc.tensor.transpose(s[0:ROPE, 3 * P:4 * P], sm[:, QL + KVL:QL + KVL + ROPE], k.ident[:, :]).then_inc(smT_ready, 1)

                def pool_windows(t):
                    after = t < LT - 1
                    pe.wait_ge(u_ready, t + 1 + after)
                    if t >= 1:
                        pe.wait_ge(mix_done, t)
                    first = True
                    for g in range(G):
                        cut = slice(g * P, (g + 1) * P)
                        for x in range(2):
                            op = nc.tensor.matmul(bank[7][:, g * P:(g + 1) * P], us[x][:, t % 4, cut], main_band(t, g),
                                                  start=first, stop=False, skip_group_check=True)
                            first = False
                            if 0 < t < LT:
                                op = nc.tensor.matmul(bank[7][:, g * P:g * P + EDGE], us[x][:, (t - 1) % 4, cut], side_band(g, 0),
                                                      start=False, stop=False, skip_group_check=True)
                            if after:
                                op = nc.tensor.matmul(bank[7][:, (g + 1) * P - EDGE:(g + 1) * P], us[x][:, (t + 1) % 4, cut],
                                                      side_band(g, 1), start=False, stop=False, skip_group_check=True)
                    op.then_inc(band_ready, 1)

                def mix(t):
                    pe.wait_ge(pooled_ready, t + 1)
                    for g in range(G):
                        cut = slice(g * P, (g + 1) * P)
                        for i, (x, y) in enumerate(((0, 0), (0, 1), (1, 0))):
                            op = nc.tensor.matmul(bank[7][:, cut], wp[x][:, cut], pT[y][:, cut], start=i == 0, stop=i == 2)
                    op.then_inc(mix_ready, 1)

                pe.wait_ge(small_loaded, 32)
                turn_x(0)
                pe.wait_ge(silu_done, 1)
                for b in range(2 * DC):
                    modulation_block(nc, pe, k, b, bank[7][:, 2 * b:2 * b + 2], b // 4 + 1, k.ada[:, b % 4, :])
                pe.wait_ge(gain_done, 2)
                for t in range(T + 3):
                    if t + 1 < T:
                        turn_x(t + 1)
                    if 0 <= t - 3 < T:
                        mix(t - 3)
                    if t == 0:
                        pe.wait_ge(raw_done, NS)
                    if t < T:
                        project(t)
                    if 0 <= t - 1 < T:
                        turn_small(t - 1, t - 1)
                    if t - 1 == T:
                        turn_small(CACHE, T)
                    if 0 <= t - 2 < T:
                        pool_windows(t - 2)


def modulation_block(nc, pe, k, b, out, use, w):
    pe.wait_ge(k.ada_loaded[b % 4], 16 * use)
    for c in range(DC):
        op = nc.tensor.matmul(out, w[:, c * P:(c + 1) * P], k.silu[:, :, c], start=c == 0, stop=c == DC - 1)
    op.then_inc(k.ada_done, 1)


def attention_phase(nc, a, k):
    with ExitStack() as ctx:
        sb, sem = memory(nc, ctx), signals(nc, ctx)
        bank = k.bank
        V = sb("V", [P, LT + 2, H, VC], F32R)
        kT = [[sb(f"kT{x}{j}", [P, NKEY], F32R) for x in "hl"] for j in range(2)]
        qT = [[sb(f"qT{x}{j}", [P, NTOK], F32R) for x in "hl"] for j in range(2)]
        whr = [sb(f"whr{j}", [P, WH]) for j in range(2)]
        wh = [[sb(f"wh{x}{j}", [P, WH], F32R) for x in "hl"] for j in range(2)]
        wv = [sb(f"wv{x}", [P, H * VD], F32R) for x in "hl"]
        wvr = sb("wvr", [P, H * VD])
        ropeq = sb("ropeq", [P, NTOK])
        q1, q2, qf = sb("q1", [P, BN]), sb("q2", [P, BN]), sb("qf", [P, BN])
        pm, mx, nm = sb("pm", [P, T, 3]), sb("mx", [P, T]), sb("nm", [P, T, 2], F32R)
        pexp = [sb(f"pexp{i}", [P, 512]) for i in range(2)]
        phi = [sb(f"phi{i}", [P, 512], F32R) for i in range(2)]
        plo = [sb(f"plo{i}", [P, 512], F32R) for i in range(2)]
        rden, lowv = sb("rden", [P, 4]), sb("lowv", [P, 4, VD])

        tabq_loaded, wv_loaded = sem("tabq_loaded"), sem("wv_loaded")
        head_loaded = [sem(f"head_loaded{j}") for j in range(2)]
        wv_hi, wv_ready, v_hi, setup_a, setup_d = sem("wv_hi"), sem("wv_ready"), sem("v_hi"), sem("setup_a"), sem("setup_d")
        wh_hi, wh_ready = sem("wh_hi"), sem("wh_ready")
        ring_filled, ring_freed = sem("ring_filled"), sem("ring_freed")
        q_nope, q_full, q_hi, q_lo, k_hi = sem("q_nope"), sem("q_full"), sem("q_hi"), sem("q_lo"), sem("k_hi")
        max_done, nm_ready, mrow_ready = sem("max_done"), sem("nm_ready"), sem("mrow_ready")
        st_filled, p_exp, p_hi, p_lo = sem("st_filled"), sem("p_exp"), sem("p_hi"), sem("p_lo")
        pv_done, pv_inv, pv_low, pv_read = sem("pv_done"), sem("pv_inv"), sem("pv_low"), sem("pv_read")
        ada_read = sem("ada_read")

        NV = LT + 2
        Q0, K0, S0 = 0, 3, 6
        M0 = S0 + 3 * LT + 1
        RU = M0 + 3
        KCUT = ((0, 512), (512, 1024), (1024, NKEY))
        HALF = LAT // 2
        KT = LKEY // P
        MS = 2 * KT + 1
        assert RU % 3 == 1 and NV % 3 == 1 and MS % 2 == 1

        def ring_bank(li):
            return bank[li % 3] if li < RU else None

        def ring_free(pe, h, li):
            before = {0: -1, 1: -3, 2: -2}.get(li, li - 3)
            pe.wait_ge(ring_freed, h * RU + (NV + before + 1))

        def ring_full(eng, h, li):
            eng.wait_ge(ring_filled, h * RU + (NV + li + 1))

        def step(s):
            if s == MS - 1:
                return LAT, 1, LKEY, CACHE, 0, True
            half, kt = divmod(s, KT)
            return half * HALF, HALF // P, kt * P, kt, kt, kt == KT - 1

        SIDE = [[] for _ in range(MS)]
        for li in range(M0):
            SIDE[min(li * 14 // M0, MS - 1)].append(li)
        SIDE[16] += [M0, M0 + 1, M0 + 2]

        with nc.Block() as block:

            @block.sync
            def _(sp):
                def load_head(h, j):
                    sp.dma_start(whr[j][:, :], a["w_head"][h]).then_inc(head_loaded[j], 16)

                def load_ada(h):
                    for s in range(4):
                        sp.dma_start(k.ada[:, s, :], a["w_ada"][4 * h + (2 * DC + s)]).then_inc(k.ada_loaded[s], 16)

                sp.dma_start(wvr[:], a["w_v"]).then_inc(wv_loaded, 16)
                sp.dma_start(ropeq[NOPE:P, :], a["ropeq"]).then_inc(tabq_loaded, 16)
                load_head(0, 0)
                load_head(1, 1)
                load_ada(0)
                for h in range(1, H):
                    sp.wait_ge(k.ada_done, 2 * DC + 4 * h)
                    load_ada(h)
                    if h + 1 < H:
                        sp.wait_ge(wh_ready, h)
                        load_head(h + 1, (h + 1) % 2)

            @block.gpsimd
            def _(pool):
                def queries(h, j):
                    for c in range(3):
                        cut = slice(c * BN, (c + 1) * BN)
                        pool.wait_ge(ring_freed, h * RU + (NV + c + 1))
                        nc.gpsimd.tensor_tensor(qf[NOPE:QK, :], q1[NOPE:QK, :], q2[NOPE:QK, :], ALU.add).then_inc(q_full, 1)
                        pool.wait_ge(q_hi, 3 * h + c + 1)
                        nc.gpsimd.tensor_tensor(qT[j][1][0:QK, cut], qf[0:QK, :], qT[j][0][0:QK, cut].bitcast(F32),
                                                ALU.subtract).then_inc(q_lo, 1)

                for h in range(H):
                    queries(h, h % 2)

            @block.scalar
            def _(act):
                def side(h, j, li):
                    if li == Q0:
                        act.wait_ge(head_loaded[j], 16 * (h // 2 + 1))
                        nc.scalar.activation(wh[j][0][:, :], whr[j][:, :], ACT.Copy).then_inc(wh_hi, 1)
                    if li < K0:
                        c = li
                        ring_full(act, h, li)
                        act.wait_ge(q_lo, 3 * h + c)
                        nc.scalar.activation(qf[0:NOPE, :], bank[li % 3][0:NOPE, 0:BN], ACT.Copy).then_inc(q_nope, 1)
                        act.wait_ge(q_full, 3 * h + c + 1)
                        act.wait_ge(q_nope, 3 * h + c + 1)
                        nc.scalar.activation(qT[j][0][0:QK, c * BN:(c + 1) * BN], qf[0:QK, :], ACT.Copy).then_inc(q_hi, 1)
                    elif li < S0:
                        lo, hi = KCUT[li - K0]
                        ring_full(act, h, li)
                        nc.scalar.activation(kT[j][0][0:NOPE, lo:hi], bank[li % 3][0:NOPE, 0:hi - lo], ACT.Copy).then_inc(k_hi, 1)

                def main(h, j, s):
                    _, nq, _, _, _, _ = step(s)
                    n, g = nq * P, MS * h + s
                    slot = (s + j) % 2
                    act.wait_ge(st_filled, g + 1)
                    act.wait_ge(p_lo, g + 1)
                    nc.scalar.activation(pexp[slot][:, 0:n], bank[3 + slot][:, 0:n], ACT.Exp, scale=SCALE).then_inc(p_exp, 1)
                    act.wait_ge(p_exp, g + 3)
                    act.wait_ge(pv_done, g + 1)
                    nc.scalar.activation(phi[slot][:, 0:n], pexp[slot][:, 0:n], ACT.Copy).then_inc(p_hi, 1)

                act.sem_inc(p_exp, 2)
                act.wait_ge(wv_loaded, 16)
                nc.scalar.activation(wv[0][:, :], wvr[:, :], ACT.Copy).then_inc(wv_hi, 1)
                for j in range(2):
                    nc.scalar.activation(kT[j][0][NOPE:QK, :], k.krT[NOPE:QK, :], ACT.Copy).then_inc(setup_a, 1)
                for v in range(NV):
                    act.wait_ge(ring_filled, v + 1)
                    nc.scalar.activation(V[:, v, :, 0:VD], bank[v % 3][:, :].rearrange("p (h d) -> p h d", h=H),
                                         ACT.Copy).then_inc(v_hi, 1)
                for li in range(RU):
                    side(0, 0, li)
                for h in range(H):
                    for s in range(MS):
                        main(h, h % 2, s)
                        if h + 1 < H:
                            for li in SIDE[s]:
                                side(h + 1, (h + 1) % 2, li)

            @block.vector
            def _(dve):
                def side(h, j, li):
                    b = bank[li % 3]
                    if li == Q0:
                        dve.wait_ge(wh_hi, h + 1)
                        nc.vector.tensor_tensor(wh[j][1][:, :], whr[j][:, :], wh[j][0][:, :].bitcast(F32),
                                                ALU.subtract).then_inc(wh_ready, 1)
                    ring_full(dve, h, li)
                    if li < K0:
                        c = li
                        cut = slice(c * BN, (c + 1) * BN)
                        dve.wait_ge(q_full, 3 * h + c)
                        nc.vector.tensor_tensor(q1[NOPE:QK, :], b[QK:P, 0:BN], ropeq[QK:P, cut], ALU.mult)
                        dve.wait_ge(q_nope, 3 * h + c + 1)
                        nc.vector.tensor_tensor(q2[NOPE:QK, :], b[NOPE:QK, 0:BN], ropeq[NOPE:QK, cut], ALU.mult).then_inc(ring_freed, 1)
                    elif li < S0:
                        lo, hi = KCUT[li - K0]
                        dve.wait_ge(k_hi, 3 * h + li - K0 + 1)
                        nc.vector.tensor_tensor(kT[j][1][0:NOPE, lo:hi], b[0:NOPE, 0:hi - lo], kT[j][0][0:NOPE, lo:hi].bitcast(F32),
                                                ALU.subtract).then_inc(ring_freed, 1)
                    elif li < M0:
                        qt, c = divmod(li - S0, 3)
                        n = BN if qt < LT else P
                        nc.vector.reduce_max(pm[:, qt, c:c + 1], b[:, 0:n], AX_X).then_inc(ring_freed, 1)
                        if li == M0 - 1:
                            dve.wait_ge(ring_freed, h * RU + (NV + M0))
                            nc.vector.tensor_reduce(mx[:, :], pm[:, :, :], AX_X, ALU.max).then_inc(max_done, 1)
                            dve.wait_ge(max_done, h + 1)
                            nc.vector.tensor_scalar(nm[:, :, 0], mx[:, :], -1.0, None, ALU.mult).then_inc(nm_ready, 1)
                            dve.wait_ge(nm_ready, 2 * h + 1)
                            nc.vector.scalar_tensor_tensor(nm[:, :, 1], mx[:, :], -1.0, nm[:, :, 0].bitcast(F32), ALU.mult,
                                                           ALU.subtract).then_inc(nm_ready, 1)
                    else:
                        c = li - M0
                        nc.vector.tensor_scalar(qT[j][0][QK:QK + 2, c * BN:(c + 1) * BN], b[0:2, 0:BN], 1.0, None,
                                                ALU.mult).then_inc(ring_freed, 1)

                def main(h, j, s):
                    _, nq, _, _, _, _ = step(s)
                    n, g = nq * P, MS * h + s
                    slot = (s + j) % 2
                    dve.wait_ge(p_hi, g + 1)
                    nc.vector.tensor_tensor(plo[slot][:, 0:n], pexp[slot][:, 0:n], phi[slot][:, 0:n].bitcast(F32),
                                            ALU.subtract).then_inc(p_lo, 1)

                def values(h, s):
                    q0, nq, _, _, _, last = step(s)
                    if not last:
                        return
                    grp = s // KT
                    n = 9 * h + 4 * grp
                    dve.wait_ge(pv_done, MS * h + s + 3)
                    for i in range((nq + 1) // 2):
                        w = min(2, nq - 2 * i)
                        op = nc.vector.reciprocal(rden[:, 2 * i:2 * i + w], bank[5 + i][:, 0:2 * VC].rearrange("p (t c) -> p t c", c=VC)[:, 0:w, VD])
                    op.then_inc(pv_inv, 1)
                    dve.wait_ge(pv_inv, 3 * h + grp + 1)
                    for i in range(nq):
                        b = bank[5 + i // 2][:, (i % 2) * VC:(i % 2 + 1) * VC]
                        op = nc.vector.tensor_scalar(lowv[:, i, :], b[:, VD + 2:VC], rden[:, i:i + 1], None, ALU.mult)
                    op.then_inc(pv_low, 1)
                    dve.wait_ge(pv_low, 3 * h + grp + 1)
                    for i in range(nq):
                        b = bank[5 + i // 2][:, (i % 2) * VC:(i % 2 + 1) * VC]
                        op = nc.vector.scalar_tensor_tensor(k.attn[:, q0 // P + i, bass.ds(h * VD, VD)], b[:, 0:VD], rden[:, i:i + 1],
                                                            lowv[:, i, :], ALU.mult, ALU.add)
                    op.then_inc(pv_read, 1)

                dve.sem_inc(p_lo, 2)
                nc.vector.memset(pm[:, LT, :], -3.0e38).then_inc(setup_d, 1)
                for j in range(2):
                    nc.vector.memset(kT[j][0][QK:QK + 2, :].bitcast(F32), 1.0).then_inc(setup_d, 1)
                nc.vector.memset(V[:, :, :, VD:VD + 2].bitcast(F32), 1.0).then_inc(setup_d, 1)
                dve.wait_ge(wv_hi, 1)
                nc.vector.tensor_tensor(wv[1][:, :], wvr[:, :], wv[0][:, :].bitcast(F32), ALU.subtract).then_inc(wv_ready, 1)
                for j in range(2):
                    dve.wait_ge(setup_a, j + 1)
                    nc.vector.tensor_tensor(kT[j][1][NOPE:QK, :], k.krT[NOPE:QK, :], kT[j][0][NOPE:QK, :].bitcast(F32),
                                            ALU.subtract).then_inc(setup_d, 1)
                for v in range(NV):
                    dve.wait_ge(v_hi, v + 1)
                    nc.vector.tensor_tensor(V[:, v, :, VD + 2:VC], bank[v % 3][:, :].rearrange("p (h d) -> p h d", h=H),
                                            V[:, v, :, 0:VD].bitcast(F32), ALU.subtract).then_inc(ring_freed, 1)
                dve.wait_ge(tabq_loaded, 16)
                for li in range(RU):
                    side(0, 0, li)
                for h in range(H):
                    for s in range(MS):
                        main(h, h % 2, s)
                        if s >= 1:
                            values(h, s - 1)
                        if s == 8:
                            dve.wait_ge(k.ada_done, 2 * DC + 4 * h + 4)
                            at = 4 * h + 2 * DC
                            for j in range(2):
                                nc.vector.tensor_tensor(k.mod[:, bass.ds(at, 4), j],
                                                        bank[7][:, 0:8].rearrange("p (b j) -> p b j", j=2)[:, :, j],
                                                        k.cols[:, bass.ds(C_BADA + at, 4)], ALU.add).then_inc(ada_read, 1)
                        if h + 1 < H:
                            for li in SIDE[s]:
                                side(h + 1, (h + 1) % 2, li)
                    values(h, MS - 1)

            @block.tensor
            def _(pe):
                def side(h, j, li):
                    b = bank[li % 3]
                    if li == Q0:
                        pe.wait_ge(wh_ready, h + 1)
                    if li == S0:
                        pe.wait_ge(q_lo, 3 * h + 3)
                        pe.wait_ge(ring_freed, h * RU + (NV + S0))
                    if li == M0:
                        pe.wait_ge(nm_ready, 2 * h + 2)
                    ring_free(pe, h, li)
                    if li < K0:
                        cut = slice(li * BN, (li + 1) * BN)
                        n = 0
                        for c in range(2):
                            for x, y in ((0, 0), (0, 1), (1, 0)):
                                op = nc.tensor.matmul(b[:, 0:BN], wh[j][x][:, c * P:(c + 1) * P], k.qnT[y][:, c, cut],
                                                      start=n == 0, stop=n == 5)
                                n += 1
                    elif li < S0:
                        lo, hi = KCUT[li - K0]
                        for n, (x, y) in enumerate(((0, 0), (0, 1), (1, 0))):
                            op = nc.tensor.matmul(b[0:NOPE, 0:hi - lo], wh[j][x][:, 2 * P:WH], k.ckvT[y][:, lo:hi],
                                                  start=n == 0, stop=n == 2)
                    elif li < M0:
                        qt, c = divmod(li - S0, 3)
                        lo, w = (c * BN, BN) if qt < LT else (LKEY, P)
                        for n, (x, y) in enumerate(((0, 0), (0, 1), (1, 0))):
                            op = nc.tensor.matmul(b[:, 0:w], qT[j][x][0:QK, qt * P:(qt + 1) * P], kT[j][y][0:QK, lo:lo + w],
                                                  start=n == 0, stop=n == 2)
                    else:
                        for i in range(3):
                            op = nc.tensor.matmul(b[0:2, i * P:(i + 1) * P], nm[:, 3 * (li - M0) + i, :], k.identr[:, :],
                                                  start=True, stop=True)
                    op.then_inc(ring_filled, 1)

                def scores(h, j, s):
                    q0, nq, k0, _, _, _ = step(s)
                    g = MS * h + s
                    slot = (s + j) % 2
                    n = nq * P
                    if s == 0:
                        pe.wait_ge(ring_freed, h * RU + (NV + RU))
                    pe.wait_ge(p_exp, g + 1)
                    b = bank[3 + slot][:, 0:n]
                    nc.tensor.matmul(b, kT[j][0][0:QK + 2, k0:k0 + P], qT[j][0][0:QK + 2, q0:q0 + n], start=True, stop=False)
                    nc.tensor.matmul(b, kT[j][0][0:QK, k0:k0 + P], qT[j][1][0:QK, q0:q0 + n], start=False, stop=False)
                    nc.tensor.matmul(b, kT[j][1][0:QK, k0:k0 + P], qT[j][0][0:QK, q0:q0 + n], start=False, stop=True).then_inc(st_filled, 1)

                def values(h, j, s):
                    _, nq, _, vt, n, last = step(s)
                    g = MS * h + s
                    slot = (s + j) % 2
                    pe.wait_ge(p_lo, g + 3)
                    if n == 0:
                        pe.wait_ge(pv_read, 3 * h + s // KT)
                    for i in range(nq):
                        b = bank[5 + i // 2]
                        at = (i % 2) * VC
                        cut = slice(i * P, (i + 1) * P)
                        nc.tensor.matmul(b[:, at:at + VC], phi[slot][:, cut], V[:, vt, h, :], start=n == 0 and i % 2 == 0,
                                         stop=False, skip_group_check=True)
                        op = nc.tensor.matmul(b[:, at:at + VD + 2], plo[slot][:, cut], V[:, vt, h, 0:VD + 2], start=False,
                                              stop=False, skip_group_check=True)
                    op.then_inc(pv_done, 1)

                pe.sem_inc(pv_done, 2)
                pe.wait_ge(wv_ready, 1)
                for v in range(NV):
                    at = key_col({LT: CACHE, LT + 1: CTX}.get(v, v))
                    if v >= 3:
                        pe.wait_ge(ring_freed, v - 2)
                    for n, (x, y) in enumerate(((0, 0), (0, 1), (1, 0))):
                        op = nc.tensor.matmul(bank[v % 3][:, :], k.ckvT[x][:, at:at + P], wv[y][:, :], start=n == 0, stop=n == 2)
                    op.then_inc(ring_filled, 1)
                pe.wait_ge(setup_d, 6)
                for li in range(RU):
                    side(0, 0, li)
                for h in range(H):
                    for s in range(MS):
                        scores(h, h % 2, s)
                        if h + 1 < H:
                            for li in SIDE[s]:
                                side(h + 1, (h + 1) % 2, li)
                        if s >= 1:
                            values(h, h % 2, s - 1)
                        if s == 4:
                            pe.wait_ge(ada_read, 2 * h)
                            for i in range(4):
                                modulation_block(nc, pe, k, i, bank[7][:, 2 * i:2 * i + 2], h + 5, k.ada[:, i, :])
                    values(h, h % 2, MS - 1)


def output_phase(nc, a, k):
    with ExitStack() as ctx:
        sb, sem = memory(nc, ctx), signals(nc, ctx)
        bank = k.bank
        wo = [sb(f"wo{x}", [P, DC, D], F32R) for x in "hl"]
        wor = sb("wor", [P, 2, D])
        aT = [sb(f"aT{x}", [P, 2, 4 * P], F32R) for x in "hl"]
        mT = [sb(f"mT{x}", [P, 2, 4 * P], F32R) for x in "hl"]
        add = sb("add", [P, 2, D])
        x_loaded = [sem(f"res_loaded{i}") for i in range(3)]
        wo_loaded = [sem(f"wo_loaded{i}") for i in range(2)]
        wo_hi, wo_ready = sem("wo_hi"), sem("wo_ready")
        gate_ready, gate_done, gain2_done = sem("gate_ready"), sem("gate_done"), sem("gain2_done")
        aT_ready, a_hi, a_ready, m_hi, m_ready = sem("aT_ready"), sem("a_hi"), sem("a_ready"), sem("m_hi"), sem("m_ready")
        out_ready, gated, x2_ready, x2_sq, x2_eps = sem("out_ready"), sem("gated"), sem("x2_ready"), sem("x2_sq"), sem("x2_eps")
        k.x2_rs = sem("x2_rs")
        GATE = {0: 2 * DC, 1: 5 * DC}
        kind = lambda t: int(t == CTX)

        with nc.Block() as block:

            @block.sync
            def _(sp):
                for n in range(DC):
                    if n >= 2:
                        sp.wait_ge(wo_ready, n - 1)
                    sp.dma_start(wor[:, n % 2, :], a["w_o"][n]).then_inc(wo_loaded[n % 2], 16)
                    if n % 3 == 1:
                        i = n // 3
                        sp.dma_start(k.x[:, 3 * i:3 * i + 3, :], a["x"][3 * i:3 * i + 3].rearrange("t p d -> p t d")).then_inc(x_loaded[i], 16)

            @block.gpsimd
            def _(pool):
                def mixer(t):
                    cut = slice(t * P, (t + 1) * P)
                    if t >= 2:
                        pool.wait_ge(out_ready, t - 1)
                    v = [m[:, t % 2, :].rearrange("p (g n) -> p g n", g=G) for m in mT]
                    nc.gpsimd.tensor_copy(v[0], k.mixT[:, :, cut]).then_inc(m_hi, 1)
                    pool.wait_ge(m_hi, t + 1)
                    nc.gpsimd.tensor_tensor(v[1], k.mixT[:, :, cut], v[0].bitcast(F32), ALU.subtract).then_inc(m_ready, 1)

                def residual(t):
                    pool.wait_ge(gated, t + 1)
                    pool.wait_ge(x_loaded[t // 3], 16)
                    nc.gpsimd.tensor_tensor(k.x[:, t, :], k.x[:, t, :], add[:, t % 2, :], ALU.add).then_inc(x2_ready, 1)
                    pool.wait_ge(x2_sq, t + 1)
                    nc.gpsimd.tensor_scalar(k.stat[:, t, 4:5], k.stat[:, t, 3:4], EPS, None, ALU.add).then_inc(x2_eps, 1)
                    pool.wait_ge(x2_eps, t + 1)
                    nc.gpsimd.tensor_tensor(k.stat[:, t, 5:6], k.stat[:, t, 4:5], k.nhalf[:, 0:1], ALU.pow).then_inc(k.x2_rs, 1)

                mixer(0)
                for t in range(T):
                    if t + 1 < T:
                        mixer(t + 1)
                    residual(t)

            @block.scalar
            def _(act):
                def turned(t):
                    act.wait_ge(aT_ready, t + 1)
                    if t >= 2:
                        act.wait_ge(out_ready, t - 1)
                    nc.scalar.activation(aT[0][:, t % 2, :], bank[t % 2][:, :], ACT.Copy).then_inc(a_hi, 1)

                for n in range(DC):
                    act.wait_ge(wo_loaded[n % 2], 16 * (n // 2 + 1))
                    nc.scalar.activation(wo[0][:, n, :], wor[:, n % 2, :], ACT.Copy).then_inc(wo_hi, 1)
                    if n < 4:
                        g, j = divmod(n, 2)
                        act.wait_ge(gate_ready, n + 1)
                        for i in range(2):
                            op = nc.scalar.activation(k.gates[:, g, j, i * 512:(i + 1) * 512], bank[6 + i][:, :], ACT.Copy)
                        op.then_inc(gate_done, 1)
                turned(0)
                for t in range(T):
                    if t + 1 < T:
                        turned(t + 1)
                    act.wait_ge(x2_ready, t + 1)
                    if t:
                        act.wait_ge(x2_sq, t)
                    nc.scalar.activation(k.junk[:, :], k.x[:, t, :], ACT.Square, scale=1.0 / 32.0,
                                         accum_out=k.stat[:, t, 3:4]).then_inc(x2_sq, 1)

            @block.vector
            def _(dve):
                def turned(t):
                    dve.wait_ge(a_hi, t + 1)
                    nc.vector.tensor_tensor(aT[1][:, t % 2, :], bank[t % 2][:, :], aT[0][:, t % 2, :].bitcast(F32),
                                            ALU.subtract).then_inc(a_ready, 1)

                for j in range(2):
                    nc.vector.scalar_tensor_tensor(k.gain2[:, :, j], k.mod[:, 4 * DC:5 * DC, j], 1.0, k.cols[:, C_N2:C_N2 + DC],
                                                   ALU.add, ALU.mult).then_inc(gain2_done, 1)
                for n in range(DC):
                    dve.wait_ge(wo_hi, n + 1)
                    nc.vector.tensor_tensor(wo[1][:, n, :], wor[:, n % 2, :], wo[0][:, n, :].bitcast(F32),
                                            ALU.subtract).then_inc(wo_ready, 1)
                dve.wait_ge(gate_done, 4)
                turned(0)
                for t in range(T):
                    if t + 1 < T:
                        turned(t + 1)
                    dve.wait_ge(out_ready, t + 1)
                    if t >= 2:
                        dve.wait_ge(x2_ready, t - 1)
                    for i in range(2):
                        cut = slice(i * 512, (i + 1) * 512)
                        op = nc.vector.tensor_tensor(add[:, t % 2, cut], bank[2 + 2 * (t % 2) + i][:, :], k.gates[:, 0, kind(t), cut], ALU.mult)
                    op.then_inc(gated, 1)

            @block.tensor
            def _(pe):
                def turn(t):
                    if t >= 2:
                        pe.wait_ge(a_ready, t - 1)
                    for c in range(4):
                        op = nc.tensor.transpose(bank[t % 2][:, c * P:(c + 1) * P], k.attn[:, t, c * P:(c + 1) * P], k.ident[:, :])
                    op.then_inc(aT_ready, 1)

                turn(0)
                for n in range(4):
                    g, j = divmod(n, 2)
                    if n >= 1:
                        pe.wait_ge(gate_done, n)
                    for c in range(DC):
                        b = GATE[g] + c
                        op = nc.tensor.matmul(bank[6 + c // 4][:, (c % 4) * P:(c % 4 + 1) * P],
                                              k.mod[:, b, j:j + 1].to_broadcast([P, P]), k.ident[:, :], start=True, stop=True)
                    op.then_inc(gate_ready, 1)
                for t in range(T):
                    if t + 1 < T:
                        turn(t + 1)
                    pe.wait_ge(a_ready, t + 1)
                    pe.wait_ge(m_ready, t + 1)
                    if t >= 2:
                        pe.wait_ge(gated, t - 1)
                    b = [bank[2 + 2 * (t % 2) + i] for i in range(2)]
                    for c in range(DC):
                        if t == 0:
                            pe.wait_ge(wo_ready, c + 1)
                        src = aT if c < 4 else mT
                        for x, y in ((0, 0), (0, 1), (1, 0)):
                            first, last = c == 0 and (x, y) == (0, 0), c == DC - 1 and (x, y) == (1, 0)
                            for i in range(2):
                                op = nc.tensor.matmul(b[i][:, :], src[x][:, t % 2, (c % 4) * P:(c % 4 + 1) * P],
                                                      wo[y][:, c, i * 512:(i + 1) * 512], start=first, stop=last)
                    op.then_inc(out_ready, 1)


def mlp_phase(nc, a, k):
    with ExitStack() as ctx:
        sb, sem = memory(nc, ctx), signals(nc, ctx)
        bank = k.bank
        xn = sb("xn2", [P, 2, D])
        hf = sb("hf2", [P, D])
        h2 = [[sb(f"h2{x}{j}", [P, DC, BN], F32R) for x in "hl"] for j in range(2)]
        raw = [[sb(f"w{m}raw{s}", [P, D]) for s in range(4)] for m in (1, 2)]
        w = [[[sb(f"w{m}{x}{s}", [P, D], F32R) for x in "hl"] for s in range(2)] for m in (1, 2)]
        relu = [sb(f"relu{s}", [P, BN]) for s in range(2)]
        sq = [sb(f"sq{s}", [P, BN]) for s in range(2)]
        rT = [[sb(f"rT{x}{s}", [P, BN], F32R) for x in "hl"] for s in range(2)]
        add = sb("add2", [P, 2, 512])
        fnorm = sb("fnorm", [P, D])
        loaded = [[sem(f"w{m}_loaded{s}") for s in range(4)] for m in (1, 2)]
        w_hi = [sem("w1_hi"), sem("w2_hi")]
        w_ready = [sem("w1_ready"), sem("w2_ready")]
        fn_loaded = sem("fn_loaded")
        xn_ready, xT_ready, hf_ready, h_hi, h_ready = sem("xn2_ready"), sem("x2T_ready"), sem("hf2_ready"), sem("h2_hi"), sem("h2_ready")
        hid_done, relu_done, sq_done, r_hi, r_ready = sem("hid_done"), sem("relu_done"), sem("sq_done"), sem("r_hi"), sem("r_ready")
        down_done, out_gated, out_added = sem("down_done"), sem("out_gated"), sem("out_added")
        y_sq, y_eps, y_rs, y_ready = sem("y_sq"), sem("y_eps"), sem("y_rs"), sem("y_ready")
        stored = [sem(f"y_stored{s}") for s in range(2)]
        kind = lambda t: int(t == CTX)

        with nc.Block() as block:

            @block.sync
            def _(sp):
                def load(g, f, j):
                    for m in range(2):
                        sp.dma_start(raw[m][j][:, :], a[("w1", "w2")[m]][f]).then_inc(loaded[m][j], 16)

                sp.dma_start(fnorm[:], a["final_norm_row"]).then_inc(fn_loaded, 16)
                for j in range(4):
                    load(j, j, j)
                for b in range(NB):
                    with sp.Fori(1 if b == 0 else 0, FC // 4) as i:
                        for j in range(4):
                            sp.wait_ge(w_ready[0], 4 * i + (FC * b + j - 3))
                            sp.wait_ge(w_ready[1], 4 * i + (FC * b + j - 3))
                            load(None, 4 * i + j, j)

            @block.gpsimd
            def _(pool):
                for b in range(NB):
                    tiles = range(BLK * b, BLK * (b + 1))
                    for t in tiles:
                        for i in range(2):
                            n = 2 * t + i
                            cut = slice(i * 512, (i + 1) * 512)
                            pool.wait_ge(out_gated, n + 1)
                            nc.gpsimd.tensor_tensor(k.x[:, t, cut], k.x[:, t, cut], add[:, i, :], ALU.add).then_inc(out_added, 1)
                    for t in tiles:
                        pool.wait_ge(y_sq, t + 1)
                        nc.gpsimd.tensor_scalar(k.stat2[:, t, 1:2], k.stat2[:, t, 0:1], EPS, None, ALU.add).then_inc(y_eps, 1)
                        pool.wait_ge(y_eps, t + 1)
                        nc.gpsimd.tensor_tensor(k.stat2[:, t, 2:3], k.stat2[:, t, 1:2], k.nhalf[:, 0:1], ALU.pow).then_inc(y_rs, 1)
                    for t in tiles:
                        pool.wait_ge(y_ready, t + 1)
                        pool.dma_start(a["y"][t], k.x[:, t, :]).then_inc(stored[t % 2], 16)
                pool.wait_ge(stored[0], 16 * ((T + 1) // 2))
                pool.wait_ge(stored[1], 16 * (T // 2))

            @block.scalar
            def _(act):
                def split_hi(m, slot, rslot, use):
                    act.wait_ge(loaded[m][rslot], use)
                    nc.scalar.activation(w[m][slot][0][:, :], raw[m][rslot][:, :], ACT.Copy).then_inc(w_hi[m], 1)

                def modulate(t):
                    act.wait_ge(xT_ready, t + 1)
                    if t >= 1:
                        act.wait_ge(h_ready, t)
                    for c in range(DC):
                        op = nc.scalar.activation(hf[:, c * P:(c + 1) * P], bank[6 + c // 4][:, (c % 4) * P:(c % 4 + 1) * P],
                                                  ACT.Identity, bias=k.mod[:, 3 * DC + c, kind(t):kind(t) + 1],
                                                  scale=k.gain2[:, c, kind(t):kind(t) + 1])
                    op.then_inc(hf_ready, 1)

                split_hi(0, 0, 0, 16)
                split_hi(0, 1, 1, 16)
                split_hi(1, 0, 0, 16)
                for t in range(BLK):
                    modulate(t)

                def step(b, i, j, first=False):
                    g = 4 * i + (FC * b + j)
                    s = j % 2
                    act.wait_ge(hid_done, g + 1)
                    nc.scalar.activation(relu[s][:, :], bank[6 + s][:, 0:BN], ACT.Relu).then_inc(relu_done, 1)
                    split_hi(0, s, (j + 2) % 4, 16 * i + 16 * ((FC // 4) * b + (j + 2) // 4 + 1))
                    act.wait_ge(sq_done, g + 1)
                    if b or j or not first:
                        act.wait_ge(down_done, g)
                    nc.scalar.activation(rT[s][0][:, :], sq[s][:, :], ACT.Copy).then_inc(r_hi, 1)
                    split_hi(1, 1 - s, (j + 1) % 4, 16 * i + 16 * ((FC // 4) * b + (j + 1) // 4 + 1))

                def last_step(g):
                    s = g % 2
                    act.wait_ge(hid_done, g + 1)
                    nc.scalar.activation(relu[s][:, :], bank[6 + s][:, 0:BN], ACT.Relu).then_inc(relu_done, 1)
                    act.wait_ge(sq_done, g + 1)
                    act.wait_ge(down_done, g)
                    nc.scalar.activation(rT[s][0][:, :], sq[s][:, :], ACT.Copy).then_inc(r_hi, 1)
                    if g + 1 < NB * FC:
                        split_hi(1, 1 - s, (g + 1) % 4, 16 * ((g + 1) // 4 + 1))

                for b in range(NB):
                    final = b == NB - 1
                    if b == 0:
                        for j in range(4):
                            step(b, 0, j, first=True)
                    with act.Fori(1 if b == 0 else 0, FC // 4 - final) as i:
                        for j in range(4):
                            step(b, i, j)
                    if final:
                        for j in range(2):
                            step(b, FC // 4 - 1, j)
                        for g in range(NB * FC - 2, NB * FC):
                            last_step(g)
                    else:
                        for t in range(BLK * (b + 1), BLK * (b + 2)):
                            modulate(t)
                    for t in range(BLK * b, BLK * (b + 1)):
                        act.wait_ge(out_added, 2 * t + 2)
                        if t:
                            act.wait_ge(y_sq, t)
                        nc.scalar.activation(k.junk[:, :], k.x[:, t, :], ACT.Square, scale=1.0 / 32.0,
                                             accum_out=k.stat2[:, t, 0:1]).then_inc(y_sq, 1)

            @block.vector
            def _(dve):
                def split_lo(m, slot, rslot, n):
                    dve.wait_ge(w_hi[m], n + 1)
                    nc.vector.tensor_tensor(w[m][slot][1][:, :], raw[m][rslot][:, :], w[m][slot][0][:, :].bitcast(F32),
                                            ALU.subtract).then_inc(w_ready[m], 1)

                def normed(t):
                    dve.wait_ge(k.x2_rs, t + 1)
                    if t >= 2:
                        dve.wait_ge(xT_ready, t - 1)
                    nc.vector.tensor_scalar(xn[:, t % 2, :], k.x[:, t, :], k.stat[:, t, 5:6], None, ALU.mult).then_inc(xn_ready, 1)

                def h_split(t):
                    j, i = (t // BLK) % 2, t % BLK
                    cut = slice(i * P, (i + 1) * P)
                    v = hf[:, :].rearrange("p (c n) -> p c n", c=DC)
                    dve.wait_ge(hf_ready, t + 1)
                    nc.vector.tensor_copy(h2[j][0][:, :, cut], v).then_inc(h_hi, 1)
                    dve.wait_ge(h_hi, t + 1)
                    nc.vector.tensor_tensor(h2[j][1][:, :, cut], v, h2[j][0][:, :, cut].bitcast(F32), ALU.subtract).then_inc(h_ready, 1)

                def prepare(b):
                    t0 = BLK * b
                    normed(t0)
                    for t in range(t0, t0 + BLK):
                        if t + 1 < t0 + BLK:
                            normed(t + 1)
                        h_split(t)

                def step(b, i, j, w1_too=True, w2_too=True):
                    g = 4 * i + (FC * b + j)
                    s = j % 2
                    dve.wait_ge(relu_done, g + 1)
                    nc.vector.tensor_tensor(sq[s][:, :], relu[s][:, :], relu[s][:, :], ALU.mult).then_inc(sq_done, 1)
                    if w1_too:
                        split_lo(0, s, (j + 2) % 4, g + 2)
                    dve.wait_ge(r_hi, g + 1)
                    nc.vector.tensor_tensor(rT[s][1][:, :], sq[s][:, :], rT[s][0][:, :].bitcast(F32), ALU.subtract).then_inc(r_ready, 1)
                    if w2_too:
                        split_lo(1, 1 - s, (j + 1) % 4, g + 1)

                def finish(b):
                    dve.wait_ge(down_done, FC * (b + 1))
                    for t in range(BLK * b, BLK * (b + 1)):
                        for i in range(2):
                            n = 2 * t + i
                            cut = slice(i * 512, (i + 1) * 512)
                            if n >= 2:
                                dve.wait_ge(out_added, n - 1)
                            nc.vector.tensor_tensor(add[:, i, :], bank[2 * (t % BLK) + i][:, :], k.gates[:, 1, kind(t), cut],
                                                    ALU.mult).then_inc(out_gated, 1)
                    for t in range(BLK * b, BLK * (b + 1)):
                        dve.wait_ge(y_rs, t + 1)
                        nc.vector.scalar_tensor_tensor(k.x[:, t, :], k.x[:, t, :], k.stat2[:, t, 2:3], fnorm[:, :], ALU.mult,
                                                       ALU.mult).then_inc(y_ready, 1)

                split_lo(0, 0, 0, 0)
                split_lo(0, 1, 1, 1)
                split_lo(1, 0, 0, 0)
                prepare(0)
                dve.wait_ge(fn_loaded, 16)
                for b in range(NB):
                    final = b == NB - 1
                    with dve.Fori(0, FC // 4 - final) as i:
                        for j in range(4):
                            step(b, i, j)
                    if final:
                        for j in range(4):
                            step(b, FC // 4 - 1, j, w1_too=j < 2, w2_too=j < 3)
                    else:
                        prepare(b + 1)
                    finish(b)

            @block.tensor
            def _(pe):
                def turn(t):
                    pe.wait_ge(xn_ready, t + 1)
                    if t % BLK:
                        pe.wait_ge(hf_ready, t)
                    elif t:
                        pe.wait_ge(relu_done, FC * (t // BLK))
                    for c in range(DC):
                        op = nc.tensor.transpose(bank[6 + c // 4][:, (c % 4) * P:(c % 4 + 1) * P], xn[:, t % 2, c * P:(c + 1) * P], k.ident[:, :])
                    op.then_inc(xT_ready, 1)

                def up(b, g, s, first=False):
                    pe.wait_ge(w_ready[0], g + 1)
                    if not first:
                        pe.wait_ge(relu_done, g - 1)
                    n = 0
                    for c in range(DC):
                        for x, y_ in ((0, 0), (0, 1), (1, 0)):
                            op = nc.tensor.matmul(bank[6 + s][:, 0:BN], w[0][s][x][:, c * P:(c + 1) * P], h2[b % 2][y_][:, c, :],
                                                  start=n == 0, stop=n == 3 * DC - 1)
                            n += 1
                    op.then_inc(hid_done, 1)

                def down(g, s, first=False, last=False):
                    pe.wait_ge(w_ready[1], g + 1)
                    pe.wait_ge(r_ready, g + 1)
                    for i in range(BLK):
                        for n, (x, y_) in enumerate(((0, 0), (0, 1), (1, 0))):
                            for half in range(2):
                                op = nc.tensor.matmul(bank[2 * i + half][:, :], rT[s][x][:, i * P:(i + 1) * P],
                                                      w[1][s][y_][:, half * 512:(half + 1) * 512],
                                                      start=first and n == 0, stop=last and n == 2, skip_group_check=True)
                    op.then_inc(down_done, 1)

                for t in range(BLK):
                    turn(t)
                for b in range(NB):
                    g0 = FC * b
                    pe.wait_ge(h_ready, BLK * (b + 1))
                    up(b, g0, 0, first=True)
                    up(b, g0 + 1, 1, first=True)
                    if b:
                        pe.wait_ge(out_gated, 2 * BLK * b)
                    down(g0, 0, first=True)
                    with pe.Fori(1, FC // 2) as i:
                        up(b, 2 * i + g0, 0)
                        down(2 * i + (g0 - 1), 1)
                        up(b, 2 * i + (g0 + 1), 1)
                        down(2 * i + g0, 0)
                    if b + 1 < NB:
                        turn(BLK * (b + 1))
                    down(g0 + FC - 1, 1, last=True)
                    if b + 1 < NB:
                        turn(BLK * (b + 1) + 1)
                        turn(BLK * (b + 1) + 2)


def rope_tables():
    inv = (1.0 / (np.float32(10000.0) ** (np.arange(8, dtype=np.float32) * np.float32(2.0) / np.float32(16.0)))).astype(np.float32)
    n = np.arange(LAT)
    pos = np.stack([n // GRID_W, n % GRID_W], 1).astype(np.float32)
    ang = (pos[:, :, None] * inv).astype(np.float32)
    cos, sin = np.cos(ang).astype(np.float32), np.sin(ang).astype(np.float32)
    cos = np.stack([cos, cos], 2).reshape(LAT, ROPE)
    sin = np.stack([-sin, sin], 2).reshape(LAT, ROPE)
    return cos, sin


def pool_tables():
    def cnt(t, w, n):
        return min(t + w // 2, n) - max(t - w // 2, 0)

    bands = np.zeros((P, BANDS), np.float32)
    inv = np.zeros((4, G, P), np.float32)
    for g, w in enumerate(WINDOWS):
        for v, (t0, n) in enumerate(((0, LAT), (P, LAT), (LAT - P, LAT), (0, P))):
            for t in range(P):
                m = bands[:, (4 * g + v) * P + t]
                m[max(t - w // 2, 0):min(t + w // 2, P)] = 1.0
                m[t] -= cnt(t0 + t, w, n)
                inv[v, g, t] = 1.0 / cnt(t0 + t, w, n)
        at = 4 * G * P + 2 * g * EDGE
        for t in range(EDGE):
            for s in range(P):
                if s - P >= t - w // 2:
                    bands[s, at + t] = 1.0
                if s + P < P - EDGE + t + w // 2:
                    bands[s, at + EDGE + t] = 1.0
    return bands, np.broadcast_to(inv.reshape(4, 1, G * P), (4, P, G * P))


def kernel(x_prompt, x_sample, cache_ckv, cache_krope, c, c_ctx, w_ada, b_ada, norm1, w_in, q_norm, w_qb,
           kv_norm, w_kvb, w_pool, pool_scale, w_o, norm2, w1, w2, final_norm):
    import concourse.bacc as bacc
    from concourse.bass_utils import run_bass_kernel_spmd

    def ar(v):
        return np.asarray(v)

    def feature_cols(v):
        return ar(v).reshape(-1, P).T

    swap = np.arange(ROPE).reshape(2, 2, 8)[:, ::-1].reshape(-1)
    wi = ar(w_in)[0]
    kr0 = QL + KVL
    wi = np.concatenate([wi[:, :kr0 + ROPE], wi[:, kr0:kr0 + ROPE][:, swap], wi[:, kr0 + ROPE:]], 1)
    wq = ar(w_qb)[0].reshape(2, P, H, QK)
    wq = np.concatenate([wq, wq[..., NOPE:][..., swap]], -1).transpose(2, 1, 0, 3).reshape(H, P, 2 * P)
    wkv = ar(w_kvb)[0].reshape(P, H, NOPE + VD)
    cos, sin = rope_tables()
    bands, inv = pool_tables()
    one, zero = np.ones((P, ROPE), np.float32), np.zeros((P, ROPE), np.float32)
    arrays = {
        "x": np.concatenate([ar(x_sample)[0], ar(x_prompt)[0]], 0).reshape(T, P, D),
        "cols": np.concatenate([feature_cols(v) for v in (c, c_ctx, b_ada, norm1, norm2, q_norm, kv_norm, pool_scale)], 1),
        "ident": np.eye(P, dtype=np.float32),
        "w_ada": ar(w_ada)[0].reshape(DC, P, ADA_BLOCKS, P).transpose(2, 1, 0, 3).reshape(ADA_BLOCKS, P, D),
        "w_in": wi.reshape(DC, P, INC),
        "w_head": np.concatenate([wq, wkv[:, :, :NOPE].transpose(1, 0, 2)], -1),
        "w_v": wkv[:, :, NOPE:].reshape(P, H * VD),
        "w_pool": ar(w_pool)[0].transpose(1, 0, 2).reshape(P, G * P),
        "bands": bands,
        "inv_count": inv,
        "ropek": np.stack([cos.reshape(LT, P, ROPE), sin.reshape(LT, P, ROPE)]).transpose(2, 0, 1, 3).reshape(P, -1),
        "ropeq": np.concatenate([np.concatenate([cos, one]).T, np.concatenate([sin, zero]).T], 0),
        "kv_norm_row": np.broadcast_to(ar(kv_norm)[0], (P, KVL)),
        "cache": np.concatenate([ar(cache_ckv)[0, 0], ar(cache_krope)[0, 0]], 1),
        "w_o": ar(w_o)[0].reshape(DC, P, D),
        "w1": ar(w1)[0].reshape(DC, P, FC, P).transpose(2, 1, 0, 3).reshape(FC, P, D),
        "w2": ar(w2)[0].reshape(FC, P, D),
        "final_norm_row": np.broadcast_to(ar(final_norm), (P, D)),
    }
    arrays = {n: np.ascontiguousarray(v) for n, v in arrays.items()}
    nc = bacc.Bacc("TRN2", target_bir_lowering=False, num_devices=1)
    aps = {n: nc.dram_tensor(f"in_{n}", v.shape, mybir.dt.from_np(v.dtype), kind="ExternalInput").ap() for n, v in arrays.items()}
    for n, shape in (("y", (T, P, D)), ("new_ckv", (P, KVL)), ("new_krope", (P, ROPE))):
        aps[n] = nc.dram_tensor(f"out_{n}", shape, F32, kind="ExternalOutput").ap()
    build(nc, aps)
    got = run_bass_kernel_spmd(nc, [{f"in_{n}": v for n, v in arrays.items()}], core_ids=[0]).results[0]
    y = got["out_y"]
    return (y[CTX][None], y[:LT].reshape(1, LAT, D), got["out_new_ckv"][None, None], got["out_new_krope"][None, None])
```

```python
from contextlib import ExitStack

import concourse.bass as bass
import numpy as np
from concourse import mybir

F32 = mybir.dt.float32
F32R = mybir.dt.float32r
BF16 = mybir.dt.bfloat16
ACT = mybir.ActivationFunctionType
ALU = mybir.AluOpType
AX_X = mybir.AxisListType.X

P = 128
D = 1024
DC = D // P
LAT = 1024
LT = LAT // P
T = LT + 1
CTX = LT
CACHE = LT + 1
NTOK = T * P
NKEY = LAT + 2 * P
LKEY = LAT + P
H = 8
NOPE, ROPE, VD = 64, 32, 64
QK = NOPE + ROPE
QL, KVL = 256, 128
POOLW = 512
G = 4
WINDOWS = (2, 4, 8, 16)
EDGE = max(WINDOWS) // 2
PA = QL + KVL + 2 * ROPE
INC = PA + POOLW
FC = 4 * D // P
BLK = 3
NB = T // BLK
BN = BLK * P
EPS = 1e-6
SCALE = 1.0 / float(np.sqrt(QK))
GRID_W = 64
WH = 2 * P + NOPE
VC = 2 * VD + 2
ADA_BLOCKS = 6 * DC

C_C, C_BADA, C_N1, C_N2, C_QN, C_KVN, C_PS = 0, 16, 64, 72, 80, 82, 83
NCOL = 87
BANDS = 4 * G * P + 2 * G * EDGE


def key_col(t):
    return {CTX: LKEY, CACHE: LAT}.get(t, t * P)


class Kept:
    pass


def memory(nc, ctx, side="left"):
    def sb(name, shape, dt=F32):
        return ctx.enter_context(nc.sbuf_tensor(name, shape, dt, side=side))

    return sb


def signals(nc, ctx):
    def sem(name):
        return ctx.enter_context(nc.semaphore(name))

    return sem


def build(nc, a):
    with ExitStack() as whole:
        sb, sem = memory(nc, whole), signals(nc, whole)
        k = Kept()
        k.bank = [whole.enter_context(nc.psum_tensor(f"bank{i}", [P, 512], F32)) for i in range(8)]
        k.cols = sb("cols", [P, NCOL])
        k.ident = sb("ident", [P, P])
        k.identr = sb("identr", [P, P], F32R)
        k.nhalf = sb("nhalf", [P, 2])
        k.mod = sb("mod", [P, ADA_BLOCKS, 2])
        k.silu = sb("silu", [P, DC, 4], F32R)
        k.pick = sb("pick", [4, 2])
        k.stat = sb("stat", [P, T, 6])
        k.stat2 = sb("stat2", [P, T, 6])
        handed = ExitStack()
        sbr = memory(nc, handed, "right")
        k.mixT = sbr("mixT", [P, G, NTOK])
        with ExitStack() as ab:
            sb = memory(nc, ab)
            k.qnT = [sb(f"qnT{x}", [P, 2, NTOK], F32R) for x in "hl"]
            k.ckvT = [sb(f"ckvT{x}", [P, NKEY], F32R) for x in "hl"]
            k.krT = sb("krT", [P, NKEY])
            project_phase(nc, a, k)
            k.attn = sbr("attn", [P, H * VD // P, NTOK])
            attention_phase(nc, a, k)
        with ExitStack() as rest:
            sb = memory(nc, rest)
            k.x = sb("x", [P, T, D])
            k.junk = sb("junk2", [P, D], BF16)
            k.gain2 = sb("gain2", [P, DC, 2])
            k.xn = sb("xn", [P, 2, D])
            k.hf = sb("h2f", [P, 2, D // 2])
            k.h2 = [[sb(f"h2{x}0", [P, DC, BN], F32R) for x in "hl"]]
            k.xn_ready, k.xT_ready, k.hf_ready = sem("xn2_ready"), sem("x2T_ready"), sem("h2f_ready")
            k.h_hi, k.h_ready = sem("h2_hi"), sem("h2_ready")
            output_phase(nc, a, k)
            handed.close()
            mlp_phase(nc, a, k)


class Modulation:

    def __init__(self, nc, a, k, sb, sem, first, raw_slots, part_slots):
        self.nc, self.a, self.k, self.first = nc, a, k, first
        self.nr, self.np = raw_slots, part_slots
        self.raw = sb(f"ada_raw_{first}", [P, raw_slots, D])
        self.parts = [sb(f"ada{x}_{first}", [P, part_slots, D], F32R) for x in "hl"]
        self.rows = sb(f"ada_rows_{first}", [4, 512 * (4 if first == 0 else 1)])
        self.loaded = [sem(f"ada_loaded{s}_{first}") for s in range(raw_slots)]
        self.hi_done = sem(f"ada_hi_{first}")
        self.ready = sem(f"ada_ready_{first}")
        self.done = sem(f"ada_done_{first}")

    def load(self, sp, n):
        if n >= self.nr:
            sp.wait_ge(self.ready, n - self.nr + 1)
        s = n % self.nr
        sp.dma_start(self.raw[:, s, :], self.a["w_ada"][self.first + n]).then_inc(self.loaded[s], 16)

    def high(self, act, n):
        act.wait_ge(self.loaded[n % self.nr], 16 * (n // self.nr + 1))
        if n >= self.np:
            act.wait_ge(self.done, n - self.np + 1)
        self.nc.scalar.activation(self.parts[0][:, n % self.np, :], self.raw[:, n % self.nr, :],
                                  ACT.Copy).then_inc(self.hi_done, 1)

    def low(self, eng, n):
        eng.wait_ge(self.hi_done, n + 1)
        eng.tensor_tensor(self.parts[1][:, n % self.np, :], self.raw[:, n % self.nr, :],
                          self.parts[0][:, n % self.np, :].bitcast(F32), ALU.subtract).then_inc(self.ready, 1)

    def multiply(self, pe, n, out):
        pe.wait_ge(self.ready, n + 1)
        for c in range(2):
            for x in range(2):
                op = self.nc.tensor.matmul(out[0:4, :], self.k.silu[:, 2 * (n % 4) + c, :],
                                           self.parts[x][:, n % self.np, c * 512:(c + 1) * 512],
                                           start=n % 4 == 0 and c == 0 and x == 0, stop=n % 4 == 3 and c == 1 and x == 1,
                                           skip_group_check=True)
        op.then_inc(self.done, 1)


def project_phase(nc, a, k):
    with ExitStack() as ctx:
        sb, sem = memory(nc, ctx), signals(nc, ctx)
        bank = k.bank
        xin = sb("xin", [P, 2, D])
        k.junk = sb("junk", [P, D], BF16)
        win = [sb(f"win{x}", [P, DC, INC], F32R) for x in "hl"]
        gain1 = sb("gain1", [P, DC, 2])
        hf = sb("hf", [P, D])
        pf = sb("pf", [P, PA])
        sm = sb("sm", [P, QL + KVL + ROPE])
        cin = sb("cin", [P, KVL + ROPE])
        rt = sb("rt", [P, 2, ROPE])
        ropek = sb("ropek", [P, 2, LT, ROPE])
        bandr = sb("bandr", [P, BANDS], F32R)
        invc = sb("invc", [P, 2, G * P])
        wp = [sb(f"wp{x}", [P, G * P], F32R) for x in "hl"]
        kvn = sb("kvn", [P, KVL])
        ckvo = sb("ckvo", [P, KVL])
        es, sf = sb("es", [P, 2 * DC]), sb("sf", [P, 2 * DC])
        junk2 = sb("junk_qk", [P, QL + KVL], BF16)
        with ExitStack() as early:
            wraw = memory(nc, early)("wraw", [P, 2, INC])
            mod = Modulation(nc, a, k, memory(nc, early), sem, 0, 4, 2)
        hT = [sb(f"hT{x}", [P, 2, D], F32R) for x in "hl"]
        us = [sb(f"us{x}", [P, 4, POOLW], F32R) for x in "hl"]
        pooled = sb("pooled", [P, G * P])
        pT = [sb(f"pT{x}", [P, G * P], F32R) for x in "hl"]

        small_loaded, tabs_loaded = sem("small_loaded"), sem("tabs_loaded")
        invc_loaded = [sem(f"invc_loaded{v}") for v in range(2)]
        x_loaded = [sem(f"x_loaded{s}") for s in range(2)]
        raw_loaded = [sem(f"raw_loaded{s}") for s in range(2)]
        raw_hi, raw_done = sem("raw_hi"), sem("raw_done")
        identr_done = sem("identr_done")
        const_done, silu_exp, silu_done, gain_done = sem("const_done"), sem("silu_exp"), sem("silu_done"), sem("gain_done")
        silu_den, silu_f, rows_done, cols_done = sem("silu_den"), sem("silu_f"), sem("rows_done"), sem("cols_done")
        x_sq, x_eps, x_rs, xn_ready = sem("x_sq"), sem("x_eps"), sem("x_rs"), sem("xn_ready")
        xT_ready, hf_ready, h_hi, h_ready = sem("xT_ready"), sem("hf_ready"), sem("h_hi"), sem("h_ready")
        proj_ready, pf_ready, u_hi, u_ready = sem("proj_ready"), sem("pf_ready"), sem("u_hi"), sem("u_ready")
        qk_sq, qk_eps, qk_rs, rope_mul, sm_ready = sem("qk_sq"), sem("qk_eps"), sem("qk_rs"), sem("rope_mul"), sem("sm_ready")
        smT_ready, sm_hi, sm_done = sem("smT_ready"), sem("sm_hi"), sem("sm_done")
        band_ready, pooled_f, pooled_hi, pooled_ready = sem("band_ready"), sem("pooled_f"), sem("pooled_hi"), sem("pooled_ready")
        mix_ready, mix_done = sem("mix_ready"), sem("mix_done")
        ckvo_done, stored = sem("ckvo_done"), sem("stored")

        staged = [(a["w_in"][c], INC, win[0][:, c, :], win[1][:, c, :]) for c in range(DC)]
        third = BANDS // 3
        staged += [(a["bands"][:, i * third:(i + 1) * third], third, bandr[:, i * third:(i + 1) * third], None) for i in range(3)]
        staged += [(a["w_pool"], G * P, wp[0][:, :], wp[1][:, :])]
        NS = len(staged)
        kind = lambda t: int(t == CTX)

        def main_band(t, g):
            variant = {0: 0, LT - 1: 2, CTX: 3}.get(t, 1)
            return bandr[:, (4 * g + variant) * P:(4 * g + variant + 1) * P]

        def side_band(g, after):
            at = 4 * G * P + (2 * g + after) * EDGE
            return bandr[:, at:at + EDGE]

        with nc.Block() as block:

            @block.sync
            def _(sp):
                sp.dma_start(k.cols[:], a["cols"]).then_inc(small_loaded, 16)
                sp.dma_start(k.ident[:], a["ident"]).then_inc(small_loaded, 16)
                sp.dma_start(k.pick[:], a["pick"]).then_inc(small_loaded, 16)
                for t in range(2):
                    sp.dma_start(xin[:, t, :], a["x"][t]).then_inc(x_loaded[t], 16)
                n = 0
                for b in range(2 * DC):
                    mod.load(sp, b)
                    if b >= 3 and n < NS:
                        if n >= 2:
                            sp.wait_ge(raw_done, n - 1)
                        src, w, _, _ = staged[n]
                        sp.dma_start(wraw[:, n % 2, 0:w], src).then_inc(raw_loaded[n % 2], 16)
                        n += 1
                assert n == NS
                sp.dma_start(ropek[:].rearrange("p a b c -> p (a b c)"), a["ropek"]).then_inc(tabs_loaded, 16)
                sp.dma_start(kvn[:], a["kv_norm_row"]).then_inc(tabs_loaded, 16)
                sp.dma_start(cin[:], a["cache"]).then_inc(tabs_loaded, 16)
                for v in range(2):
                    sp.dma_start(invc[:, v, :], a["inv_count"][v]).then_inc(invc_loaded[v], 16)
                for t in range(2, T):
                    sp.wait_ge(xT_ready, t - 1)
                    sp.dma_start(xin[:, t % 2, :], a["x"][t]).then_inc(x_loaded[t % 2], 16)
                    if t == 6:
                        sp.wait_ge(pooled_f, 1)
                        sp.dma_start(invc[:, 0, :], a["inv_count"][2]).then_inc(invc_loaded[0], 16)
                sp.wait_ge(pooled_f, LT - 1)
                sp.dma_start(invc[:, 1, :], a["inv_count"][3]).then_inc(invc_loaded[1], 16)
                sp.wait_ge(pf_ready, T)
                sp.dma_start(a["new_krope"], pf[:, QL + KVL:QL + KVL + ROPE]).then_inc(stored, 16)
                sp.wait_ge(ckvo_done, 1)
                sp.dma_start(a["new_ckv"], ckvo[:]).then_inc(stored, 16)
                sp.wait_ge(stored, 32)

            def rs_qk(pool, t):
                pool.wait_ge(qk_sq, 2 * t + 2)
                pool.tensor_scalar(k.stat2[:, t, 2:4], k.stat2[:, t, 0:2], EPS, None, ALU.add).then_inc(qk_eps, 1)
                pool.wait_ge(qk_eps, t + 1)
                pool.tensor_tensor(k.stat2[:, t, 4:6], k.stat2[:, t, 2:4], k.nhalf[:, 0:2], ALU.pow).then_inc(qk_rs, 1)

            def rs_x(pool, t):
                pool.wait_ge(x_sq, t + 1)
                pool.tensor_scalar(k.stat[:, t, 1:2], k.stat[:, t, 0:1], EPS, None, ALU.add).then_inc(x_eps, 1)
                pool.wait_ge(x_eps, t + 1)
                pool.tensor_tensor(k.stat[:, t, 2:3], k.stat[:, t, 1:2], k.nhalf[:, 0:1], ALU.pow).then_inc(x_rs, 1)

            @block.gpsimd
            def _(pool):
                def split_lo(n):
                    _, w, hi, lo = staged[n]
                    if lo is None:
                        pool.wait_ge(raw_loaded[n % 2], 16 * (n // 2 + 1))
                        nc.gpsimd.tensor_copy(hi, wraw[:, n % 2, 0:w]).then_inc(raw_done, 1)
                    else:
                        pool.wait_ge(raw_hi, sum(x[3] is not None for x in staged[:n + 1]))
                        nc.gpsimd.tensor_tensor(lo, wraw[:, n % 2, 0:w], hi.bitcast(F32), ALU.subtract).then_inc(raw_done, 1)

                pool.memset(k.nhalf[:], -0.5).then_inc(const_done, 1)
                pool.wait_ge(const_done, 1)
                for t in range(2):
                    rs_x(pool, t)
                for n in range(NS):
                    split_lo(n)
                for t in range(T):
                    if t + 2 < T:
                        rs_x(pool, t + 2)
                    rs_qk(pool, t)

            @block.scalar
            def _(act):
                def square(t):
                    act.wait_ge(x_loaded[t % 2], 16 * (t // 2 + 1))
                    if t:
                        act.wait_ge(x_sq, t)
                    nc.scalar.activation(k.junk[:, :], xin[:, t % 2, :], ACT.Square, scale=1.0 / 32.0,
                                         accum_out=k.stat[:, t, 0:1]).then_inc(x_sq, 1)

                def modulate(t):
                    act.wait_ge(xT_ready, t + 1)
                    if t >= 1:
                        act.wait_ge(h_ready, t)
                    for c in range(DC):
                        op = nc.scalar.activation(hf[:, c * P:(c + 1) * P], bank[c // 4][:, (c % 4) * P:(c % 4 + 1) * P],
                                                  ACT.Identity, bias=k.mod[:, c, kind(t):kind(t) + 1],
                                                  scale=gain1[:, c, kind(t):kind(t) + 1])
                    op.then_inc(hf_ready, 1)

                def projected(t):
                    pa, pu = bank[2 + 2 * (t % 2)], bank[3 + 2 * (t % 2)]
                    act.wait_ge(proj_ready, t + 1)
                    if t >= 4:
                        act.wait_ge(band_ready, t - 2)
                    nc.scalar.activation(us[0][:, t % 4, :], pu[:, 0:POOLW], ACT.Copy).then_inc(u_hi, 1)
                    if t >= 1:
                        act.wait_ge(sm_ready, t)
                    nc.scalar.activation(pf[:, :], pa[:, 0:PA], ACT.Copy).then_inc(pf_ready, 1)
                    act.wait_ge(pf_ready, t + 1)
                    if t:
                        act.wait_ge(qk_sq, 2 * t)
                    nc.scalar.activation(junk2[:, 0:QL], pf[:, 0:QL], ACT.Square, scale=1.0 / 16.0,
                                         accum_out=k.stat2[:, t, 0:1]).then_inc(qk_sq, 1)
                    nc.scalar.activation(junk2[:, QL:QL + KVL], pf[:, QL:QL + KVL], ACT.Square, scale=float(KVL) ** -0.5,
                                         accum_out=k.stat2[:, t, 1:2]).then_inc(qk_sq, 1)

                def small_hi(t, n):
                    act.wait_ge(smT_ready, n + 1)
                    at = key_col(t)
                    s = bank[6]
                    if t != CACHE:
                        for c in range(2):
                            nc.scalar.activation(k.qnT[0][:, c, t * P:(t + 1) * P], s[:, c * P:(c + 1) * P], ACT.Copy,
                                                 scale=k.cols[:, C_QN + c:C_QN + c + 1])
                    gain = 1.0 if t == CACHE else k.cols[:, C_KVN:C_KVN + 1]
                    nc.scalar.activation(k.ckvT[0][:, at:at + P], s[:, 2 * P:3 * P], ACT.Copy, scale=gain)
                    nc.scalar.activation(k.krT[NOPE:QK, at:at + P], s[0:ROPE, 3 * P:4 * P], ACT.Copy).then_inc(sm_hi, 1)

                def split_hi(n):
                    _, w, hi, lo = staged[n]
                    if lo is None:
                        return
                    act.wait_ge(raw_loaded[n % 2], 16 * (n // 2 + 1))
                    nc.scalar.activation(hi, wraw[:, n % 2, 0:w], ACT.Copy).then_inc(raw_hi, 1)

                def pooled_high(t):
                    act.wait_ge(pooled_f, t + 1)
                    if t >= 1:
                        act.wait_ge(mix_ready, t)
                    nc.scalar.activation(pT[0][:, :], pooled[:, :], ACT.Copy).then_inc(pooled_hi, 1)

                def mixed(t):
                    act.wait_ge(mix_ready, t + 1)
                    for g in range(G):
                        op = nc.scalar.activation(k.mixT[:, g, t * P:(t + 1) * P], bank[7][:, g * P:(g + 1) * P], ACT.Copy,
                                                  scale=k.cols[:, C_PS + g:C_PS + g + 1])
                    op.then_inc(mix_done, 1)

                act.wait_ge(small_loaded, 48)
                nc.scalar.activation(es[:, :], k.cols[:, C_C:C_C + 2 * DC], ACT.Exp, scale=-1.0).then_inc(silu_exp, 1)
                square(0)
                square(1)
                for b in range(2 * DC):
                    mod.high(act, b)
                    if 3 <= b < NS + 3:
                        split_hi(b - 3)
                act.wait_ge(gain_done, 4)
                modulate(0)
                for t in range(T + 3):
                    if t + 2 < T:
                        square(t + 2)
                    if t + 1 < T:
                        modulate(t + 1)
                    if 0 <= t - 3 < T:
                        mixed(t - 3)
                    if t < T:
                        projected(t)
                    if 0 <= t - 1 < T:
                        small_hi(t - 1, t - 1)
                    if t - 1 == T:
                        small_hi(CACHE, T)
                    if 0 <= t - 2 < T:
                        pooled_high(t - 2)

            @block.vector
            def _(dve):
                def normed(t):
                    dve.wait_ge(x_rs, t + 1)
                    nc.vector.tensor_scalar(xin[:, t % 2, :], xin[:, t % 2, :], k.stat[:, t, 2:3], None, ALU.mult).then_inc(xn_ready, 1)

                def h_split(t):
                    dve.wait_ge(hf_ready, t + 1)
                    if t >= 2:
                        dve.wait_ge(proj_ready, t - 1)
                    nc.vector.tensor_copy(hT[0][:, t % 2, :], hf[:, :]).then_inc(h_hi, 1)
                    dve.wait_ge(h_hi, t + 1)
                    nc.vector.tensor_tensor(hT[1][:, t % 2, :], hf[:, :], hT[0][:, t % 2, :].bitcast(F32),
                                            ALU.subtract).then_inc(h_ready, 1)

                def projected(t):
                    pu = bank[3 + 2 * (t % 2)]
                    dve.wait_ge(u_hi, t + 1)
                    nc.vector.tensor_tensor(us[1][:, t % 4, :], pu[:, 0:POOLW], us[0][:, t % 4, :].bitcast(F32),
                                            ALU.subtract).then_inc(u_ready, 1)
                    kv, kr, kw = QL, QL + KVL, QL + KVL + ROPE
                    dve.wait_ge(qk_rs, t + 1)
                    if t >= 1:
                        dve.wait_ge(smT_ready, t)
                    nc.vector.tensor_scalar(sm[:, 0:QL], pf[:, 0:QL], k.stat2[:, t, 4:5], None, ALU.mult)
                    if t == CTX:
                        nc.vector.tensor_scalar(sm[:, kv:kr], pf[:, kv:kr], k.stat2[:, t, 5:6], None,
                                                ALU.mult).then_inc(rope_mul, 1)
                        nc.vector.tensor_copy(sm[:, kr:kr + ROPE], pf[:, kr:kw]).then_inc(sm_ready, 1)
                        dve.wait_ge(rope_mul, LT + 1)
                        nc.vector.tensor_tensor(ckvo[:, :], sm[:, kv:kr], kvn[:, :], ALU.mult).then_inc(ckvo_done, 1)
                        return
                    nc.vector.tensor_scalar(sm[:, kv:kr], pf[:, kv:kr], k.stat2[:, t, 5:6], None, ALU.mult)
                    nc.vector.tensor_tensor(rt[:, 0, :], pf[:, kr:kw], ropek[:, 0, t, :], ALU.mult)
                    nc.vector.tensor_tensor(rt[:, 1, :], pf[:, kw:PA], ropek[:, 1, t, :], ALU.mult).then_inc(rope_mul, 1)
                    dve.wait_ge(rope_mul, t + 1)
                    nc.vector.tensor_tensor(sm[:, kr:kr + ROPE], rt[:, 0, :], rt[:, 1, :], ALU.add).then_inc(sm_ready, 1)

                def small_lo(t, n):
                    dve.wait_ge(sm_hi, n + 1)
                    at = key_col(t)
                    s = bank[6]
                    if t != CACHE:
                        for c in range(2):
                            cut = slice(t * P, (t + 1) * P)
                            nc.vector.scalar_tensor_tensor(k.qnT[1][:, c, cut], s[:, c * P:(c + 1) * P],
                                                           k.cols[:, C_QN + c:C_QN + c + 1],
                                                           k.qnT[0][:, c, cut].bitcast(F32), ALU.mult, ALU.subtract)
                    gain = 1.0 if t == CACHE else k.cols[:, C_KVN:C_KVN + 1]
                    nc.vector.scalar_tensor_tensor(k.ckvT[1][:, at:at + P], s[:, 2 * P:3 * P], gain,
                                                   k.ckvT[0][:, at:at + P].bitcast(F32), ALU.mult,
                                                   ALU.subtract).then_inc(sm_done, 1)

                def pooled_split(t):
                    variant = {0: 0, LT - 1: 2, CTX: 3}.get(t, 1)
                    dve.wait_ge(invc_loaded[variant % 2], 16 * (variant // 2 + 1))
                    dve.wait_ge(band_ready, t + 1)
                    nc.vector.tensor_tensor(pooled[:, :], bank[7][:, :], invc[:, variant % 2, :], ALU.mult).then_inc(pooled_f, 1)
                    dve.wait_ge(pooled_hi, t + 1)
                    nc.vector.tensor_tensor(pT[1][:, :], pooled[:, :], pT[0][:, :].bitcast(F32), ALU.subtract).then_inc(pooled_ready, 1)

                dve.wait_ge(small_loaded, 48)
                nc.vector.tensor_copy(k.identr[:, :], k.ident[:, :]).then_inc(identr_done, 1)
                dve.wait_ge(silu_exp, 1)
                nc.vector.tensor_scalar(es[:, :], es[:, :], 1.0, None, ALU.add).then_inc(silu_den, 1)
                dve.wait_ge(silu_den, 1)
                nc.vector.reciprocal(es[:, :], es[:, :]).then_inc(silu_den, 1)
                dve.wait_ge(silu_den, 2)
                nc.vector.tensor_tensor(sf[:, :], k.cols[:, C_C:C_C + 2 * DC], es[:, :], ALU.mult).then_inc(silu_f, 1)
                dve.wait_ge(silu_f, 1)
                for j in range(2):
                    nc.vector.tensor_copy(k.silu[:, :, j], sf[:, j * DC:(j + 1) * DC]).then_inc(silu_f, 1)
                dve.wait_ge(silu_f, 3)
                for j in range(2):
                    nc.vector.tensor_tensor(k.silu[:, :, 2 + j], sf[:, j * DC:(j + 1) * DC], k.silu[:, :, j].bitcast(F32),
                                            ALU.subtract).then_inc(silu_done, 1)
                normed(0)
                normed(1)
                for b in range(2 * DC):
                    mod.low(nc.vector, b)
                dve.wait_ge(mod.done, 2 * DC)
                for g in range(4):
                    op = nc.vector.tensor_copy(mod.rows[:, g * 512:(g + 1) * 512], bank[4 + g][0:4, :])
                op.then_inc(rows_done, 1)
                dve.wait_ge(cols_done, 1)
                for j in range(2):
                    nc.vector.tensor_tensor(k.mod[:, 0:2 * DC, j], bank[2][:, 0:4 * DC].rearrange("p (b j) -> p b j", j=2)[:, :, j],
                                            k.cols[:, C_BADA:C_BADA + 2 * DC], ALU.add).then_inc(gain_done, 1)
                dve.wait_ge(gain_done, 2)
                for j in range(2):
                    nc.vector.scalar_tensor_tensor(gain1[:, :, j], k.mod[:, DC:2 * DC, j], 1.0, k.cols[:, C_N1:C_N1 + DC],
                                                   ALU.add, ALU.mult).then_inc(gain_done, 1)
                dve.wait_ge(tabs_loaded, 48)
                dve.wait_ge(raw_done, NS)
                h_split(0)
                for t in range(T + 3):
                    if t + 1 < T:
                        h_split(t + 1)
                    if t + 2 < T:
                        normed(t + 2)
                    if t < T:
                        projected(t)
                    if 0 <= t - 1 < T:
                        small_lo(t - 1, t - 1)
                    if t - 1 == T:
                        small_lo(CACHE, T)
                    if 0 <= t - 2 < T:
                        pooled_split(t - 2)

            @block.tensor
            def _(pe):
                def turn_x(t):
                    pe.wait_ge(xn_ready, t + 1)
                    if t >= 1:
                        pe.wait_ge(hf_ready, t)
                    for c in range(DC):
                        op = nc.tensor.transpose(bank[c // 4][:, (c % 4) * P:(c % 4 + 1) * P], xin[:, t % 2, c * P:(c + 1) * P], k.ident[:, :])
                    op.then_inc(xT_ready, 1)

                def project(t):
                    pa, pu = bank[2 + 2 * (t % 2)], bank[3 + 2 * (t % 2)]
                    pe.wait_ge(h_ready, t + 1)
                    if t >= 2:
                        pe.wait_ge(pf_ready, t - 1)
                        pe.wait_ge(u_ready, t - 1)
                    for c in range(DC):
                        if c == DC // 2 and t >= 3:
                            mix(t - 3)
                        for x, y in ((0, 0), (0, 1), (1, 0)):
                            w = hT[x][:, t % 2, c * P:(c + 1) * P]
                            first, last = c == 0 and (x, y) == (0, 0), c == DC - 1 and (x, y) == (1, 0)
                            nc.tensor.matmul(pa[:, 0:PA], w, win[y][:, c, 0:PA], start=first, stop=last)
                            op = nc.tensor.matmul(pu[:, 0:POOLW], w, win[y][:, c, PA:INC], start=first, stop=last)
                    op.then_inc(proj_ready, 1)

                def turn_small(t, n):
                    s = bank[6]
                    if n >= 1:
                        pe.wait_ge(sm_done, n)
                    if t == CACHE:
                        pe.wait_ge(tabs_loaded, 48)
                        nc.tensor.transpose(s[:, 2 * P:3 * P], cin[:, 0:KVL], k.ident[:, :])
                        nc.tensor.transpose(s[0:ROPE, 3 * P:4 * P], cin[:, KVL:KVL + ROPE], k.ident[:, :]).then_inc(smT_ready, 1)
                        return
                    pe.wait_ge(sm_ready, t + 1)
                    for c in range(3):
                        nc.tensor.transpose(s[:, c * P:(c + 1) * P], sm[:, c * P:(c + 1) * P], k.ident[:, :])
                    nc.tensor.transpose(s[0:ROPE, 3 * P:4 * P], sm[:, QL + KVL:QL + KVL + ROPE], k.ident[:, :]).then_inc(smT_ready, 1)

                def pool_windows(t):
                    after = t < LT - 1
                    pe.wait_ge(u_ready, t + 1 + after)
                    if t >= 1:
                        pe.wait_ge(mix_done, t)
                    first = True
                    for g in range(G):
                        cut = slice(g * P, (g + 1) * P)
                        for x in range(2):
                            op = nc.tensor.matmul(bank[7][:, g * P:(g + 1) * P], us[x][:, t % 4, cut], main_band(t, g),
                                                  start=first, stop=False, skip_group_check=True)
                            first = False
                            if 0 < t < LT:
                                op = nc.tensor.matmul(bank[7][:, g * P:g * P + EDGE], us[x][:, (t - 1) % 4, cut], side_band(g, 0),
                                                      start=False, stop=False, skip_group_check=True)
                            if after:
                                op = nc.tensor.matmul(bank[7][:, (g + 1) * P - EDGE:(g + 1) * P], us[x][:, (t + 1) % 4, cut],
                                                      side_band(g, 1), start=False, stop=False, skip_group_check=True)
                    op.then_inc(band_ready, 1)

                def mix(t):
                    pe.wait_ge(pooled_ready, t + 1)
                    for g in range(G):
                        cut = slice(g * P, (g + 1) * P)
                        for i, (x, y) in enumerate(((0, 0), (0, 1), (1, 0))):
                            op = nc.tensor.matmul(bank[7][:, cut], wp[x][:, cut], pT[y][:, cut], start=i == 0, stop=i == 2)
                    op.then_inc(mix_ready, 1)

                pe.wait_ge(small_loaded, 48)
                turn_x(0)
                pe.wait_ge(silu_done, 2)
                for b in range(2 * DC):
                    mod.multiply(pe, b, bank[4 + b // 4])
                pe.wait_ge(rows_done, 1)
                for b in range(2 * DC):
                    op = nc.tensor.matmul(bank[2][:, 2 * b:2 * b + 2], mod.rows[:, b * P:(b + 1) * P], k.pick[:, :],
                                          start=True, stop=True)
                op.then_inc(cols_done, 1)
                pe.wait_ge(gain_done, 2)
                for t in range(T + 3):
                    if t + 1 < T:
                        turn_x(t + 1)
                    if T <= t < T + 3:
                        mix(t - 3)
                    if t == 0:
                        pe.wait_ge(raw_done, NS)
                    if t < T:
                        project(t)
                    if 0 <= t - 1 < T:
                        turn_small(t - 1, t - 1)
                    if t - 1 == T:
                        turn_small(CACHE, T)
                    if 0 <= t - 2 < T:
                        pool_windows(t - 2)


def attention_phase(nc, a, k):
    with ExitStack() as ctx:
        sb, sem = memory(nc, ctx), signals(nc, ctx)
        bank = k.bank
        V = sb("V", [P, LT + 2, H, 2 * VD], F32R)
        kT = [[sb(f"kT{x}{j}", [P, NKEY], F32R) for x in "hl"] for j in range(2)]
        qT = [[sb(f"qT{x}{j}", [P, NTOK], F32R) for x in "hl"] for j in range(2)]
        whr = [sb(f"whr{j}", [P, WH]) for j in range(2)]
        wh = [[sb(f"wh{x}{j}", [P, WH], F32R) for x in "hl"] for j in range(2)]
        ropeq = sb("ropeq", [P, NTOK])
        q1, q2, qf = sb("q1", [P, BN]), sb("q2", [P, BN]), sb("qf", [P, BN])
        pm, mx, nm = sb("pm", [P, T, 3]), sb("mx", [P, T]), sb("nm", [P, T, 2], F32R)
        pexp = [sb(f"pexp{i}", [P, 512]) for i in range(2)]
        phi = [sb(f"phi{i}", [P, 512], F32R) for i in range(2)]
        plo = [sb(f"plo{i}", [P, 512], F32R) for i in range(2)]
        ones = sb("ones", [P, 2])
        out_h, out_l = sb("out_h", [VD, 512]), sb("out_l", [VD, 512])
        mod = Modulation(nc, a, k, sb, sem, 2 * DC, 2, 1)
        with ExitStack() as early:
            sbe = memory(nc, early)
            wv = [sbe(f"wv{x}", [P, H * VD], F32R) for x in "hl"]
            wvr = sbe("wvr", [P, H * VD])
        psum = [sb(f"psum{i}", [P, 512]) for i in range(2)]
        rsum, rcol = sb("rsum", [P, 512]), sb("rcol", [P, 4])

        tabq_loaded, wv_loaded = sem("tabq_loaded"), sem("wv_loaded")
        head_loaded = [sem(f"head_loaded{j}") for j in range(2)]
        wv_hi, wv_ready, v_hi, setup_a, setup_d = sem("wv_hi"), sem("wv_ready"), sem("v_hi"), sem("setup_a"), sem("setup_d")
        wh_hi, wh_ready = sem("wh_hi"), sem("wh_ready")
        ring_filled, ring_freed = sem("ring_filled"), sem("ring_freed")
        q_nope, q_full, q_hi, q_lo, k_hi = sem("q_nope"), sem("q_full"), sem("q_hi"), sem("q_lo"), sem("k_hi")
        max_done, nm_ready, mrow_ready = sem("max_done"), sem("nm_ready"), sem("mrow_ready")
        st_filled, p_exp, p_hi, p_lo = sem("st_filled"), sem("p_exp"), sem("p_hi"), sem("p_lo")
        pv_done, p_summed, sum_ready = sem("pv_done"), sem("p_summed"), sem("sum_ready")
        spread_ready, spread_read = sem("spread_ready"), sem("spread_read")
        inv_done, pv_read, attn_done = sem("inv_done"), sem("pv_read"), sem("attn_done")
        rows_done, cols_done, ada_read = sem("ada_rows_done"), sem("ada_cols_done"), sem("ada_read")

        NV = LT + 2
        S0 = 6
        M0 = S0 + 3 * LT + 1
        RU = M0 + 3
        KCUT = ((0, 512), (512, 1024), (1024, NKEY))
        HALF = LAT // 2
        KT = LKEY // P
        MS = 2 * KT + 1
        assert RU % 3 == 1 and NV % 3 == 1 and MS % 2 == 1

        def is_q(li):
            return li in (0, 2, 4)

        def is_k(li):
            return li in (1, 3, 5)

        def ring_free(pe, h, li):
            before = {0: -1, 1: -3, 2: -2}.get(li, li - 3)
            pe.wait_ge(ring_freed, h * RU + (NV + before + 1))

        def ring_full(eng, h, li):
            eng.wait_ge(ring_filled, h * RU + (NV + li + 1))

        def step(s):
            if s == MS - 1:
                return LAT, 1, LKEY, CACHE, 0, True
            half, kt = divmod(s, KT)
            return half * HALF, HALF // P, kt * P, kt, kt, kt == KT - 1

        def group(g):
            return 3 * (g // MS) + g % MS // KT

        SIDE = [[li] for li in range(S0)] + [[] for _ in range(S0, MS)]
        for li in range(S0, M0):
            SIDE[S0 + (li - S0) * 9 // (M0 - S0)].append(li)
        SIDE[MS - 3] += [M0, M0 + 1, M0 + 2]
        MOD_AT = {3: 0, 5: 1, 7: 2, 9: 3}
        ROWS_AT, COLS_AT = 11, 12
        SPLIT_HEAD_AT = 10
        SUMS_AFTER = (5, 2, 3)
        SPREAD_AFTER = (6, 3, 4)
        HI_LAG, PV_LAG = 1, 2

        def ending(g, after):
            return [g - lag for i, lag in enumerate(after) if g >= lag and step((g - lag) % MS)[-1] and group(g - lag) % 3 == i]

        with nc.Block() as block:

            @block.sync
            def _(sp):
                def load_head(h, j):
                    sp.dma_start(whr[j][:, :], a["w_head"][h]).then_inc(head_loaded[j], 16)

                def load_ada(h):
                    for i in range(4):
                        mod.load(sp, 4 * h + i)

                sp.dma_start(wvr[:], a["w_v"]).then_inc(wv_loaded, 16)
                sp.dma_start(ropeq[NOPE:P, :], a["ropeq"]).then_inc(tabq_loaded, 16)
                load_head(0, 0)
                load_head(1, 1)
                load_ada(0)
                for h in range(1, H):
                    if h + 1 < H:
                        sp.wait_ge(wh_ready, h)
                        load_head(h + 1, (h + 1) % 2)
                    load_ada(h)

            @block.gpsimd
            def _(pool):
                def low_query(h, j, c):
                    cut = slice(c * BN, (c + 1) * BN)
                    pool.wait_ge(q_hi, 3 * h + c + 1)
                    nc.gpsimd.tensor_tensor(qT[j][1][0:QK, cut], qf[0:QK, :], qT[j][0][0:QK, cut].bitcast(F32),
                                            ALU.subtract).then_inc(q_lo, 1)

                def add_up(g):
                    _, nq, _, _, first, last = step(g % MS)
                    n, q = nq * P, group(g)
                    pool.wait_ge(p_exp, g + 3)
                    if first == 0:
                        if q >= 2:
                            pool.wait_ge(sum_ready, q - 1)
                        op = nc.gpsimd.tensor_copy(psum[q % 2][:, 0:n], pexp[g % 2][:, 0:n])
                    else:
                        pool.wait_ge(p_summed, g + 2)
                        op = nc.gpsimd.tensor_tensor(psum[q % 2][:, 0:n], psum[q % 2][:, 0:n], pexp[g % 2][:, 0:n], ALU.add)
                    op.then_inc(p_summed, 1)

                def hand_over(g):
                    q0, nq, _, _, _, _ = step(g % MS)
                    n, h, row = nq * P, g // MS, g // MS % 2 * VD
                    pool.wait_ge(pv_read, group(g) + 1)
                    nc.gpsimd.tensor_tensor(k.attn[row:row + VD, h // 2, q0:q0 + n], out_h[:, 0:n], out_l[:, 0:n],
                                            ALU.add).then_inc(attn_done, 1)

                pool.sem_inc(p_summed, 2)
                for c in range(3):
                    low_query(0, 0, c)
                pool.wait_ge(q_lo, 3)
                for g in range(H * MS + 6):
                    h, s = divmod(g, MS)
                    if h < H:
                        add_up(g)
                        if h + 1 < H and s in (1, 3, 5):
                            pool.wait_ge(p_summed, g + 3)
                            low_query(h + 1, (h + 1) % 2, s // 2)
                            pool.wait_ge(q_lo, 3 * (h + 1) + s // 2 + 1)
                    for e in ending(g, [n + 1 for n in SPREAD_AFTER]):
                        if e < H * MS:
                            pool.wait_ge(p_summed, min(g, H * MS - 1) + 3)
                            hand_over(e)
                            pool.wait_ge(attn_done, group(e) + 1)

            @block.scalar
            def _(act):
                def split_head(h):
                    j = h % 2
                    act.wait_ge(head_loaded[j], 16 * (h // 2 + 1))
                    nc.scalar.activation(wh[j][0][:, :], whr[j][:, :], ACT.Copy).then_inc(wh_hi, 1)

                def side(h, j, li):
                    if is_q(li):
                        c = li // 2
                        ring_full(act, h, li)
                        act.wait_ge(q_lo, 3 * h + c)
                        nc.scalar.activation(qf[0:NOPE, :], bank[li % 3][0:NOPE, 0:BN], ACT.Copy).then_inc(q_nope, 1)
                    elif is_k(li):
                        lo, hi = KCUT[li // 2]
                        ring_full(act, h, li)
                        nc.scalar.activation(kT[j][0][0:NOPE, lo:hi], bank[li % 3][0:NOPE, 0:hi - lo], ACT.Copy).then_inc(k_hi, 1)

                def high_query(h, j, c):
                    act.wait_ge(q_full, 3 * h + c + 1)
                    act.wait_ge(q_nope, 3 * h + c + 1)
                    nc.scalar.activation(qT[j][0][0:QK, c * BN:(c + 1) * BN], qf[0:QK, :], ACT.Copy).then_inc(q_hi, 1)

                def main(h, j, s):
                    _, nq, _, _, _, _ = step(s)
                    n, g = nq * P, MS * h + s
                    slot = g % 2
                    act.wait_ge(st_filled, g + 1)
                    act.wait_ge(p_lo, g + 1)
                    act.wait_ge(p_summed, g + 1)
                    nc.scalar.activation(pexp[slot][:, 0:n], bank[3 + slot][:, 0:n], ACT.Exp, scale=SCALE).then_inc(p_exp, 1)

                def high(g):
                    n = step(g % MS)[1] * P
                    slot = g % 2
                    act.wait_ge(p_exp, g + 3)
                    act.wait_ge(pv_done, g + 1)
                    nc.scalar.activation(phi[slot][:, 0:n], pexp[slot][:, 0:n], ACT.Copy).then_inc(p_hi, 1)

                act.sem_inc(p_exp, 2)
                act.wait_ge(wv_loaded, 16)
                nc.scalar.activation(wv[0][:, :], wvr[:, :], ACT.Copy).then_inc(wv_hi, 1)
                for j in range(2):
                    nc.scalar.activation(kT[j][0][NOPE:QK, :], k.krT[NOPE:QK, :], ACT.Copy).then_inc(setup_a, 1)
                for v in range(NV):
                    act.wait_ge(ring_filled, v + 1)
                    nc.scalar.activation(V[:, v, :, 0:VD], bank[v % 3][:, :].rearrange("p (h d) -> p h d", h=H),
                                         ACT.Copy).then_inc(v_hi, 1)
                split_head(0)
                split_head(1)
                for li in range(S0):
                    side(0, 0, li)
                    if is_q(li):
                        high_query(0, 0, li // 2)
                for g in range(H * MS + 5):
                    h, s = divmod(g, MS)
                    if h < H:
                        main(h, h % 2, s)
                    if 0 <= g - HI_LAG < H * MS:
                        high(g - HI_LAG)
                    for e in ending(g, SPREAD_AFTER):
                        if e < H * MS:
                            n, q = step(e % MS)[1] * P, group(e)
                            act.wait_ge(spread_ready, q + 1)
                            if q:
                                act.wait_ge(pv_read, q)
                            nc.scalar.activation(rsum[:, 0:n], bank[7][:, 0:n], ACT.Copy).then_inc(spread_read, 1)
                    if h < H:
                        if s in MOD_AT:
                            mod.high(act, 4 * h + MOD_AT[s])
                        if s == SPLIT_HEAD_AT and h + 2 < H:
                            split_head(h + 2)
                        if h + 1 < H:
                            if s in (1, 3, 5):
                                high_query(h + 1, (h + 1) % 2, s // 2)
                            for li in SIDE[s]:
                                side(h + 1, (h + 1) % 2, li)

            @block.vector
            def _(dve):
                def split_head(h):
                    j = h % 2
                    dve.wait_ge(wh_hi, h + 1)
                    nc.vector.tensor_tensor(wh[j][1][:, :], whr[j][:, :], wh[j][0][:, :].bitcast(F32),
                                            ALU.subtract).then_inc(wh_ready, 1)

                def side(h, j, li):
                    b = bank[li % 3]
                    ring_full(dve, h, li)
                    if is_q(li):
                        c = li // 2
                        cut = slice(c * BN, (c + 1) * BN)
                        if c or h:
                            dve.wait_ge(q_full, 3 * h + c)
                            dve.wait_ge(q_lo, 3 * h + c)
                        nc.vector.tensor_tensor(q1[NOPE:QK, :], b[QK:P, 0:BN], ropeq[QK:P, cut], ALU.mult)
                        dve.wait_ge(q_nope, 3 * h + c + 1)
                        nc.vector.tensor_tensor(q2[NOPE:QK, :], b[NOPE:QK, 0:BN], ropeq[NOPE:QK, cut], ALU.mult).then_inc(ring_freed, 1)
                        dve.wait_ge(ring_freed, h * RU + (NV + li + 1))
                        nc.vector.tensor_tensor(qf[NOPE:QK, :], q1[NOPE:QK, :], q2[NOPE:QK, :], ALU.add).then_inc(q_full, 1)
                    elif is_k(li):
                        lo, hi = KCUT[li // 2]
                        dve.wait_ge(k_hi, 3 * h + li // 2 + 1)
                        nc.vector.tensor_tensor(kT[j][1][0:NOPE, lo:hi], b[0:NOPE, 0:hi - lo], kT[j][0][0:NOPE, lo:hi].bitcast(F32),
                                                ALU.subtract).then_inc(ring_freed, 1)
                    elif li < M0:
                        qt, c = divmod(li - S0, 3)
                        n = BN if qt < LT else P
                        nc.vector.reduce_max(pm[:, qt, c:c + 1], b[:, 0:n], AX_X).then_inc(ring_freed, 1)
                        if li == M0 - 1:
                            dve.wait_ge(ring_freed, h * RU + (NV + M0))
                            nc.vector.tensor_reduce(mx[:, :], pm[:, :, :], AX_X, ALU.max).then_inc(max_done, 1)
                            dve.wait_ge(max_done, h + 1)
                            nc.vector.tensor_scalar(nm[:, :, 0], mx[:, :], -1.0, None, ALU.mult).then_inc(nm_ready, 1)
                            dve.wait_ge(nm_ready, 2 * h + 1)
                            nc.vector.scalar_tensor_tensor(nm[:, :, 1], mx[:, :], -1.0, nm[:, :, 0].bitcast(F32), ALU.mult,
                                                           ALU.subtract).then_inc(nm_ready, 1)
                    else:
                        c = li - M0
                        nc.vector.tensor_scalar(qT[j][0][QK:QK + 2, c * BN:(c + 1) * BN], b[0:2, 0:BN], 1.0, None,
                                                ALU.mult).then_inc(ring_freed, 1)

                def low(g):
                    n = step(g % MS)[1] * P
                    slot = g % 2
                    dve.wait_ge(p_hi, g + 1)
                    nc.vector.tensor_tensor(plo[slot][:, 0:n], pexp[slot][:, 0:n], phi[slot][:, 0:n].bitcast(F32),
                                            ALU.subtract).then_inc(p_lo, 1)

                def invert(g):
                    nq, q = step(g % MS)[1], group(g)
                    dve.wait_ge(sum_ready, q + 1)
                    if q:
                        dve.wait_ge(spread_ready, q)
                    nc.vector.reciprocal(rcol[:, 0:nq], bank[7][:, 0:2 * nq].rearrange("p (i j) -> p i j", j=2)[:, :, 0]).then_inc(inv_done, 1)

                def values(g):
                    _, nq, _, _, _, _ = step(g % MS)
                    n, q = nq * P, group(g)
                    b = bank[5 + q % 2]
                    dve.wait_ge(spread_read, q + 1)
                    dve.wait_ge(pv_done, g + 3)
                    if q:
                        dve.wait_ge(attn_done, q)
                    nc.vector.tensor_tensor(out_h[:, 0:n], b[0:VD, 0:n], rsum[0:VD, 0:n], ALU.mult)
                    nc.vector.tensor_tensor(out_l[:, 0:n], b[VD:P, 0:n], rsum[VD:P, 0:n], ALU.mult).then_inc(pv_read, 1)

                dve.sem_inc(p_lo, 2)
                nc.vector.memset(pm[:, LT, :], -3.0e38).then_inc(setup_d, 1)
                for j in range(2):
                    nc.vector.memset(kT[j][0][QK:QK + 2, :].bitcast(F32), 1.0).then_inc(setup_d, 1)
                nc.vector.memset(ones[:, :], 1.0).then_inc(setup_d, 1)
                dve.wait_ge(wv_hi, 1)
                nc.vector.tensor_tensor(wv[1][:, :], wvr[:, :], wv[0][:, :].bitcast(F32), ALU.subtract).then_inc(wv_ready, 1)
                for j in range(2):
                    dve.wait_ge(setup_a, j + 1)
                    nc.vector.tensor_tensor(kT[j][1][NOPE:QK, :], k.krT[NOPE:QK, :], kT[j][0][NOPE:QK, :].bitcast(F32),
                                            ALU.subtract).then_inc(setup_d, 1)
                for v in range(NV):
                    dve.wait_ge(v_hi, v + 1)
                    nc.vector.tensor_tensor(V[:, v, :, VD:2 * VD], bank[v % 3][:, :].rearrange("p (h d) -> p h d", h=H),
                                            V[:, v, :, 0:VD].bitcast(F32), ALU.subtract).then_inc(ring_freed, 1)
                dve.wait_ge(tabq_loaded, 16)
                split_head(0)
                split_head(1)
                for li in range(RU):
                    side(0, 0, li)
                for g in range(H * MS + 6):
                    h, s = divmod(g, MS)
                    if 0 <= g - HI_LAG < H * MS:
                        low(g - HI_LAG)
                    if h < H:
                        if s in MOD_AT:
                            mod.low(nc.vector, 4 * h + MOD_AT[s])
                        if s == ROWS_AT:
                            dve.wait_ge(mod.done, 4 * h + 4)
                            nc.vector.tensor_copy(mod.rows[:, :], bank[7][0:4, :]).then_inc(rows_done, 1)
                        if s == COLS_AT:
                            dve.wait_ge(cols_done, h + 1)
                            at = 4 * h + 2 * DC
                            for j in range(2):
                                nc.vector.tensor_tensor(k.mod[:, at:at + 4, j],
                                                        bank[7][:, 0:8].rearrange("p (b j) -> p b j", j=2)[:, :, j],
                                                        k.cols[:, C_BADA + at:C_BADA + at + 4], ALU.add).then_inc(ada_read, 1)
                        if s == SPLIT_HEAD_AT and h + 2 < H:
                            split_head(h + 2)
                        if h + 1 < H:
                            for li in SIDE[s]:
                                side(h + 1, (h + 1) % 2, li)
                    for e in ending(g, SUMS_AFTER):
                        if e < H * MS:
                            invert(e)
                    for e in ending(g, SPREAD_AFTER):
                        if e < H * MS:
                            values(e)

            @block.tensor
            def _(pe):
                def side(h, j, li):
                    b = bank[li % 3]
                    if li == 0:
                        pe.wait_ge(wh_ready, h + 1)
                    if S0 <= li < M0 and (li - S0) % (3 * BLK) == 0:
                        pe.wait_ge(q_lo, 3 * h + (li - S0) // (3 * BLK) + 1)
                    if li == S0:
                        pe.wait_ge(ring_freed, h * RU + (NV + S0))
                    if li == M0:
                        pe.wait_ge(nm_ready, 2 * h + 2)
                    ring_free(pe, h, li)
                    if is_q(li):
                        cut = slice(li // 2 * BN, (li // 2 + 1) * BN)
                        n = 0
                        for c in range(2):
                            for x, y in ((0, 0), (0, 1), (1, 0)):
                                op = nc.tensor.matmul(b[:, 0:BN], wh[j][x][:, c * P:(c + 1) * P], k.qnT[y][:, c, cut],
                                                      start=n == 0, stop=n == 5)
                                n += 1
                    elif is_k(li):
                        lo, hi = KCUT[li // 2]
                        for n, (x, y) in enumerate(((0, 0), (0, 1), (1, 0))):
                            op = nc.tensor.matmul(b[0:NOPE, 0:hi - lo], wh[j][x][:, 2 * P:WH], k.ckvT[y][:, lo:hi],
                                                  start=n == 0, stop=n == 2)
                    elif li < M0:
                        qt, c = divmod(li - S0, 3)
                        lo, w = (c * BN, BN) if qt < LT else (LKEY, P)
                        for n, (x, y) in enumerate(((0, 0), (0, 1), (1, 0))):
                            op = nc.tensor.matmul(b[:, 0:w], qT[j][x][0:QK, qt * P:(qt + 1) * P], kT[j][y][0:QK, lo:lo + w],
                                                  start=n == 0, stop=n == 2)
                    else:
                        for i in range(3):
                            op = nc.tensor.matmul(b[0:2, i * P:(i + 1) * P], nm[:, 3 * (li - M0) + i, :], k.identr[:, :],
                                                  start=True, stop=True)
                    op.then_inc(ring_filled, 1)

                def scores(h, j, s):
                    q0, nq, k0, _, _, _ = step(s)
                    g = MS * h + s
                    slot = g % 2
                    n = nq * P
                    if s == 0:
                        pe.wait_ge(ring_freed, h * RU + (NV + RU))
                    pe.wait_ge(p_exp, g + 1)
                    b = bank[3 + slot][:, 0:n]
                    nc.tensor.matmul(b, kT[j][0][0:QK + 2, k0:k0 + P], qT[j][0][0:QK + 2, q0:q0 + n], start=True, stop=False)
                    nc.tensor.matmul(b, kT[j][0][0:QK, k0:k0 + P], qT[j][1][0:QK, q0:q0 + n], start=False, stop=False)
                    nc.tensor.matmul(b, kT[j][1][0:QK, k0:k0 + P], qT[j][0][0:QK, q0:q0 + n], start=False, stop=True).then_inc(st_filled, 1)

                def values(g):
                    _, nq, _, vt, pos, last = step(g % MS)
                    n, h, q = nq * P, g // MS, group(g)
                    pe.wait_ge(p_lo, g + 3)
                    if pos == 0 and q >= 2:
                        pe.wait_ge(pv_read, q - 1)
                    b = bank[5 + q % 2][:, 0:n]
                    nc.tensor.matmul(b, V[:, vt, h, :], phi[g % 2][:, 0:n], start=pos == 0, stop=False)
                    nc.tensor.matmul(b, V[:, vt, h, :], plo[g % 2][:, 0:n], start=False, stop=last).then_inc(pv_done, 1)

                def sums(g):
                    _, nq, _, _, _, _ = step(g % MS)
                    h, q = g // MS, group(g)
                    pe.wait_ge(p_summed, g + 3)
                    if q % 3 == 0:
                        pe.wait_ge(ada_read, 2 * h + 2)
                    else:
                        pe.wait_ge(spread_read, q)
                    for i in range(nq):
                        op = nc.tensor.matmul(bank[7][:, 2 * i:2 * i + 2], psum[q % 2][:, i * P:(i + 1) * P], ones[:, :],
                                              start=True, stop=True)
                    op.then_inc(sum_ready, 1)

                def spread(g):
                    nq, q = step(g % MS)[1], group(g)
                    pe.wait_ge(inv_done, q + 1)
                    for i in range(nq):
                        op = nc.tensor.matmul(bank[7][:, i * P:(i + 1) * P], rcol[:, i:i + 1].to_broadcast([P, P]), k.ident[:, :],
                                              start=True, stop=True)
                    op.then_inc(spread_ready, 1)

                pe.sem_inc(pv_done, 2)
                pe.wait_ge(wv_ready, 1)
                for v in range(NV):
                    at = key_col({LT: CACHE, LT + 1: CTX}.get(v, v))
                    if v >= 3:
                        pe.wait_ge(ring_freed, v - 2)
                    for n, (x, y) in enumerate(((0, 0), (0, 1), (1, 0))):
                        op = nc.tensor.matmul(bank[v % 3][:, :], k.ckvT[x][:, at:at + P], wv[y][:, :], start=n == 0, stop=n == 2)
                    op.then_inc(ring_filled, 1)
                pe.wait_ge(setup_d, 6)
                for li in range(RU):
                    side(0, 0, li)
                for g in range(H * MS + 5):
                    h, s = divmod(g, MS)
                    if h < H:
                        if s == COLS_AT:
                            pe.wait_ge(rows_done, h + 1)
                            for i in range(4):
                                op = nc.tensor.matmul(bank[7][:, 2 * i:2 * i + 2], mod.rows[:, i * P:(i + 1) * P], k.pick[:, :],
                                                      start=True, stop=True)
                            op.then_inc(cols_done, 1)
                        scores(h, h % 2, s)
                    for e in ending(g, SPREAD_AFTER):
                        if e < H * MS:
                            spread(e)
                    for e in ending(g, SUMS_AFTER):
                        if e < H * MS:
                            sums(e)
                    if h + 1 < H:
                        for li in SIDE[s]:
                            side(h + 1, (h + 1) % 2, li)
                    if 0 <= g - PV_LAG < H * MS:
                        values(g - PV_LAG)
                    if h < H and s - 1 in MOD_AT:
                        if s - 1 == min(MOD_AT) and h:
                            pe.wait_ge(spread_read, 3 * h)
                        mod.multiply(pe, 4 * h + MOD_AT[s - 1], bank[7])


def normed_again(nc, dve, k, t):
    dve.wait_ge(k.x2_rs, t + 1)
    if t >= 2:
        dve.wait_ge(k.xT_ready, 2 * t - 2)
    nc.vector.tensor_scalar(k.xn[:, t % 2, :], k.x[:, t, :], k.stat[:, t, 5:6], None, ALU.mult).then_inc(k.xn_ready, 1)


def turn_half(nc, pe, k, n, out):
    t, q = divmod(n, 2)
    pe.wait_ge(k.xn_ready, t + 1)
    for c in range(4):
        at = (4 * q + c) * P
        op = nc.tensor.transpose(out[:, c * P:(c + 1) * P], k.xn[:, t % 2, at:at + P], k.ident[:, :])
    op.then_inc(k.xT_ready, 1)


def modulate_half(nc, act, k, n, out):
    t, q = divmod(n, 2)
    j = int(t == CTX)
    act.wait_ge(k.xT_ready, n + 1)
    if n >= 2:
        act.wait_ge(k.h_ready, n - 1)
    for c in range(4):
        f = 4 * q + c
        op = nc.scalar.activation(k.hf[:, q, c * P:(c + 1) * P], out[:, c * P:(c + 1) * P], ACT.Identity,
                                  bias=k.mod[:, 3 * DC + f, j:j + 1], scale=k.gain2[:, f, j:j + 1])
    op.then_inc(k.hf_ready, 1)


def split_half(nc, dve, k, n):
    t, q = divmod(n, 2)
    h, at = k.h2[t // BLK % 2], t % BLK * P
    hi, lo = (x[:, 4 * q:4 * q + 4, at:at + P] for x in h)
    v = k.hf[:, q, :].rearrange("p (c n) -> p c n", c=4)
    dve.wait_ge(k.hf_ready, n + 1)
    nc.vector.tensor_copy(hi, v).then_inc(k.h_hi, 1)
    dve.wait_ge(k.h_hi, n + 1)
    nc.vector.tensor_tensor(lo, v, hi.bitcast(F32), ALU.subtract).then_inc(k.h_ready, 1)


def spread_gate(nc, pe, k, section, j, out, ready):
    for c in range(DC):
        op = nc.tensor.matmul(out[c // 4][:, (c % 4) * P:(c % 4 + 1) * P],
                              k.mod[:, section * DC + c, j:j + 1].to_broadcast([P, P]), k.ident[:, :], start=True, stop=True)
    op.then_inc(ready, 1)


def read_gate(nc, act, gate, out, ready, done, n):
    act.wait_ge(ready, n + 1)
    for i in range(2):
        op = nc.scalar.activation(gate[:, i * 512:(i + 1) * 512], out[i][:, :], ACT.Copy)
    op.then_inc(done, 1)


def output_phase(nc, a, k):
    with ExitStack() as ctx:
        sb, sem = memory(nc, ctx), signals(nc, ctx)
        bank = k.bank
        wo = [sb(f"wo{x}", [P, DC, D], F32R) for x in "hl"]
        wor = k.xn
        aT = [sb(f"aT{x}", [P, 2, 4, P], F32R) for x in "hl"]
        mT = [sb(f"mT{x}", [P, 2, 4, P], F32R) for x in "hl"]
        add = sb("add", [P, 2, D // 2])
        gate = sb("gate1", [P, 2, D])
        x_loaded = [sem(f"res_loaded{i}") for i in range(3)]
        wo_loaded = [sem(f"wo_loaded{i}") for i in range(2)]
        wo_hi, wo_ready = sem("wo_hi"), sem("wo_ready")
        gate_ready, gate_done, gain2_done = sem("gate_ready"), sem("gate_done"), sem("gain2_done")
        a_hi, a_ready, m_hi, m_ready = sem("a_hi"), sem("a_ready"), sem("m_hi"), sem("m_ready")
        out_ready, gated, x2_ready, x2_sq, x2_eps = sem("out_ready"), sem("gated"), sem("x2_ready"), sem("x2_sq"), sem("x2_eps")
        k.x2_rs = sem("x2_rs")
        kind = lambda t: int(t == CTX)

        with nc.Block() as block:

            @block.sync
            def _(sp):
                for n in range(DC):
                    if n >= 2:
                        sp.wait_ge(wo_ready, n - 1)
                    sp.dma_start(wor[:, n % 2, :], a["w_o"][n]).then_inc(wo_loaded[n % 2], 16)
                    if n % 3 == 1:
                        i = n // 3
                        sp.dma_start(k.x[:, 3 * i:3 * i + 3, :], a["x"][3 * i:3 * i + 3].rearrange("t p d -> p t d")).then_inc(x_loaded[i], 16)

            @block.gpsimd
            def _(pool):
                def mixer(t):
                    cut = slice(t * P, (t + 1) * P)
                    if t >= 2:
                        pool.wait_ge(out_ready, t - 1)
                    v = [m[:, t % 2, :, :] for m in mT]
                    nc.gpsimd.tensor_copy(v[0], k.mixT[:, :, cut]).then_inc(m_hi, 1)
                    pool.wait_ge(m_hi, t + 1)
                    nc.gpsimd.tensor_tensor(v[1], k.mixT[:, :, cut], v[0].bitcast(F32), ALU.subtract).then_inc(m_ready, 1)

                def residual(t):
                    pool.wait_ge(x_loaded[t // 3], 16)
                    for i in range(2):
                        cut = slice(i * 512, (i + 1) * 512)
                        pool.wait_ge(gated, 2 * t + i + 1)
                        nc.gpsimd.tensor_tensor(k.x[:, t, cut], k.x[:, t, cut], add[:, i, :], ALU.add).then_inc(x2_ready, 1)
                    pool.wait_ge(x2_sq, t + 1)
                    nc.gpsimd.tensor_scalar(k.stat[:, t, 4:5], k.stat[:, t, 3:4], EPS, None, ALU.add).then_inc(x2_eps, 1)
                    pool.wait_ge(x2_eps, t + 1)
                    nc.gpsimd.tensor_tensor(k.stat[:, t, 5:6], k.stat[:, t, 4:5], k.nhalf[:, 0:1], ALU.pow).then_inc(k.x2_rs, 1)

                mixer(0)
                for t in range(T):
                    if t + 1 < T:
                        mixer(t + 1)
                    residual(t)

            @block.scalar
            def _(act):
                def turned(t):
                    if t >= 2:
                        act.wait_ge(out_ready, t - 1)
                    nc.scalar.activation(aT[0][:, t % 2, :, :], k.attn[:, :, t * P:(t + 1) * P], ACT.Copy).then_inc(a_hi, 1)

                turned(0)
                for n in range(DC):
                    act.wait_ge(wo_loaded[n % 2], 16 * (n // 2 + 1))
                    nc.scalar.activation(wo[0][:, n, :], wor[:, n % 2, :], ACT.Copy).then_inc(wo_hi, 1)
                    if n < 2:
                        read_gate(nc, act, gate[:, n, :], [bank[4 + 2 * n], bank[5 + 2 * n]], gate_ready, gate_done, n)
                for t in range(T):
                    if t + 1 < T:
                        turned(t + 1)
                    act.wait_ge(x2_ready, 2 * t + 2)
                    if t:
                        act.wait_ge(x2_sq, t)
                    nc.scalar.activation(k.junk[:, :], k.x[:, t, :], ACT.Square, scale=1.0 / 32.0,
                                         accum_out=k.stat[:, t, 3:4]).then_inc(x2_sq, 1)
                    if 0 <= t - 2 < BLK:
                        for q in range(2):
                            modulate_half(nc, act, k, 2 * (t - 2) + q, bank[6 + q])

            @block.vector
            def _(dve):
                def turned(t):
                    dve.wait_ge(a_hi, t + 1)
                    nc.vector.tensor_tensor(aT[1][:, t % 2, :, :], k.attn[:, :, t * P:(t + 1) * P], aT[0][:, t % 2, :, :].bitcast(F32),
                                            ALU.subtract).then_inc(a_ready, 1)

                turned(0)
                for j in range(2):
                    nc.vector.scalar_tensor_tensor(k.gain2[:, :, j], k.mod[:, 4 * DC:5 * DC, j], 1.0, k.cols[:, C_N2:C_N2 + DC],
                                                   ALU.add, ALU.mult).then_inc(gain2_done, 1)
                for n in range(DC):
                    dve.wait_ge(wo_hi, n + 1)
                    nc.vector.tensor_tensor(wo[1][:, n, :], wor[:, n % 2, :], wo[0][:, n, :].bitcast(F32),
                                            ALU.subtract).then_inc(wo_ready, 1)
                dve.wait_ge(gate_done, 2)
                for t in range(T):
                    if t + 1 < T:
                        turned(t + 1)
                    dve.wait_ge(out_ready, t + 1)
                    for i in range(2):
                        cut = slice(i * 512, (i + 1) * 512)
                        if t:
                            dve.wait_ge(x2_ready, 2 * t + i - 1)
                        nc.vector.tensor_tensor(add[:, i, :], bank[2 + 2 * (t % 2) + i][:, :], gate[:, kind(t), cut],
                                                ALU.mult).then_inc(gated, 1)
                    if 0 <= t - 1 < BLK:
                        normed_again(nc, dve, k, t - 1)
                    if 0 <= t - 2 < BLK:
                        for q in range(2):
                            split_half(nc, dve, k, 2 * (t - 2) + q)

            @block.tensor
            def _(pe):
                for n in range(2):
                    spread_gate(nc, pe, k, 2, n, [bank[4 + 2 * n], bank[5 + 2 * n]], gate_ready)
                for t in range(T):
                    pe.wait_ge(a_ready, t + 1)
                    pe.wait_ge(m_ready, t + 1)
                    if t == 1:
                        pe.wait_ge(gate_done, 2)
                    if t >= 2:
                        pe.wait_ge(gated, 2 * t - 2)
                    b = [bank[2 + 2 * (t % 2) + i] for i in range(2)]
                    for c in range(DC):
                        if t == 0:
                            pe.wait_ge(wo_ready, c + 1)
                        src = aT if c < 4 else mT
                        for x, y in ((0, 0), (0, 1), (1, 0)):
                            first, last = c == 0 and (x, y) == (0, 0), c == DC - 1 and (x, y) == (1, 0)
                            for i in range(2):
                                op = nc.tensor.matmul(b[i][:, :], src[x][:, t % 2, c % 4, :],
                                                      wo[y][:, c, i * 512:(i + 1) * 512], start=first, stop=last)
                    op.then_inc(out_ready, 1)
                    if 0 <= t - 2 < BLK:
                        if t == 2:
                            pe.wait_ge(gate_done, 2)
                        else:
                            pe.wait_ge(k.hf_ready, 2 * (t - 2))
                        for q in range(2):
                            turn_half(nc, pe, k, 2 * (t - 2) + q, bank[6 + q])


def mlp_phase(nc, a, k):
    with ExitStack() as ctx:
        sb, sem = memory(nc, ctx), signals(nc, ctx)
        bank = k.bank
        k.h2.append([sb(f"h2{x}1", [P, DC, BN], F32R) for x in "hl"])
        raw = [[sb(f"w{m}raw{s}", [P, D]) for s in range(4)] for m in (1, 2)]
        w = [[[sb(f"w{m}{x}{s}", [P, D], F32R) for x in "hl"] for s in range(2)] for m in (1, 2)]
        relu = [sb(f"relu{s}", [P, BN]) for s in range(2)]
        sq = [sb(f"sq{s}", [P, BN]) for s in range(2)]
        rT = [[sb(f"rT{x}{s}", [P, BN], F32R) for x in "hl"] for s in range(2)]
        add = sb("add2", [P, 2, 512])
        fnorm = sb("fnorm", [P, D])
        gate = sb("gate2", [P, 2, D])
        gate_ready, gate_done = sem("gate2_ready"), sem("gate2_done")
        loaded = [[sem(f"w{m}_loaded{s}") for s in range(4)] for m in (1, 2)]
        w_hi = [sem("w1_hi"), sem("w2_hi")]
        w_ready = [sem("w1_ready"), sem("w2_ready")]
        fn_loaded = sem("fn_loaded")
        hid_done, relu_done, sq_done, r_hi, r_ready = sem("hid_done"), sem("relu_done"), sem("sq_done"), sem("r_hi"), sem("r_ready")
        down_done, out_gated, out_added = sem("down_done"), sem("out_gated"), sem("out_added")
        y_sq, y_eps, y_rs, y_ready = sem("y_sq"), sem("y_eps"), sem("y_rs"), sem("y_ready")
        stored = [sem(f"y_stored{s}") for s in range(2)]
        kind = lambda t: int(t == CTX)
        HALVES, PEEL = 2 * BLK, 2
        assert 4 * PEEL > HALVES

        with nc.Block() as block:

            @block.sync
            def _(sp):
                def load(g, f, j):
                    for m in range(2):
                        sp.dma_start(raw[m][j][:, :], a[("w1", "w2")[m]][f]).then_inc(loaded[m][j], 16)

                sp.dma_start(fnorm[:], a["final_norm_row"]).then_inc(fn_loaded, 16)
                for j in range(4):
                    load(j, j, j)
                for b in range(NB):
                    with sp.Fori(1 if b == 0 else 0, FC // 4) as i:
                        for j in range(4):
                            sp.wait_ge(w_ready[0], 4 * i + (FC * b + j - 3))
                            sp.wait_ge(w_ready[1], 4 * i + (FC * b + j - 3))
                            load(None, 4 * i + j, j)

            @block.gpsimd
            def _(pool):
                for b in range(NB):
                    tiles = range(BLK * b, BLK * (b + 1))
                    for t in tiles:
                        for i in range(2):
                            n = 2 * t + i
                            cut = slice(i * 512, (i + 1) * 512)
                            pool.wait_ge(out_gated, n + 1)
                            nc.gpsimd.tensor_tensor(k.x[:, t, cut], k.x[:, t, cut], add[:, i, :], ALU.add).then_inc(out_added, 1)
                    for t in tiles:
                        pool.wait_ge(y_sq, t + 1)
                        nc.gpsimd.tensor_scalar(k.stat2[:, t, 1:2], k.stat2[:, t, 0:1], EPS, None, ALU.add).then_inc(y_eps, 1)
                        pool.wait_ge(y_eps, t + 1)
                        nc.gpsimd.tensor_tensor(k.stat2[:, t, 2:3], k.stat2[:, t, 1:2], k.nhalf[:, 0:1], ALU.pow).then_inc(y_rs, 1)
                    for t in tiles:
                        pool.wait_ge(y_ready, t + 1)
                        pool.dma_start(a["y"][t], k.x[:, t, :]).then_inc(stored[t % 2], 16)
                pool.wait_ge(stored[0], 16 * ((T + 1) // 2))
                pool.wait_ge(stored[1], 16 * (T // 2))

            @block.scalar
            def _(act):
                def split_hi(m, slot, rslot, use):
                    act.wait_ge(loaded[m][rslot], use)
                    nc.scalar.activation(w[m][slot][0][:, :], raw[m][rslot][:, :], ACT.Copy).then_inc(w_hi[m], 1)

                split_hi(0, 0, 0, 16)
                split_hi(0, 1, 1, 16)
                split_hi(1, 0, 0, 16)
                for n in range(2):
                    read_gate(nc, act, gate[:, n, :], bank[2 * n:2 * n + 2], gate_ready, gate_done, n)

                def step(b, i, j, first=False, half=None):
                    g = 4 * i + (FC * b + j)
                    s = j % 2
                    act.wait_ge(hid_done, g + 1)
                    nc.scalar.activation(relu[s][:, :], bank[6 + s][:, 0:BN], ACT.Relu).then_inc(relu_done, 1)
                    if half is not None:
                        modulate_half(nc, act, k, half, bank[7 - s])
                    split_hi(0, s, (j + 2) % 4, 16 * i + 16 * ((FC // 4) * b + (j + 2) // 4 + 1))
                    act.wait_ge(sq_done, g + 1)
                    if b or j or not first:
                        act.wait_ge(down_done, g)
                    nc.scalar.activation(rT[s][0][:, :], sq[s][:, :], ACT.Copy).then_inc(r_hi, 1)
                    split_hi(1, 1 - s, (j + 1) % 4, 16 * i + 16 * ((FC // 4) * b + (j + 1) // 4 + 1))

                def last_step(g):
                    s = g % 2
                    act.wait_ge(hid_done, g + 1)
                    nc.scalar.activation(relu[s][:, :], bank[6 + s][:, 0:BN], ACT.Relu).then_inc(relu_done, 1)
                    act.wait_ge(sq_done, g + 1)
                    act.wait_ge(down_done, g)
                    nc.scalar.activation(rT[s][0][:, :], sq[s][:, :], ACT.Copy).then_inc(r_hi, 1)
                    if g + 1 < NB * FC:
                        split_hi(1, 1 - s, (g + 1) % 4, 16 * ((g + 1) // 4 + 1))

                def squares(b):
                    for t in range(BLK * b, BLK * (b + 1)):
                        act.wait_ge(out_added, 2 * t + 2)
                        if t:
                            act.wait_ge(y_sq, t)
                        nc.scalar.activation(k.junk[:, :], k.x[:, t, :], ACT.Square, scale=1.0 / 32.0,
                                             accum_out=k.stat2[:, t, 0:1]).then_inc(y_sq, 1)

                for b in range(NB):
                    final = b == NB - 1
                    for j in range(4):
                        step(b, 0, j, first=b == 0)
                        if b and j == 1:
                            squares(b - 1)
                    with act.Fori(1, FC // 4 - (1 if final else PEEL)) as i:
                        for j in range(4):
                            step(b, i, j)
                    if final:
                        for j in range(2):
                            step(b, FC // 4 - 1, j)
                        for g in range(NB * FC - 2, NB * FC):
                            last_step(g)
                    else:
                        for n in range(4 * PEEL):
                            step(b, FC // 4 - PEEL + n // 4, n % 4, half=HALVES * (b + 1) + n if n < HALVES else None)
                squares(NB - 1)

            @block.vector
            def _(dve):
                def split_lo(m, slot, rslot, n):
                    dve.wait_ge(w_hi[m], n + 1)
                    nc.vector.tensor_tensor(w[m][slot][1][:, :], raw[m][rslot][:, :], w[m][slot][0][:, :].bitcast(F32),
                                            ALU.subtract).then_inc(w_ready[m], 1)

                def step(b, i, j, w1_too=True, w2_too=True):
                    g = 4 * i + (FC * b + j)
                    s = j % 2
                    dve.wait_ge(relu_done, g + 1)
                    nc.vector.tensor_tensor(sq[s][:, :], relu[s][:, :], relu[s][:, :], ALU.mult).then_inc(sq_done, 1)
                    if w1_too:
                        split_lo(0, s, (j + 2) % 4, g + 2)
                    dve.wait_ge(r_hi, g + 1)
                    nc.vector.tensor_tensor(rT[s][1][:, :], sq[s][:, :], rT[s][0][:, :].bitcast(F32), ALU.subtract).then_inc(r_ready, 1)
                    if w2_too:
                        split_lo(1, 1 - s, (j + 1) % 4, g + 1)

                def finish(b):
                    dve.wait_ge(down_done, FC * (b + 1))
                    for t in range(BLK * b, BLK * (b + 1)):
                        for i in range(2):
                            n = 2 * t + i
                            cut = slice(i * 512, (i + 1) * 512)
                            if n >= 2:
                                dve.wait_ge(out_added, n - 1)
                            nc.vector.tensor_tensor(add[:, i, :], bank[2 * (t % BLK) + i][:, :], gate[:, kind(t), cut],
                                                    ALU.mult).then_inc(out_gated, 1)

                def last_norm(b):
                    for t in range(BLK * b, BLK * (b + 1)):
                        dve.wait_ge(y_rs, t + 1)
                        nc.vector.scalar_tensor_tensor(k.x[:, t, :], k.x[:, t, :], k.stat2[:, t, 2:3], fnorm[:, :], ALU.mult,
                                                       ALU.mult).then_inc(y_ready, 1)

                split_lo(0, 0, 0, 0)
                split_lo(0, 1, 1, 1)
                split_lo(1, 0, 0, 0)
                for b in range(NB):
                    final = b == NB - 1
                    for j in range(4):
                        step(b, 0, j)
                    if b == 0:
                        dve.wait_ge(fn_loaded, 16)
                        dve.wait_ge(gate_done, 2)
                    else:
                        last_norm(b - 1)
                    with dve.Fori(1, FC // 4 - (1 if final else PEEL)) as i:
                        for j in range(4):
                            step(b, i, j)
                    if final:
                        for j in range(4):
                            step(b, FC // 4 - 1, j, w1_too=j < 2, w2_too=j < 3)
                    else:
                        for n in range(4 * PEEL):
                            if n % 2 == 0 and n < HALVES:
                                normed_again(nc, dve, k, BLK * (b + 1) + n // 2)
                            step(b, FC // 4 - PEEL + n // 4, n % 4)
                            if n < HALVES:
                                split_half(nc, dve, k, HALVES * (b + 1) + n)
                    finish(b)
                last_norm(NB - 1)

            @block.tensor
            def _(pe):
                def up(b, g, s, first=False):
                    pe.wait_ge(w_ready[0], g + 1)
                    if not first:
                        pe.wait_ge(relu_done, g - 1)
                    n = 0
                    for c in range(DC):
                        for x, y_ in ((0, 0), (0, 1), (1, 0)):
                            op = nc.tensor.matmul(bank[6 + s][:, 0:BN], w[0][s][x][:, c * P:(c + 1) * P], k.h2[b % 2][y_][:, c, :],
                                                  start=n == 0, stop=n == 3 * DC - 1)
                            n += 1
                    op.then_inc(hid_done, 1)

                def down(g, s, first=False, last=False):
                    pe.wait_ge(w_ready[1], g + 1)
                    pe.wait_ge(r_ready, g + 1)
                    for i in range(BLK):
                        for n, (x, y_) in enumerate(((0, 0), (0, 1), (1, 0))):
                            for half in range(2):
                                op = nc.tensor.matmul(bank[2 * i + half][:, :], rT[s][x][:, i * P:(i + 1) * P],
                                                      w[1][s][y_][:, half * 512:(half + 1) * 512],
                                                      start=first and n == 0, stop=last and n == 2, skip_group_check=True)
                    op.then_inc(down_done, 1)

                for n in range(2):
                    spread_gate(nc, pe, k, 5, n, bank[2 * n:2 * n + 2], gate_ready)
                for b in range(NB):
                    g0 = FC * b
                    pe.wait_ge(k.h_ready, HALVES * (b + 1))
                    if b:
                        pe.wait_ge(relu_done, g0)
                    up(b, g0, 0, first=True)
                    up(b, g0 + 1, 1, first=True)
                    if b:
                        pe.wait_ge(out_gated, 2 * BLK * b)
                    else:
                        pe.wait_ge(gate_done, 2)
                    down(g0, 0, first=True)
                    peel = 4 * PEEL if b + 1 < NB else 0
                    with pe.Fori(1, (FC - peel) // 2) as i:
                        up(b, 2 * i + g0, 0)
                        down(2 * i + (g0 - 1), 1)
                        up(b, 2 * i + (g0 + 1), 1)
                        down(2 * i + g0, 0)
                    for n in range(peel):
                        g, s = g0 + FC - peel + n, n % 2
                        half = HALVES * (b + 1) + n
                        if 0 < n <= HALVES:
                            pe.wait_ge(k.hf_ready, half)
                        up(b, g, s)
                        if n < HALVES:
                            pe.wait_ge(relu_done, g)
                            turn_half(nc, pe, k, half, bank[7 - s])
                        down(g - 1, 1 - s)
                    down(g0 + FC - 1, 1, last=True)


def rope_tables():
    inv = (1.0 / (np.float32(10000.0) ** (np.arange(8, dtype=np.float32) * np.float32(2.0) / np.float32(16.0)))).astype(np.float32)
    n = np.arange(LAT)
    pos = np.stack([n // GRID_W, n % GRID_W], 1).astype(np.float32)
    ang = (pos[:, :, None] * inv).astype(np.float32)
    cos, sin = np.cos(ang).astype(np.float32), np.sin(ang).astype(np.float32)
    cos = np.stack([cos, cos], 2).reshape(LAT, ROPE)
    sin = np.stack([-sin, sin], 2).reshape(LAT, ROPE)
    return cos, sin


def pool_tables():
    def cnt(t, w, n):
        return min(t + w // 2, n) - max(t - w // 2, 0)

    bands = np.zeros((P, BANDS), np.float32)
    inv = np.zeros((4, G, P), np.float32)
    for g, w in enumerate(WINDOWS):
        for v, (t0, n) in enumerate(((0, LAT), (P, LAT), (LAT - P, LAT), (0, P))):
            for t in range(P):
                m = bands[:, (4 * g + v) * P + t]
                m[max(t - w // 2, 0):min(t + w // 2, P)] = 1.0
                m[t] -= cnt(t0 + t, w, n)
                inv[v, g, t] = 1.0 / cnt(t0 + t, w, n)
        at = 4 * G * P + 2 * g * EDGE
        for t in range(EDGE):
            for s in range(P):
                if s - P >= t - w // 2:
                    bands[s, at + t] = 1.0
                if s + P < P - EDGE + t + w // 2:
                    bands[s, at + EDGE + t] = 1.0
    return bands, np.broadcast_to(inv.reshape(4, 1, G * P), (4, P, G * P))


def kernel(x_prompt, x_sample, cache_ckv, cache_krope, c, c_ctx, w_ada, b_ada, norm1, w_in, q_norm, w_qb,
           kv_norm, w_kvb, w_pool, pool_scale, w_o, norm2, w1, w2, final_norm):
    import concourse.bacc as bacc
    from concourse.bass_utils import run_bass_kernel_spmd

    def ar(v):
        return np.asarray(v)

    def feature_cols(v):
        return ar(v).reshape(-1, P).T

    swap = np.arange(ROPE).reshape(2, 2, 8)[:, ::-1].reshape(-1)
    wi = ar(w_in)[0]
    kr0 = QL + KVL
    wi = np.concatenate([wi[:, :kr0 + ROPE], wi[:, kr0:kr0 + ROPE][:, swap], wi[:, kr0 + ROPE:]], 1)
    wq = ar(w_qb)[0].reshape(2, P, H, QK)
    wq = np.concatenate([wq, wq[..., NOPE:][..., swap]], -1).transpose(2, 1, 0, 3).reshape(H, P, 2 * P)
    wkv = ar(w_kvb)[0].reshape(P, H, NOPE + VD)
    cos, sin = rope_tables()
    bands, inv = pool_tables()
    one, zero = np.ones((P, ROPE), np.float32), np.zeros((P, ROPE), np.float32)
    arrays = {
        "x": np.concatenate([ar(x_sample)[0], ar(x_prompt)[0]], 0).reshape(T, P, D),
        "cols": np.concatenate([feature_cols(v) for v in (c, c_ctx, b_ada, norm1, norm2, q_norm, kv_norm, pool_scale)], 1),
        "ident": np.eye(P, dtype=np.float32),
        "pick": np.tile(np.eye(2, dtype=np.float32), (2, 1)),
        "w_ada": ar(w_ada)[0].reshape(4, 2, P, 12, 512).transpose(3, 0, 2, 1, 4).reshape(ADA_BLOCKS, P, D),
        "w_in": wi.reshape(DC, P, INC),
        "w_head": np.concatenate([wq, wkv[:, :, :NOPE].transpose(1, 0, 2)], -1),
        "w_v": wkv[:, :, NOPE:].reshape(P, H * VD),
        "w_pool": ar(w_pool)[0].transpose(1, 0, 2).reshape(P, G * P),
        "bands": bands,
        "inv_count": inv,
        "ropek": np.stack([cos.reshape(LT, P, ROPE), sin.reshape(LT, P, ROPE)]).transpose(2, 0, 1, 3).reshape(P, -1),
        "ropeq": np.concatenate([np.concatenate([cos, one]).T, np.concatenate([sin, zero]).T], 0),
        "kv_norm_row": np.broadcast_to(ar(kv_norm)[0], (P, KVL)),
        "cache": np.concatenate([ar(cache_ckv)[0, 0], ar(cache_krope)[0, 0]], 1),
        "w_o": ar(w_o)[0].reshape(DC, P, D),
        "w1": ar(w1)[0].reshape(DC, P, FC, P).transpose(2, 1, 0, 3).reshape(FC, P, D),
        "w2": ar(w2)[0].reshape(FC, P, D),
        "final_norm_row": np.broadcast_to(ar(final_norm), (P, D)),
    }
    arrays = {n: np.ascontiguousarray(v) for n, v in arrays.items()}
    nc = bacc.Bacc("TRN2", target_bir_lowering=False, num_devices=1)
    aps = {n: nc.dram_tensor(f"in_{n}", v.shape, mybir.dt.from_np(v.dtype), kind="ExternalInput").ap() for n, v in arrays.items()}
    for n, shape in (("y", (T, P, D)), ("new_ckv", (P, KVL)), ("new_krope", (P, ROPE))):
        aps[n] = nc.dram_tensor(f"out_{n}", shape, F32, kind="ExternalOutput").ap()
    build(nc, aps)
    got = run_bass_kernel_spmd(nc, [{f"in_{n}": v for n, v in arrays.items()}], core_ids=[0]).results[0]
    y = got["out_y"]
    return (y[CTX][None], y[:LT].reshape(1, LAT, D), got["out_new_ckv"][None, None], got["out_new_krope"][None, None])
```

```python
from contextlib import ExitStack

import concourse.bass as bass
import numpy as np
from concourse import mybir

F32 = mybir.dt.float32
F32R = mybir.dt.float32r
BF16 = mybir.dt.bfloat16
ACT = mybir.ActivationFunctionType
ALU = mybir.AluOpType
AX_X = mybir.AxisListType.X

P = 128
D = 1024
DC = D // P
LAT = 1024
LT = LAT // P
T = LT + 1
CTX = LT
CACHE = LT + 1
NTOK = T * P
NKEY = LAT + 2 * P
LKEY = LAT + P
H = 8
NOPE, ROPE, VD = 64, 32, 64
QK = NOPE + ROPE
QL, KVL = 256, 128
POOLW = 512
G = 4
WINDOWS = (2, 4, 8, 16)
EDGE = max(WINDOWS) // 2
PA = QL + KVL + 2 * ROPE
INC = PA + POOLW
FC = 4 * D // P
BLK = 3
NB = T // BLK
BN = BLK * P
EPS = 1e-6
SCALE = 1.0 / float(np.sqrt(QK))
GRID_W = 64
WH = 2 * P + NOPE
ADA_BLOCKS = 6 * DC

C_C, C_BADA, C_N1, C_N2, C_QN, C_KVN, C_PS = 0, 16, 64, 72, 80, 82, 83
NCOL = 87
BANDS = 4 * G * P + 2 * G * EDGE


def key_col(t):
    return {CTX: LKEY, CACHE: LAT}.get(t, t * P)


class Kept:
    pass


def memory(nc, ctx, side="left"):
    def sb(name, shape, dt=F32):
        return ctx.enter_context(nc.sbuf_tensor(name, shape, dt, side=side))

    return sb


def signals(nc, ctx):
    def sem(name):
        return ctx.enter_context(nc.semaphore(name))

    return sem


def build(nc, a):
    with ExitStack() as whole:
        sb, sem = memory(nc, whole), signals(nc, whole)
        k = Kept()
        k.bank = [whole.enter_context(nc.psum_tensor(f"bank{i}", [P, 512], F32)) for i in range(8)]
        k.cols = sb("cols", [P, NCOL])
        k.ident = sb("ident", [P, P])
        k.identr = sb("identr", [P, P], F32R)
        k.nhalf = sb("nhalf", [P, 2])
        k.mod = sb("mod", [P, ADA_BLOCKS, 2])
        k.silu = sb("silu", [P, DC, 4], F32R)
        k.pick = sb("pick", [4, 2])
        k.stat = sb("stat", [P, T, 6])
        k.stat2 = sb("stat2", [P, T, 6])
        handed = ExitStack()
        sbr = memory(nc, handed, "right")
        k.mixT = sbr("mixT", [P, G, NTOK])
        with ExitStack() as ab:
            sb = memory(nc, ab)
            k.qnT = [sb(f"qnT{x}", [P, 2, NTOK], F32R) for x in "hl"]
            k.ckvT = [sb(f"ckvT{x}", [P, NKEY], F32R) for x in "hl"]
            k.krT = sb("krT", [P, NKEY])
            k.whr = [sb(f"whr{j}", [P, WH]) for j in range(2)]
            k.head_loaded = [sem(f"head_loaded{j}") for j in range(2)]
            project_phase(nc, a, k)
            k.attn = sbr("attn", [P, H * VD // P, NTOK])
            attention_phase(nc, a, k)
        with ExitStack() as rest:
            sb = memory(nc, rest)
            k.x = sb("x", [P, T, D])
            k.junk = sb("junk2", [P, D], BF16)
            k.gain2 = sb("gain2", [P, DC, 2])
            k.xn = sb("xn", [P, 2, D])
            k.hf = sb("h2f", [P, 2, D // 2])
            k.h2 = [[sb(f"h2{x}0", [P, DC, BN], F32R) for x in "hl"]]
            k.xn_ready, k.xT_ready, k.hf_ready = sem("xn2_ready"), sem("x2T_ready"), sem("h2f_ready")
            k.h_hi, k.h_ready = sem("h2_hi"), sem("h2_ready")
            output_phase(nc, a, k)
            handed.close()
            mlp_phase(nc, a, k)


class Modulation:

    def __init__(self, nc, a, k, sb, sem, first, raw_slots, part_slots):
        self.nc, self.a, self.k, self.first = nc, a, k, first
        self.nr, self.np = raw_slots, part_slots
        self.raw = sb(f"ada_raw_{first}", [P, raw_slots, D])
        self.parts = [sb(f"ada{x}_{first}", [P, part_slots, D], F32R) for x in "hl"]
        self.rows = sb(f"ada_rows_{first}", [4, 512 * (4 if first == 0 else 1)])
        self.loaded = [sem(f"ada_loaded{s}_{first}") for s in range(raw_slots)]
        self.hi_done = sem(f"ada_hi_{first}")
        self.ready = [sem(f"ada_ready{c}_{first}") for c in range(2)]
        self.done = sem(f"ada_done_{first}")

    def load(self, sp, n):
        if n >= self.nr:
            for c in range(2):
                sp.wait_ge(self.ready[c], n - self.nr + 1)
        s = n % self.nr
        sp.dma_start(self.raw[:, s, :], self.a["w_ada"][self.first + n]).then_inc(self.loaded[s], 16)

    def high(self, act, n):
        act.wait_ge(self.loaded[n % self.nr], 16 * (n // self.nr + 1))
        if n >= self.np:
            act.wait_ge(self.done, n - self.np + 1)
        self.nc.scalar.activation(self.parts[0][:, n % self.np, :], self.raw[:, n % self.nr, :],
                                  ACT.Copy).then_inc(self.hi_done, 1)

    def low(self, eng, n, c):
        cut = slice(c * 512, (c + 1) * 512)
        eng.wait_ge(self.hi_done, n + 1)
        eng.tensor_tensor(self.parts[1][:, n % self.np, cut], self.raw[:, n % self.nr, cut],
                          self.parts[0][:, n % self.np, cut].bitcast(F32), ALU.subtract).then_inc(self.ready[c], 1)

    def multiply(self, pe, n, out):
        for c in range(2):
            pe.wait_ge(self.ready[c], n + 1)
            for x in range(2):
                op = self.nc.tensor.matmul(out[0:4, :], self.k.silu[:, 2 * (n % 4) + c, :],
                                           self.parts[x][:, n % self.np, c * 512:(c + 1) * 512],
                                           start=n % 4 == 0 and c == 0 and x == 0, stop=n % 4 == 3 and c == 1 and x == 1,
                                           skip_group_check=True)
        op.then_inc(self.done, 1)


def project_phase(nc, a, k):
    with ExitStack() as ctx:
        sb, sem = memory(nc, ctx), signals(nc, ctx)
        bank = k.bank
        xin = sb("xin", [P, 2, D])
        k.junk = sb("junk", [P, D], BF16)
        win = [sb(f"win{x}", [P, DC, INC], F32R) for x in "hl"]
        gain1 = sb("gain1", [P, DC, 2])
        hf = sb("hf", [P, D])
        pf = sb("pf", [P, PA])
        sm = sb("sm", [P, QL + KVL + ROPE])
        cin = sb("cin", [P, KVL + ROPE])
        rt = sb("rt", [P, 2, ROPE])
        ropek = sb("ropek", [P, 2, LT, ROPE])
        bandr = sb("bandr", [P, BANDS], F32R)
        invc = sb("invc", [P, 2, G * P])
        wp = [sb(f"wp{x}", [P, G * P], F32R) for x in "hl"]
        kvn = sb("kvn", [P, KVL])
        ckvo = sb("ckvo", [P, KVL])
        es, sf = sb("es", [P, 2 * DC]), sb("sf", [P, 2 * DC])
        junk2 = sb("junk_qk", [P, QL + KVL], BF16)
        with ExitStack() as early:
            wraw = memory(nc, early)("wraw", [P, 2, INC])
            mod = Modulation(nc, a, k, memory(nc, early), sem, 0, 4, 2)
        hT = [sb(f"hT{x}", [P, 2, D], F32R) for x in "hl"]
        us = [sb(f"us{x}", [P, 4, POOLW], F32R) for x in "hl"]
        pooled = sb("pooled", [P, G * P])
        pT = [sb(f"pT{x}", [P, G * P], F32R) for x in "hl"]

        small_loaded, tabs_loaded = sem("small_loaded"), sem("tabs_loaded")
        invc_loaded = [sem(f"invc_loaded{v}") for v in range(2)]
        x_loaded = [sem(f"x_loaded{s}") for s in range(2)]
        raw_loaded = [sem(f"raw_loaded{s}") for s in range(2)]
        raw_hi, raw_done = sem("raw_hi"), sem("raw_done")
        identr_done = sem("identr_done")
        const_done, silu_exp, silu_done, gain_done = sem("const_done"), sem("silu_exp"), sem("silu_done"), sem("gain_done")
        silu_den, silu_f, rows_done, cols_done = sem("silu_den"), sem("silu_f"), sem("rows_done"), sem("cols_done")
        x_sq, x_eps, x_rs, xn_ready = sem("x_sq"), sem("x_eps"), sem("x_rs"), sem("xn_ready")
        xT_ready, hf_ready, h_hi, h_ready = sem("xT_ready"), sem("hf_ready"), sem("h_hi"), sem("h_ready")
        proj_ready, pf_ready, u_hi, u_ready = sem("proj_ready"), sem("pf_ready"), sem("u_hi"), sem("u_ready")
        qk_sq, qk_eps, qk_rs, rope_mul, sm_ready = sem("qk_sq"), sem("qk_eps"), sem("qk_rs"), sem("rope_mul"), sem("sm_ready")
        smT_ready, sm_hi, sm_done = sem("smT_ready"), sem("sm_hi"), sem("sm_done")
        band_ready, pooled_f, pooled_hi, pooled_ready = sem("band_ready"), sem("pooled_f"), sem("pooled_hi"), sem("pooled_ready")
        mix_ready, mix_done = sem("mix_ready"), sem("mix_done")
        ckvo_done, stored = sem("ckvo_done"), sem("stored")

        staged = [(a["w_in"][c], INC, win[0][:, c, :], win[1][:, c, :]) for c in range(DC)]
        third = BANDS // 3
        staged += [(a["bands"][:, i * third:(i + 1) * third], third, bandr[:, i * third:(i + 1) * third], None) for i in range(3)]
        staged += [(a["w_pool"], G * P, wp[0][:, :], wp[1][:, :])]
        NS = len(staged)
        AHEAD = 6
        assert NS + AHEAD >= 2 * DC
        kind = lambda t: int(t == CTX)

        def main_band(t, g):
            variant = {0: 0, LT - 1: 2, CTX: 3}.get(t, 1)
            return bandr[:, (4 * g + variant) * P:(4 * g + variant + 1) * P]

        def pool_bank(t):
            return {LT - 1: bank[0], CTX: bank[1]}.get(t, bank[7])

        def side_band(g, after):
            at = 4 * G * P + (2 * g + after) * EDGE
            return bandr[:, at:at + EDGE]

        with nc.Block() as block:

            @block.sync
            def _(sp):
                sp.dma_start(k.cols[:], a["cols"]).then_inc(small_loaded, 16)
                sp.dma_start(k.ident[:], a["ident"]).then_inc(small_loaded, 16)
                sp.dma_start(k.pick[:], a["pick"]).then_inc(small_loaded, 16)
                for t in range(2):
                    sp.dma_start(xin[:, t, :], a["x"][t]).then_inc(x_loaded[t], 16)
                for b in range(NS + AHEAD):
                    if b < 2 * DC:
                        mod.load(sp, b)
                    if b >= AHEAD:
                        n = b - AHEAD
                        if n >= 2:
                            sp.wait_ge(raw_done, n - 1)
                        src, w, _, _ = staged[n]
                        sp.dma_start(wraw[:, n % 2, 0:w], src).then_inc(raw_loaded[n % 2], 16)
                sp.dma_start(ropek[:].rearrange("p a b c -> p (a b c)"), a["ropek"]).then_inc(tabs_loaded, 16)
                sp.dma_start(kvn[:], a["kv_norm_row"]).then_inc(tabs_loaded, 16)
                sp.dma_start(cin[:], a["cache"]).then_inc(tabs_loaded, 16)
                for v in range(2):
                    sp.dma_start(invc[:, v, :], a["inv_count"][v]).then_inc(invc_loaded[v], 16)
                for t in range(2, T):
                    sp.wait_ge(xT_ready, t - 1)
                    sp.dma_start(xin[:, t % 2, :], a["x"][t]).then_inc(x_loaded[t % 2], 16)
                    if t == 6:
                        sp.wait_ge(pooled_f, 1)
                        sp.dma_start(invc[:, 0, :], a["inv_count"][2]).then_inc(invc_loaded[0], 16)
                sp.wait_ge(pooled_f, LT - 1)
                sp.dma_start(invc[:, 1, :], a["inv_count"][3]).then_inc(invc_loaded[1], 16)
                for j in range(2):
                    sp.dma_start(k.whr[j][:, :], a["w_head"][j]).then_inc(k.head_loaded[j], 16)
                sp.wait_ge(pf_ready, T)
                sp.dma_start(a["new_krope"], pf[:, QL + KVL:QL + KVL + ROPE]).then_inc(stored, 16)
                sp.wait_ge(ckvo_done, 1)
                sp.dma_start(a["new_ckv"], ckvo[:]).then_inc(stored, 16)
                sp.wait_ge(stored, 32)

            def rs_qk(pool, t):
                pool.wait_ge(qk_sq, 2 * t + 2)
                pool.tensor_scalar(k.stat2[:, t, 2:4], k.stat2[:, t, 0:2], EPS, None, ALU.add).then_inc(qk_eps, 1)
                pool.wait_ge(qk_eps, t + 1)
                pool.tensor_tensor(k.stat2[:, t, 4:6], k.stat2[:, t, 2:4], k.nhalf[:, 0:2], ALU.pow).then_inc(qk_rs, 1)

            def rs_x(pool, t):
                pool.wait_ge(x_sq, t + 1)
                pool.tensor_scalar(k.stat[:, t, 1:2], k.stat[:, t, 0:1], EPS, None, ALU.add).then_inc(x_eps, 1)
                pool.wait_ge(x_eps, t + 1)
                pool.tensor_tensor(k.stat[:, t, 2:3], k.stat[:, t, 1:2], k.nhalf[:, 0:1], ALU.pow).then_inc(x_rs, 1)

            @block.gpsimd
            def _(pool):
                def split_lo(n):
                    _, w, hi, lo = staged[n]
                    if lo is None:
                        pool.wait_ge(raw_loaded[n % 2], 16 * (n // 2 + 1))
                        nc.gpsimd.tensor_copy(hi, wraw[:, n % 2, 0:w]).then_inc(raw_done, 1)
                    else:
                        pool.wait_ge(raw_hi, sum(x[3] is not None for x in staged[:n + 1]))
                        nc.gpsimd.tensor_tensor(lo, wraw[:, n % 2, 0:w], hi.bitcast(F32), ALU.subtract).then_inc(raw_done, 1)

                pool.memset(k.nhalf[:], -0.5).then_inc(const_done, 1)
                pool.wait_ge(const_done, 1)
                for t in range(2):
                    rs_x(pool, t)
                for n in range(NS):
                    split_lo(n)
                for t in range(T):
                    if t + 2 < T:
                        rs_x(pool, t + 2)
                    rs_qk(pool, t)

            @block.scalar
            def _(act):
                def square(t):
                    act.wait_ge(x_loaded[t % 2], 16 * (t // 2 + 1))
                    if t:
                        act.wait_ge(x_sq, t)
                    nc.scalar.activation(k.junk[:, :], xin[:, t % 2, :], ACT.Square, scale=1.0 / 32.0,
                                         accum_out=k.stat[:, t, 0:1]).then_inc(x_sq, 1)

                def modulate(t):
                    act.wait_ge(xT_ready, t + 1)
                    if t >= 1:
                        act.wait_ge(h_ready, t)
                    for c in range(DC):
                        op = nc.scalar.activation(hf[:, c * P:(c + 1) * P], bank[c // 4][:, (c % 4) * P:(c % 4 + 1) * P],
                                                  ACT.Identity, bias=k.mod[:, c, kind(t):kind(t) + 1],
                                                  scale=gain1[:, c, kind(t):kind(t) + 1])
                    op.then_inc(hf_ready, 1)

                def projected(t):
                    pa, pu = bank[2 + 2 * (t % 2)], bank[3 + 2 * (t % 2)]
                    act.wait_ge(proj_ready, t + 1)
                    if t >= 4:
                        act.wait_ge(band_ready, t - 2)
                    nc.scalar.activation(us[0][:, t % 4, :], pu[:, 0:POOLW], ACT.Copy).then_inc(u_hi, 1)
                    if t >= 1:
                        act.wait_ge(sm_ready, t)
                    nc.scalar.activation(pf[:, :], pa[:, 0:PA], ACT.Copy).then_inc(pf_ready, 1)
                    act.wait_ge(pf_ready, t + 1)
                    if t:
                        act.wait_ge(qk_sq, 2 * t)
                    nc.scalar.activation(junk2[:, 0:QL], pf[:, 0:QL], ACT.Square, scale=1.0 / 16.0,
                                         accum_out=k.stat2[:, t, 0:1]).then_inc(qk_sq, 1)
                    nc.scalar.activation(junk2[:, QL:QL + KVL], pf[:, QL:QL + KVL], ACT.Square, scale=float(KVL) ** -0.5,
                                         accum_out=k.stat2[:, t, 1:2]).then_inc(qk_sq, 1)

                def small_hi(t, n):
                    act.wait_ge(smT_ready, n + 1)
                    at = key_col(t)
                    s = bank[6]
                    if t != CACHE:
                        for c in range(2):
                            nc.scalar.activation(k.qnT[0][:, c, t * P:(t + 1) * P], s[:, c * P:(c + 1) * P], ACT.Copy,
                                                 scale=k.cols[:, C_QN + c:C_QN + c + 1])
                    gain = 1.0 if t == CACHE else k.cols[:, C_KVN:C_KVN + 1]
                    nc.scalar.activation(k.ckvT[0][:, at:at + P], s[:, 2 * P:3 * P], ACT.Copy, scale=gain)
                    nc.scalar.activation(k.krT[NOPE:QK, at:at + P], s[0:ROPE, 3 * P:4 * P], ACT.Copy).then_inc(sm_hi, 1)

                def split_hi(n):
                    _, w, hi, lo = staged[n]
                    if lo is None:
                        return
                    act.wait_ge(raw_loaded[n % 2], 16 * (n // 2 + 1))
                    nc.scalar.activation(hi, wraw[:, n % 2, 0:w], ACT.Copy).then_inc(raw_hi, 1)

                def pooled_high(t):
                    act.wait_ge(pooled_f, t + 1)
                    if t >= 1:
                        act.wait_ge(mix_ready, t)
                    nc.scalar.activation(pT[0][:, :], pooled[:, :], ACT.Copy).then_inc(pooled_hi, 1)

                def mixed(t):
                    act.wait_ge(mix_ready, t + 1)
                    for g in range(G):
                        op = nc.scalar.activation(k.mixT[:, g, t * P:(t + 1) * P], pool_bank(t)[:, g * P:(g + 1) * P], ACT.Copy,
                                                  scale=k.cols[:, C_PS + g:C_PS + g + 1])
                    op.then_inc(mix_done, 1)

                act.wait_ge(small_loaded, 48)
                nc.scalar.activation(es[:, :], k.cols[:, C_C:C_C + 2 * DC], ACT.Exp, scale=-1.0).then_inc(silu_exp, 1)
                square(0)
                square(1)
                for b in range(NS + AHEAD):
                    if b < 2 * DC:
                        mod.high(act, b)
                    if b >= AHEAD:
                        split_hi(b - AHEAD)
                act.wait_ge(gain_done, 4)
                modulate(0)
                for t in range(T):
                    if t + 2 < T:
                        square(t + 2)
                    if t + 1 < T:
                        modulate(t + 1)
                    if t >= 3:
                        mixed(t - 3)
                    projected(t)
                    if t >= 1:
                        small_hi(t - 1, t - 1)
                    if t >= 2:
                        pooled_high(t - 2)
                small_hi(CTX, CTX)
                mixed(T - 3)
                pooled_high(T - 2)
                small_hi(CACHE, T)
                mixed(T - 2)
                pooled_high(T - 1)
                mixed(T - 1)

            @block.vector
            def _(dve):
                def rows(g):
                    dve.wait_ge(mod.done, 4 * g + 4)
                    nc.vector.tensor_copy(mod.rows[:, g * 512:(g + 1) * 512], bank[4 + g][0:4, :]).then_inc(rows_done, 1)

                def normed(t):
                    dve.wait_ge(x_rs, t + 1)
                    nc.vector.tensor_scalar(xin[:, t % 2, :], xin[:, t % 2, :], k.stat[:, t, 2:3], None, ALU.mult).then_inc(xn_ready, 1)

                def h_split(t):
                    dve.wait_ge(hf_ready, t + 1)
                    if t >= 2:
                        dve.wait_ge(proj_ready, t - 1)
                    nc.vector.tensor_copy(hT[0][:, t % 2, :], hf[:, :]).then_inc(h_hi, 1)
                    dve.wait_ge(h_hi, t + 1)
                    nc.vector.tensor_tensor(hT[1][:, t % 2, :], hf[:, :], hT[0][:, t % 2, :].bitcast(F32),
                                            ALU.subtract).then_inc(h_ready, 1)

                def projected(t):
                    pu = bank[3 + 2 * (t % 2)]
                    dve.wait_ge(u_hi, t + 1)
                    nc.vector.tensor_tensor(us[1][:, t % 4, :], pu[:, 0:POOLW], us[0][:, t % 4, :].bitcast(F32),
                                            ALU.subtract).then_inc(u_ready, 1)
                    kv, kr, kw = QL, QL + KVL, QL + KVL + ROPE
                    dve.wait_ge(qk_rs, t + 1)
                    if t >= 1:
                        dve.wait_ge(smT_ready, t)
                    nc.vector.tensor_scalar(sm[:, 0:QL], pf[:, 0:QL], k.stat2[:, t, 4:5], None, ALU.mult)
                    if t == CTX:
                        nc.vector.tensor_scalar(sm[:, kv:kr], pf[:, kv:kr], k.stat2[:, t, 5:6], None,
                                                ALU.mult).then_inc(rope_mul, 1)
                        nc.vector.tensor_copy(sm[:, kr:kr + ROPE], pf[:, kr:kw]).then_inc(sm_ready, 1)
                        dve.wait_ge(rope_mul, LT + 1)
                        nc.vector.tensor_tensor(ckvo[:, :], sm[:, kv:kr], kvn[:, :], ALU.mult).then_inc(ckvo_done, 1)
                        return
                    nc.vector.tensor_scalar(sm[:, kv:kr], pf[:, kv:kr], k.stat2[:, t, 5:6], None, ALU.mult)
                    nc.vector.tensor_tensor(rt[:, 0, :], pf[:, kr:kw], ropek[:, 0, t, :], ALU.mult)
                    nc.vector.tensor_tensor(rt[:, 1, :], pf[:, kw:PA], ropek[:, 1, t, :], ALU.mult).then_inc(rope_mul, 1)
                    dve.wait_ge(rope_mul, t + 1)
                    nc.vector.tensor_tensor(sm[:, kr:kr + ROPE], rt[:, 0, :], rt[:, 1, :], ALU.add).then_inc(sm_ready, 1)

                def small_lo(t, n):
                    dve.wait_ge(sm_hi, n + 1)
                    at = key_col(t)
                    s = bank[6]
                    if t != CACHE:
                        for c in range(2):
                            cut = slice(t * P, (t + 1) * P)
                            nc.vector.scalar_tensor_tensor(k.qnT[1][:, c, cut], s[:, c * P:(c + 1) * P],
                                                           k.cols[:, C_QN + c:C_QN + c + 1],
                                                           k.qnT[0][:, c, cut].bitcast(F32), ALU.mult, ALU.subtract)
                    gain = 1.0 if t == CACHE else k.cols[:, C_KVN:C_KVN + 1]
                    nc.vector.scalar_tensor_tensor(k.ckvT[1][:, at:at + P], s[:, 2 * P:3 * P], gain,
                                                   k.ckvT[0][:, at:at + P].bitcast(F32), ALU.mult,
                                                   ALU.subtract).then_inc(sm_done, 1)

                def pooled_split(t):
                    variant = {0: 0, LT - 1: 2, CTX: 3}.get(t, 1)
                    dve.wait_ge(invc_loaded[variant % 2], 16 * (variant // 2 + 1))
                    dve.wait_ge(band_ready, t + 1)
                    if t >= 1:
                        dve.wait_ge(pooled_ready, t)
                    nc.vector.tensor_tensor(pooled[:, :], pool_bank(t)[:, :], invc[:, variant % 2, :], ALU.mult).then_inc(pooled_f, 1)
                    dve.wait_ge(pooled_hi, t + 1)
                    nc.vector.tensor_tensor(pT[1][:, :], pooled[:, :], pT[0][:, :].bitcast(F32), ALU.subtract).then_inc(pooled_ready, 1)

                dve.wait_ge(small_loaded, 48)
                nc.vector.tensor_copy(k.identr[:, :], k.ident[:, :]).then_inc(identr_done, 1)
                dve.wait_ge(silu_exp, 1)
                nc.vector.tensor_scalar(es[:, :], es[:, :], 1.0, None, ALU.add).then_inc(silu_den, 1)
                dve.wait_ge(silu_den, 1)
                nc.vector.reciprocal(es[:, :], es[:, :]).then_inc(silu_den, 1)
                dve.wait_ge(silu_den, 2)
                nc.vector.tensor_tensor(sf[:, :], k.cols[:, C_C:C_C + 2 * DC], es[:, :], ALU.mult).then_inc(silu_f, 1)
                dve.wait_ge(silu_f, 1)
                for j in range(2):
                    nc.vector.tensor_copy(k.silu[:, :, j], sf[:, j * DC:(j + 1) * DC]).then_inc(silu_f, 1)
                dve.wait_ge(silu_f, 3)
                for j in range(2):
                    nc.vector.tensor_tensor(k.silu[:, :, 2 + j], sf[:, j * DC:(j + 1) * DC], k.silu[:, :, j].bitcast(F32),
                                            ALU.subtract).then_inc(silu_done, 1)
                normed(0)
                normed(1)
                for b in range(2 * DC):
                    for c in range(2):
                        mod.low(nc.vector, b, c)
                    if b > 4 and b % 4 == 1:
                        rows(b // 4 - 1)
                rows(3)
                dve.wait_ge(cols_done, 4)
                for j in range(2):
                    nc.vector.tensor_tensor(k.mod[:, 0:2 * DC, j], bank[2][:, 0:4 * DC].rearrange("p (b j) -> p b j", j=2)[:, :, j],
                                            k.cols[:, C_BADA:C_BADA + 2 * DC], ALU.add).then_inc(gain_done, 1)
                dve.wait_ge(gain_done, 2)
                for j in range(2):
                    nc.vector.scalar_tensor_tensor(gain1[:, :, j], k.mod[:, DC:2 * DC, j], 1.0, k.cols[:, C_N1:C_N1 + DC],
                                                   ALU.add, ALU.mult).then_inc(gain_done, 1)
                dve.wait_ge(tabs_loaded, 48)
                dve.wait_ge(raw_done, NS)
                h_split(0)
                for t in range(T):
                    if t + 1 < T:
                        h_split(t + 1)
                    if t + 2 < T:
                        normed(t + 2)
                    projected(t)
                    if t >= 1:
                        small_lo(t - 1, t - 1)
                    if t >= 2:
                        pooled_split(t - 2)
                small_lo(CTX, CTX)
                pooled_split(T - 2)
                small_lo(CACHE, T)
                pooled_split(T - 1)

            @block.tensor
            def _(pe):
                def turn_x(t):
                    pe.wait_ge(xn_ready, t + 1)
                    if t >= 1:
                        pe.wait_ge(hf_ready, t)
                    for c in range(DC):
                        op = nc.tensor.transpose(bank[c // 4][:, (c % 4) * P:(c % 4 + 1) * P], xin[:, t % 2, c * P:(c + 1) * P], k.ident[:, :])
                    op.then_inc(xT_ready, 1)

                def project(t):
                    pa, pu = bank[2 + 2 * (t % 2)], bank[3 + 2 * (t % 2)]
                    pe.wait_ge(h_ready, t + 1)
                    if t >= 2:
                        pe.wait_ge(pf_ready, t - 1)
                        pe.wait_ge(u_ready, t - 1)
                    for c in range(DC):
                        if c == DC // 2 and t >= 3:
                            mix(t - 3)
                        for x, y in ((0, 0), (0, 1), (1, 0)):
                            w = hT[x][:, t % 2, c * P:(c + 1) * P]
                            first, last = c == 0 and (x, y) == (0, 0), c == DC - 1 and (x, y) == (1, 0)
                            nc.tensor.matmul(pa[:, 0:PA], w, win[y][:, c, 0:PA], start=first, stop=last)
                            op = nc.tensor.matmul(pu[:, 0:POOLW], w, win[y][:, c, PA:INC], start=first, stop=last)
                    op.then_inc(proj_ready, 1)

                def turn_small(t, n):
                    s = bank[6]
                    if n >= 1:
                        pe.wait_ge(sm_done, n)
                    if t == CACHE:
                        pe.wait_ge(tabs_loaded, 48)
                        nc.tensor.transpose(s[:, 2 * P:3 * P], cin[:, 0:KVL], k.ident[:, :])
                        nc.tensor.transpose(s[0:ROPE, 3 * P:4 * P], cin[:, KVL:KVL + ROPE], k.ident[:, :]).then_inc(smT_ready, 1)
                        return
                    pe.wait_ge(sm_ready, t + 1)
                    for c in range(3):
                        nc.tensor.transpose(s[:, c * P:(c + 1) * P], sm[:, c * P:(c + 1) * P], k.ident[:, :])
                    nc.tensor.transpose(s[0:ROPE, 3 * P:4 * P], sm[:, QL + KVL:QL + KVL + ROPE], k.ident[:, :]).then_inc(smT_ready, 1)

                def pool_windows(t):
                    after = t < LT - 1
                    pe.wait_ge(u_ready, t + 1 + after)
                    if t in (LT - 1, CTX):
                        pe.wait_ge(hf_ready, T)
                    elif t >= 1:
                        pe.wait_ge(mix_done, t)
                    first = True
                    for g in range(G):
                        cut = slice(g * P, (g + 1) * P)
                        for x in range(2):
                            op = nc.tensor.matmul(pool_bank(t)[:, g * P:(g + 1) * P], us[x][:, t % 4, cut], main_band(t, g),
                                                  start=first, stop=False, skip_group_check=True)
                            first = False
                            if 0 < t < LT:
                                op = nc.tensor.matmul(pool_bank(t)[:, g * P:g * P + EDGE], us[x][:, (t - 1) % 4, cut], side_band(g, 0),
                                                      start=False, stop=False, skip_group_check=True)
                            if after:
                                op = nc.tensor.matmul(pool_bank(t)[:, (g + 1) * P - EDGE:(g + 1) * P], us[x][:, (t + 1) % 4, cut],
                                                      side_band(g, 1), start=False, stop=False, skip_group_check=True)
                    op.then_inc(band_ready, 1)

                def mix(t):
                    pe.wait_ge(pooled_ready, t + 1)
                    for g in range(G):
                        cut = slice(g * P, (g + 1) * P)
                        for i, (x, y) in enumerate(((0, 0), (0, 1), (1, 0))):
                            op = nc.tensor.matmul(pool_bank(t)[:, cut], wp[x][:, cut], pT[y][:, cut], start=i == 0, stop=i == 2)
                    op.then_inc(mix_ready, 1)

                def columns(g):
                    pe.wait_ge(rows_done, g + 1)
                    for b in range(4 * g, 4 * g + 4):
                        op = nc.tensor.matmul(bank[2][:, 2 * b:2 * b + 2], mod.rows[:, b * P:(b + 1) * P], k.pick[:, :],
                                              start=True, stop=True)
                    op.then_inc(cols_done, 1)

                pe.wait_ge(small_loaded, 48)
                turn_x(0)
                pe.wait_ge(silu_done, 2)
                for b in range(2 * DC):
                    mod.multiply(pe, b, bank[4 + b // 4])
                    if b > 4 and b % 4 == 3:
                        columns(b // 4 - 1)
                columns(3)
                pe.wait_ge(gain_done, 2)
                for t in range(T):
                    if t + 1 < T:
                        turn_x(t + 1)
                    if t == 0:
                        pe.wait_ge(raw_done, NS)
                    project(t)
                    if t >= 1:
                        turn_small(t - 1, t - 1)
                    if t >= 2:
                        pool_windows(t - 2)
                pool_windows(T - 2)
                turn_small(CTX, CTX)
                pool_windows(T - 1)
                mix(T - 3)
                turn_small(CACHE, T)
                mix(T - 2)
                mix(T - 1)


def attention_phase(nc, a, k):
    with ExitStack() as ctx:
        sb, sem = memory(nc, ctx), signals(nc, ctx)
        bank = k.bank
        V = sb("V", [P, LT + 2, H, 2 * VD], F32R)
        kT = [[sb(f"kT{x}{j}", [P, NKEY], F32R) for x in "hl"] for j in range(2)]
        qT = [[sb(f"qT{x}{j}", [P, NTOK], F32R) for x in "hl"] for j in range(2)]
        wh = [[sb(f"wh{x}{j}", [P, WH], F32R) for x in "hl"] for j in range(2)]
        ropeq = sb("ropeq", [P, NTOK])
        q1, q2, qf = sb("q1", [P, BN]), sb("q2", [P, BN]), sb("qf", [P, BN])
        pm, mx, nm = sb("pm", [P, T, 3]), sb("mx", [P, T]), sb("nm", [P, T, 2], F32R)
        pexp = [sb(f"pexp{i}", [P, 512]) for i in range(2)]
        phi = [sb(f"phi{i}", [P, 512], F32R) for i in range(3)]
        plo = [sb(f"plo{i}", [P, 512], F32R) for i in range(3)]
        ones = sb("ones", [P, 2])
        out_h, out_l = sb("out_h", [VD, 512]), sb("out_l", [VD, 512])
        mod = Modulation(nc, a, k, sb, sem, 2 * DC, 1, 1)
        with ExitStack() as early:
            sbe = memory(nc, early)
            wv = [sbe(f"wv{x}", [P, H * VD], F32R) for x in "hl"]
            wvr = sbe("wvr", [P, H * VD])
        psum = [sb(f"psum{i}", [P, 512]) for i in range(2)]
        rsum, rcol = sb("rsum", [VD, 512]), sb("rcol", [P, 4])

        tabq_loaded, wv_loaded = sem("tabq_loaded"), sem("wv_loaded")
        wv_hi, wv_ready, v_hi, setup_a, setup_d, setup_p = sem("wv_hi"), sem("wv_ready"), sem("v_hi"), sem("setup_a"), sem("setup_d"), sem("setup_p")
        wh_hi, wh_ready = sem("wh_hi"), sem("wh_ready")
        ring_filled, ring_freed = sem("ring_filled"), sem("ring_freed")
        q_nope, q_full, q_hi, q_lo, k_hi = sem("q_nope"), sem("q_full"), sem("q_hi"), sem("q_lo"), sem("k_hi")
        max_done, nm_ready, mrow_ready = sem("max_done"), sem("nm_ready"), sem("mrow_ready")
        st_filled, p_exp, p_hi, p_lo = sem("st_filled"), sem("p_exp"), sem("p_hi"), sem("p_lo")
        pv_done, p_summed, sum_ready = sem("pv_done"), sem("p_summed"), sem("sum_ready")
        spread_ready, spread_read, out_low = sem("spread_ready"), sem("spread_read"), sem("out_low")
        inv_done, pv_read, attn_done = sem("inv_done"), sem("pv_read"), sem("attn_done")
        rows_done, cols_done, ada_read = sem("ada_rows_done"), sem("ada_cols_done"), sem("ada_read")

        NV = LT + 2
        S0 = 6
        M0 = S0 + 3 * LT + 1
        RU = M0 + 3
        KCUT = ((0, 512), (512, 1024), (1024, NKEY))
        HALF = LAT // 2
        KT = LKEY // P
        MS = 2 * KT + 1
        assert RU % 3 == 1 and NV % 3 == 1 and MS % 2 == 1

        Q_USE = {0: 0, 2: 1, 4: 2}
        K_USE = {1: 0, 3: 1, 5: 2}

        def ring_at(h, li):
            return li if h == 0 and li < S0 else h * RU + NV + li

        def ring_free(pe, h, li):
            if h == 0 and li < 3:
                return
            before = {0: 1, 1: 4, 2: 4}.get(li - S0 if h == 0 else li, 3)
            pe.wait_ge(ring_freed, ring_at(h, li) - before + 1)

        def ring_full(eng, h, li):
            eng.wait_ge(ring_filled, ring_at(h, li) + 1)

        def step(s):
            if s == MS - 1:
                return LAT, 1, LKEY, CACHE, 0, True
            half, kt = divmod(s, KT)
            return half * HALF, HALF // P, kt * P, kt, kt, kt == KT - 1

        def group(g):
            return 3 * (g // MS) + g % MS // KT

        SIDE = [[li] for li in range(S0)] + [[] for _ in range(S0, MS)]
        for li in range(S0, M0):
            SIDE[S0 + (li - S0) * 9 // (M0 - S0)].append(li)
        SIDE[MS - 3] += [M0, M0 + 1, M0 + 2]
        MOD_AT = {4: 0, 6: 1, 8: 2, 10: 3}
        ROWS_AT, COLS_AT = 12, 13
        SPLIT_HEAD_AT = 12
        SUMS_AFTER = (7, 3, 4)
        SPREAD_AFTER = (8, 4, 5)
        OUT_AFTER = (4, 4, 5)
        HI_LAG, PV_LAG = 1, 3

        def ending(g, after):
            return [g - lag for i, lag in enumerate(after) if g >= lag and step((g - lag) % MS)[-1] and group(g - lag) % 3 == i]

        with nc.Block() as block:

            @block.sync
            def _(sp):
                def load_head(h, j):
                    sp.dma_start(k.whr[j][:, :], a["w_head"][h]).then_inc(k.head_loaded[j], 16)

                def load_ada(h):
                    for i in range(4):
                        mod.load(sp, 4 * h + i)

                sp.dma_start(wvr[:], a["w_v"]).then_inc(wv_loaded, 16)
                sp.dma_start(ropeq[NOPE:P, :], a["ropeq"]).then_inc(tabq_loaded, 16)
                load_ada(0)
                for h in range(1, H):
                    if h + 1 < H:
                        sp.wait_ge(wh_ready, h)
                        load_head(h + 1, (h + 1) % 2)
                    load_ada(h)

            @block.gpsimd
            def _(pool):
                def low_query(h, j, c):
                    cut = slice(c * BN, (c + 1) * BN)
                    pool.wait_ge(q_hi, 3 * h + c + 1)
                    nc.gpsimd.tensor_tensor(qT[j][1][0:QK, cut], qf[0:QK, :], qT[j][0][0:QK, cut].bitcast(F32),
                                            ALU.subtract).then_inc(q_lo, 1)

                def add_up(g):
                    _, nq, _, _, first, last = step(g % MS)
                    n, q = nq * P, group(g)
                    pool.wait_ge(p_exp, g + 3)
                    if first == 0:
                        if q >= 2:
                            pool.wait_ge(sum_ready, q - 1)
                        op = nc.gpsimd.tensor_copy(psum[q % 2][:, 0:n], pexp[g % 2][:, 0:n])
                    else:
                        pool.wait_ge(p_summed, g + 2)
                        op = nc.gpsimd.tensor_tensor(psum[q % 2][:, 0:n], psum[q % 2][:, 0:n], pexp[g % 2][:, 0:n], ALU.add)
                    op.then_inc(p_summed, 1)

                def hand_over(g):
                    q0, nq, _, _, _, _ = step(g % MS)
                    n, h, row = nq * P, g // MS, g // MS % 2 * VD
                    pool.wait_ge(pv_read, group(g) + 1)
                    pool.wait_ge(spread_read, group(g) + 1)
                    nc.gpsimd.tensor_tensor(k.attn[row:row + VD, h // 2, q0:q0 + n], out_h[:, 0:n], rsum[:, 0:n],
                                            ALU.mult).then_inc(attn_done, 1)

                pool.sem_inc(p_summed, 2)
                for j in range(2):
                    nc.gpsimd.memset(kT[j][0][QK:QK + 2, :].bitcast(F32), 1.0).then_inc(setup_p, 1)
                pool.wait_ge(setup_p, 2)
                for c in range(3):
                    low_query(0, 0, c)
                pool.wait_ge(q_lo, 3)
                for g in range(H * MS + 7):
                    h, s = divmod(g, MS)
                    if h < H:
                        add_up(g)
                        if h + 1 < H and s - 1 in Q_USE:
                            pool.wait_ge(p_summed, g + 3)
                            if h or s > min(MOD_AT):
                                pool.wait_ge(mod.ready[1], 4 * h + sum(at < s for at in MOD_AT))
                            low_query(h + 1, (h + 1) % 2, Q_USE[s - 1])
                            pool.wait_ge(q_lo, 3 * (h + 1) + Q_USE[s - 1] + 1)
                        if s in MOD_AT:
                            mod.low(nc.gpsimd, 4 * h + MOD_AT[s], 1)
                    for e in ending(g, [n + 1 for n in SPREAD_AFTER]):
                        if e < H * MS:
                            pool.wait_ge(p_summed, min(g, H * MS - 1) + 3)
                            pool.wait_ge(mod.ready[1], min(4 * h + sum(at <= s for at in MOD_AT), 4 * H))
                            hand_over(e)
                            pool.wait_ge(attn_done, group(e) + 1)

            @block.scalar
            def _(act):
                def split_head(h):
                    j = h % 2
                    act.wait_ge(k.head_loaded[j], 16 * (h // 2 + 1))
                    nc.scalar.activation(wh[j][0][:, :], k.whr[j][:, :], ACT.Copy).then_inc(wh_hi, 1)

                def side(h, j, li):
                    if li in Q_USE:
                        c = Q_USE[li]
                        ring_full(act, h, li)
                        act.wait_ge(q_lo, 3 * h + c)
                        nc.scalar.activation(qf[0:NOPE, :], bank[li % 3][0:NOPE, 0:BN], ACT.Copy).then_inc(q_nope, 1)
                    elif li in K_USE:
                        lo, hi = KCUT[K_USE[li]]
                        ring_full(act, h, li)
                        nc.scalar.activation(kT[j][0][0:NOPE, lo:hi], bank[li % 3][0:NOPE, 0:hi - lo], ACT.Copy).then_inc(k_hi, 1)

                def high_query(h, j, c):
                    act.wait_ge(q_full, 3 * h + c + 1)
                    act.wait_ge(q_nope, 3 * h + c + 1)
                    nc.scalar.activation(qT[j][0][0:QK, c * BN:(c + 1) * BN], qf[0:QK, :], ACT.Copy).then_inc(q_hi, 1)

                def main(h, j, s):
                    _, nq, _, _, _, _ = step(s)
                    n, g = nq * P, MS * h + s
                    slot = g % 2
                    act.wait_ge(st_filled, g + 1)
                    act.wait_ge(p_lo, g + 1)
                    act.wait_ge(p_summed, g + 1)
                    nc.scalar.activation(pexp[slot][:, 0:n], bank[3 + slot][:, 0:n], ACT.Exp, scale=SCALE).then_inc(p_exp, 1)

                def high(g):
                    n = step(g % MS)[1] * P
                    act.wait_ge(p_exp, g + 3)
                    act.wait_ge(pv_done, g + 1)
                    nc.scalar.activation(phi[g % 3][:, 0:n], pexp[g % 2][:, 0:n], ACT.Copy).then_inc(p_hi, 1)

                act.sem_inc(p_exp, 2)
                split_head(0)
                act.wait_ge(wv_loaded, 16)
                nc.scalar.activation(wv[0][:, :], wvr[:, :], ACT.Copy).then_inc(wv_hi, 1)
                split_head(1)
                for li in range(S0):
                    side(0, 0, li)
                    if li in Q_USE:
                        high_query(0, 0, Q_USE[li])
                nc.scalar.activation(kT[0][0][NOPE:QK, :], k.krT[NOPE:QK, :], ACT.Copy).then_inc(setup_a, 1)
                for v in range(NV):
                    act.wait_ge(ring_filled, S0 + v + 1)
                    nc.scalar.activation(V[:, v, :, 0:VD], bank[v % 3][:, :].rearrange("p (h d) -> p h d", h=H),
                                         ACT.Copy).then_inc(v_hi, 1)
                nc.scalar.activation(kT[1][0][NOPE:QK, :], k.krT[NOPE:QK, :], ACT.Copy).then_inc(setup_a, 1)
                for g in range(H * MS + 6):
                    h, s = divmod(g, MS)
                    if h < H:
                        main(h, h % 2, s)
                    if 0 <= g - HI_LAG < H * MS:
                        high(g - HI_LAG)
                    for e in ending(g, OUT_AFTER):
                        if e < H * MS:
                            n, q = step(e % MS)[1] * P, group(e)
                            act.wait_ge(pv_done, e + 4)
                            if q:
                                act.wait_ge(pv_read, q)
                            nc.scalar.activation(out_l[:, 0:n], bank[5 + q % 2][VD:P, 0:n], ACT.Copy).then_inc(out_low, 1)
                    for e in ending(g, SPREAD_AFTER):
                        if e < H * MS:
                            n, q = step(e % MS)[1] * P, group(e)
                            act.wait_ge(spread_ready, q + 1)
                            if q:
                                act.wait_ge(attn_done, q)
                            nc.scalar.activation(rsum[:, 0:n], bank[7][0:VD, 0:n], ACT.Copy).then_inc(spread_read, 1)
                    if h < H:
                        if s == SPLIT_HEAD_AT and h + 2 < H:
                            split_head(h + 2)
                        if h + 1 < H:
                            if s - 1 in Q_USE:
                                high_query(h + 1, (h + 1) % 2, Q_USE[s - 1])
                            for li in SIDE[s]:
                                side(h + 1, (h + 1) % 2, li)
                        if s in MOD_AT:
                            mod.high(act, 4 * h + MOD_AT[s])

            @block.vector
            def _(dve):
                def split_head(h):
                    j = h % 2
                    dve.wait_ge(wh_hi, h + 1)
                    nc.vector.tensor_tensor(wh[j][1][:, :], k.whr[j][:, :], wh[j][0][:, :].bitcast(F32),
                                            ALU.subtract).then_inc(wh_ready, 1)

                def side(h, j, li):
                    b = bank[li % 3]
                    ring_full(dve, h, li)
                    if li in Q_USE:
                        c = Q_USE[li]
                        cut = slice(c * BN, (c + 1) * BN)
                        if c or h:
                            dve.wait_ge(q_full, 3 * h + c)
                            dve.wait_ge(q_lo, 3 * h + c)
                        nc.vector.tensor_tensor(q1[NOPE:QK, :], b[QK:P, 0:BN], ropeq[QK:P, cut], ALU.mult)
                        dve.wait_ge(q_nope, 3 * h + c + 1)
                        nc.vector.tensor_tensor(q2[NOPE:QK, :], b[NOPE:QK, 0:BN], ropeq[NOPE:QK, cut], ALU.mult).then_inc(ring_freed, 1)
                        dve.wait_ge(ring_freed, ring_at(h, li) + 1)
                        nc.vector.tensor_tensor(qf[NOPE:QK, :], q1[NOPE:QK, :], q2[NOPE:QK, :], ALU.add).then_inc(q_full, 1)
                    elif li in K_USE:
                        lo, hi = KCUT[K_USE[li]]
                        dve.wait_ge(k_hi, 3 * h + K_USE[li] + 1)
                        nc.vector.tensor_tensor(kT[j][1][0:NOPE, lo:hi], b[0:NOPE, 0:hi - lo], kT[j][0][0:NOPE, lo:hi].bitcast(F32),
                                                ALU.subtract).then_inc(ring_freed, 1)
                    elif li < M0:
                        qt, c = divmod(li - S0, 3)
                        n = BN if qt < LT else P
                        nc.vector.reduce_max(pm[:, qt, c:c + 1], b[:, 0:n], AX_X).then_inc(ring_freed, 1)
                        if li == M0 - 1:
                            dve.wait_ge(ring_freed, h * RU + (NV + M0))
                            nc.vector.tensor_reduce(mx[:, :], pm[:, :, :], AX_X, ALU.max).then_inc(max_done, 1)
                            dve.wait_ge(max_done, h + 1)
                            nc.vector.tensor_scalar(nm[:, :, 0], mx[:, :], -1.0, None, ALU.mult).then_inc(nm_ready, 1)
                            dve.wait_ge(nm_ready, 2 * h + 1)
                            nc.vector.scalar_tensor_tensor(nm[:, :, 1], mx[:, :], -1.0, nm[:, :, 0].bitcast(F32), ALU.mult,
                                                           ALU.subtract).then_inc(nm_ready, 1)
                    else:
                        c = li - M0
                        nc.vector.tensor_scalar(qT[j][0][QK:QK + 2, c * BN:(c + 1) * BN], b[0:2, 0:BN], 1.0, None,
                                                ALU.mult).then_inc(ring_freed, 1)

                def low(g):
                    n = step(g % MS)[1] * P
                    dve.wait_ge(p_hi, g + 1)
                    nc.vector.tensor_tensor(plo[g % 3][:, 0:n], pexp[g % 2][:, 0:n], phi[g % 3][:, 0:n].bitcast(F32),
                                            ALU.subtract).then_inc(p_lo, 1)

                def invert(g):
                    nq, q = step(g % MS)[1], group(g)
                    dve.wait_ge(sum_ready, q + 1)
                    if q:
                        dve.wait_ge(spread_ready, q)
                    nc.vector.reciprocal(rcol[:, 0:nq], bank[7][:, 0:2 * nq].rearrange("p (i j) -> p i j", j=2)[:, :, 0]).then_inc(inv_done, 1)

                def values(g):
                    n, q = step(g % MS)[1] * P, group(g)
                    dve.wait_ge(out_low, q + 1)
                    if q:
                        dve.wait_ge(attn_done, q)
                    nc.vector.tensor_tensor(out_h[:, 0:n], bank[5 + q % 2][0:VD, 0:n], out_l[:, 0:n], ALU.add).then_inc(pv_read, 1)

                dve.sem_inc(p_lo, 2)
                nc.vector.memset(pm[:, LT, :], -3.0e38).then_inc(setup_d, 1)
                nc.vector.memset(ones[:, :], 1.0).then_inc(setup_d, 1)
                split_head(0)
                dve.wait_ge(wv_hi, 1)
                nc.vector.tensor_tensor(wv[1][:, :], wvr[:, :], wv[0][:, :].bitcast(F32), ALU.subtract).then_inc(wv_ready, 1)
                split_head(1)
                dve.wait_ge(tabq_loaded, 16)
                for li in range(S0):
                    side(0, 0, li)
                dve.wait_ge(setup_a, 1)
                nc.vector.tensor_tensor(kT[0][1][NOPE:QK, :], k.krT[NOPE:QK, :], kT[0][0][NOPE:QK, :].bitcast(F32),
                                    ALU.subtract).then_inc(setup_d, 1)
                for v in range(NV):
                    dve.wait_ge(v_hi, v + 1)
                    nc.vector.tensor_tensor(V[:, v, :, VD:2 * VD], bank[v % 3][:, :].rearrange("p (h d) -> p h d", h=H),
                                            V[:, v, :, 0:VD].bitcast(F32), ALU.subtract).then_inc(ring_freed, 1)
                for li in range(S0, RU):
                    side(0, 0, li)
                dve.wait_ge(setup_a, 2)
                nc.vector.tensor_tensor(kT[1][1][NOPE:QK, :], k.krT[NOPE:QK, :], kT[1][0][NOPE:QK, :].bitcast(F32),
                                    ALU.subtract).then_inc(setup_d, 1)
                for g in range(H * MS + 6):
                    h, s = divmod(g, MS)
                    for e in ending(g, SUMS_AFTER):
                        if e < H * MS:
                            invert(e)
                    now = SIDE[s] if h + 1 < H else []
                    for li in now[:int(s >= S0)]:
                        side(h + 1, (h + 1) % 2, li)
                    if 0 <= g - HI_LAG < H * MS:
                        low(g - HI_LAG)
                    for li in now[int(s >= S0):]:
                        side(h + 1, (h + 1) % 2, li)
                    if h < H:
                        if s in MOD_AT:
                            mod.low(nc.vector, 4 * h + MOD_AT[s], 0)
                        if s == ROWS_AT:
                            dve.wait_ge(mod.done, 4 * h + 4)
                            nc.vector.tensor_copy(mod.rows[:, :], bank[7][0:4, :]).then_inc(rows_done, 1)
                        if s == COLS_AT:
                            dve.wait_ge(cols_done, h + 1)
                            at = 4 * h + 2 * DC
                            for j in range(2):
                                nc.vector.tensor_tensor(k.mod[:, at:at + 4, j],
                                                        bank[7][:, 0:8].rearrange("p (b j) -> p b j", j=2)[:, :, j],
                                                        k.cols[:, C_BADA + at:C_BADA + at + 4], ALU.add).then_inc(ada_read, 1)
                        if s == SPLIT_HEAD_AT and h + 2 < H:
                            split_head(h + 2)
                    for e in ending(g, OUT_AFTER):
                        if e < H * MS:
                            values(e)

            @block.tensor
            def _(pe):
                def side(h, j, li):
                    b = bank[li % 3]
                    if li == 0:
                        pe.wait_ge(wh_ready, h + 1)
                    if S0 <= li < M0 and (li - S0) % (3 * BLK) == 0:
                        pe.wait_ge(q_lo, 3 * h + (li - S0) // (3 * BLK) + 1)
                    if li == S0 and h == 0:
                        pe.wait_ge(setup_d, 3)
                        pe.wait_ge(setup_p, 2)
                    if li == S0 and h == 1:
                        pe.wait_ge(setup_d, 4)
                    if li == S0:
                        pe.wait_ge(ring_freed, h * RU + (NV + max(K_USE) + 1))
                    if li == M0:
                        pe.wait_ge(nm_ready, 2 * h + 2)
                    ring_free(pe, h, li)
                    if li in Q_USE:
                        cut = slice(Q_USE[li] * BN, (Q_USE[li] + 1) * BN)
                        n = 0
                        for c in range(2):
                            for x, y in ((0, 0), (0, 1), (1, 0)):
                                op = nc.tensor.matmul(b[:, 0:BN], wh[j][x][:, c * P:(c + 1) * P], k.qnT[y][:, c, cut],
                                                      start=n == 0, stop=n == 5)
                                n += 1
                    elif li in K_USE:
                        lo, hi = KCUT[K_USE[li]]
                        for n, (x, y) in enumerate(((0, 0), (0, 1), (1, 0))):
                            op = nc.tensor.matmul(b[0:NOPE, 0:hi - lo], wh[j][x][:, 2 * P:WH], k.ckvT[y][:, lo:hi],
                                                  start=n == 0, stop=n == 2)
                    elif li < M0:
                        qt, c = divmod(li - S0, 3)
                        lo, w = (c * BN, BN) if qt < LT else (LKEY, P)
                        for n, (x, y) in enumerate(((0, 0), (0, 1), (1, 0))):
                            op = nc.tensor.matmul(b[:, 0:w], qT[j][x][0:QK, qt * P:(qt + 1) * P], kT[j][y][0:QK, lo:lo + w],
                                                  start=n == 0, stop=n == 2)
                    else:
                        for i in range(3):
                            op = nc.tensor.matmul(b[0:2, i * P:(i + 1) * P], nm[:, 3 * (li - M0) + i, :], k.identr[:, :],
                                                  start=True, stop=True)
                    op.then_inc(ring_filled, 1)

                def scores(h, j, s):
                    q0, nq, k0, _, _, _ = step(s)
                    g = MS * h + s
                    slot = g % 2
                    n = nq * P
                    if s == 0:
                        pe.wait_ge(ring_freed, h * RU + (NV + RU))
                    pe.wait_ge(p_exp, g + 1)
                    b = bank[3 + slot][:, 0:n]
                    nc.tensor.matmul(b, kT[j][0][0:QK + 2, k0:k0 + P], qT[j][0][0:QK + 2, q0:q0 + n], start=True, stop=False)
                    nc.tensor.matmul(b, kT[j][0][0:QK, k0:k0 + P], qT[j][1][0:QK, q0:q0 + n], start=False, stop=False)
                    nc.tensor.matmul(b, kT[j][1][0:QK, k0:k0 + P], qT[j][0][0:QK, q0:q0 + n], start=False, stop=True).then_inc(st_filled, 1)

                def values(g):
                    _, nq, _, vt, pos, last = step(g % MS)
                    n, h, q = nq * P, g // MS, group(g)
                    pe.wait_ge(p_lo, g + 3)
                    if pos == 0 and q >= 2:
                        pe.wait_ge(pv_read, q - 1)
                    b = bank[5 + q % 2][:, 0:n]
                    nc.tensor.matmul(b, V[:, vt, h, :], phi[g % 3][:, 0:n], start=pos == 0, stop=False)
                    nc.tensor.matmul(b, V[:, vt, h, :], plo[g % 3][:, 0:n], start=False, stop=last).then_inc(pv_done, 1)

                def sums(g):
                    _, nq, _, _, _, _ = step(g % MS)
                    h, q = g // MS, group(g)
                    pe.wait_ge(p_summed, g + 3)
                    if q % 3 == 0:
                        pe.wait_ge(ada_read, 2 * h + 2)
                    else:
                        pe.wait_ge(spread_read, q)
                    for i in range(nq):
                        op = nc.tensor.matmul(bank[7][:, 2 * i:2 * i + 2], psum[q % 2][:, i * P:(i + 1) * P], ones[:, :],
                                              start=True, stop=True)
                    op.then_inc(sum_ready, 1)

                def spread(g):
                    nq, q = step(g % MS)[1], group(g)
                    pe.wait_ge(inv_done, q + 1)
                    for i in range(nq):
                        op = nc.tensor.matmul(bank[7][:, i * P:(i + 1) * P], rcol[:, i:i + 1].to_broadcast([P, P]), k.ident[:, :],
                                              start=True, stop=True)
                    op.then_inc(spread_ready, 1)

                pe.sem_inc(pv_done, 3)
                for li in range(S0):
                    side(0, 0, li)
                pe.wait_ge(wv_ready, 1)
                for v in range(NV):
                    at = key_col({LT: CACHE, LT + 1: CTX}.get(v, v))
                    pe.wait_ge(ring_freed, S0 + v - 2)
                    for n, (x, y) in enumerate(((0, 0), (0, 1), (1, 0))):
                        op = nc.tensor.matmul(bank[v % 3][:, :], k.ckvT[x][:, at:at + P], wv[y][:, :], start=n == 0, stop=n == 2)
                    op.then_inc(ring_filled, 1)
                for li in range(S0, RU):
                    side(0, 0, li)
                for g in range(H * MS + 6):
                    h, s = divmod(g, MS)
                    if h < H:
                        scores(h, h % 2, s)
                    for e in ending(g, SPREAD_AFTER):
                        if e < H * MS:
                            spread(e)
                    for e in ending(g, SUMS_AFTER):
                        if e < H * MS:
                            sums(e)
                    if h + 1 < H:
                        for li in SIDE[s]:
                            side(h + 1, (h + 1) % 2, li)
                    if h < H:
                        if s == COLS_AT:
                            pe.wait_ge(rows_done, h + 1)
                            for i in range(4):
                                op = nc.tensor.matmul(bank[7][:, 2 * i:2 * i + 2], mod.rows[:, i * P:(i + 1) * P], k.pick[:, :],
                                                      start=True, stop=True)
                            op.then_inc(cols_done, 1)
                    if 0 <= g - PV_LAG < H * MS:
                        values(g - PV_LAG)
                    if h < H and s - 1 in MOD_AT:
                        if s - 1 == min(MOD_AT) and h:
                            pe.wait_ge(spread_read, 3 * h)
                        mod.multiply(pe, 4 * h + MOD_AT[s - 1], bank[7])


def normed_again(nc, dve, k, t):
    dve.wait_ge(k.x2_rs, t + 1)
    if t >= 2:
        dve.wait_ge(k.xT_ready, 2 * t - 2)
    nc.vector.tensor_scalar(k.xn[:, t % 2, :], k.x[:, t, :], k.stat[:, t, 5:6], None, ALU.mult).then_inc(k.xn_ready, 1)


def turn_half(nc, pe, k, n, out):
    t, q = divmod(n, 2)
    pe.wait_ge(k.xn_ready, t + 1)
    for c in range(4):
        at = (4 * q + c) * P
        op = nc.tensor.transpose(out[:, c * P:(c + 1) * P], k.xn[:, t % 2, at:at + P], k.ident[:, :])
    op.then_inc(k.xT_ready, 1)


def modulate_half(nc, act, k, n, out):
    t, q = divmod(n, 2)
    j = int(t == CTX)
    act.wait_ge(k.xT_ready, n + 1)
    if n >= 2:
        act.wait_ge(k.h_ready, n - 1)
    for c in range(4):
        f = 4 * q + c
        op = nc.scalar.activation(k.hf[:, q, c * P:(c + 1) * P], out[:, c * P:(c + 1) * P], ACT.Identity,
                                  bias=k.mod[:, 3 * DC + f, j:j + 1], scale=k.gain2[:, f, j:j + 1])
    op.then_inc(k.hf_ready, 1)


def split_half(nc, dve, k, n):
    t, q = divmod(n, 2)
    h, at = k.h2[t // BLK % 2], t % BLK * P
    hi, lo = (x[:, 4 * q:4 * q + 4, at:at + P] for x in h)
    v = k.hf[:, q, :].rearrange("p (c n) -> p c n", c=4)
    dve.wait_ge(k.hf_ready, n + 1)
    nc.vector.tensor_copy(hi, v).then_inc(k.h_hi, 1)
    dve.wait_ge(k.h_hi, n + 1)
    nc.vector.tensor_tensor(lo, v, hi.bitcast(F32), ALU.subtract).then_inc(k.h_ready, 1)


def spread_gate(nc, pe, k, section, j, out, ready):
    for c in range(DC):
        op = nc.tensor.matmul(out[c // 4][:, (c % 4) * P:(c % 4 + 1) * P],
                              k.mod[:, section * DC + c, j:j + 1].to_broadcast([P, P]), k.ident[:, :], start=True, stop=True)
    op.then_inc(ready, 1)


def read_gate(nc, act, gate, out, ready, done, n):
    act.wait_ge(ready, n + 1)
    for i in range(2):
        op = nc.scalar.activation(gate[:, i * 512:(i + 1) * 512], out[i][:, :], ACT.Copy)
    op.then_inc(done, 1)


def output_phase(nc, a, k):
    with ExitStack() as ctx:
        sb, sem = memory(nc, ctx), signals(nc, ctx)
        bank = k.bank
        wo = [sb(f"wo{x}", [P, DC, D], F32R) for x in "hl"]
        aT = [sb(f"aT{x}", [P, 2, 4, P], F32R) for x in "hl"]
        mT = [sb(f"mT{x}", [P, 2, 4, P], F32R) for x in "hl"]
        add = sb("add", [P, 2, D // 2])
        gate = sb("gate1", [P, 2, D])
        wor = [k.xn[:, 0, :], k.xn[:, 1, :], k.hf[:, :, :].rearrange("p a b -> p (a b)"), add[:, :, :].rearrange("p a b -> p (a b)")]
        NW = len(wor)
        x_loaded = [sem(f"res_loaded{i}") for i in range(3)]
        wo_loaded = [sem(f"wo_loaded{i}") for i in range(NW)]
        wo_hi, wo_ready = sem("wo_hi"), sem("wo_ready")
        gate_ready, gate_done, gain2_done = sem("gate_ready"), sem("gate_done"), sem("gain2_done")
        a_hi, a_ready, m_hi, m_ready = sem("a_hi"), sem("a_ready"), sem("m_hi"), sem("m_ready")
        out_ready, gated, x2_ready, x2_sq, x2_eps = sem("out_ready"), sem("gated"), sem("x2_ready"), sem("x2_sq"), sem("x2_eps")
        k.x2_rs = sem("x2_rs")
        kind = lambda t: int(t == CTX)

        with nc.Block() as block:

            @block.sync
            def _(sp):
                for n in range(DC):
                    if n >= NW:
                        sp.wait_ge(wo_ready, n - NW + 1)
                    sp.dma_start(wor[n % NW], a["w_o"][n]).then_inc(wo_loaded[n % NW], 16)
                for i in range(3):
                    sp.dma_start(k.x[:, 3 * i:3 * i + 3, :], a["x"][3 * i:3 * i + 3].rearrange("t p d -> p t d")).then_inc(x_loaded[i], 16)

            @block.gpsimd
            def _(pool):
                def mixer(t):
                    cut = slice(t * P, (t + 1) * P)
                    if t >= 2:
                        pool.wait_ge(out_ready, t - 1)
                    v = [m[:, t % 2, :, :] for m in mT]
                    nc.gpsimd.tensor_copy(v[0], k.mixT[:, :, cut]).then_inc(m_hi, 1)
                    pool.wait_ge(m_hi, t + 1)
                    nc.gpsimd.tensor_tensor(v[1], k.mixT[:, :, cut], v[0].bitcast(F32), ALU.subtract).then_inc(m_ready, 1)

                def residual(t):
                    pool.wait_ge(x_loaded[t // 3], 16)
                    for i in range(2):
                        cut = slice(i * 512, (i + 1) * 512)
                        pool.wait_ge(gated, 2 * t + i + 1)
                        nc.gpsimd.tensor_tensor(k.x[:, t, cut], k.x[:, t, cut], add[:, i, :], ALU.add).then_inc(x2_ready, 1)
                    pool.wait_ge(x2_sq, t + 1)
                    nc.gpsimd.tensor_scalar(k.stat[:, t, 4:5], k.stat[:, t, 3:4], EPS, None, ALU.add).then_inc(x2_eps, 1)
                    pool.wait_ge(x2_eps, t + 1)
                    nc.gpsimd.tensor_tensor(k.stat[:, t, 5:6], k.stat[:, t, 4:5], k.nhalf[:, 0:1], ALU.pow).then_inc(k.x2_rs, 1)

                mixer(0)
                for t in range(T):
                    if t + 1 < T:
                        mixer(t + 1)
                    residual(t)

            @block.scalar
            def _(act):
                def turned(t):
                    if t >= 2:
                        act.wait_ge(out_ready, t - 1)
                    nc.scalar.activation(aT[0][:, t % 2, :, :], k.attn[:, :, t * P:(t + 1) * P], ACT.Copy).then_inc(a_hi, 1)

                turned(0)
                for n in range(DC):
                    act.wait_ge(wo_loaded[n % NW], 16 * (n // NW + 1))
                    nc.scalar.activation(wo[0][:, n, :], wor[n % NW], ACT.Copy).then_inc(wo_hi, 1)
                    if n < 2:
                        read_gate(nc, act, gate[:, n, :], [bank[4 + 2 * n], bank[5 + 2 * n]], gate_ready, gate_done, n)
                for t in range(T):
                    if t + 1 < T:
                        turned(t + 1)
                    act.wait_ge(x2_ready, 2 * t + 2)
                    if t:
                        act.wait_ge(x2_sq, t)
                    nc.scalar.activation(k.junk[:, :], k.x[:, t, :], ACT.Square, scale=1.0 / 32.0,
                                         accum_out=k.stat[:, t, 3:4]).then_inc(x2_sq, 1)
                    if 0 <= t - 2 < BLK:
                        for q in range(2):
                            modulate_half(nc, act, k, 2 * (t - 2) + q, bank[6 + q])

            @block.vector
            def _(dve):
                def turned(t):
                    dve.wait_ge(a_hi, t + 1)
                    nc.vector.tensor_tensor(aT[1][:, t % 2, :, :], k.attn[:, :, t * P:(t + 1) * P], aT[0][:, t % 2, :, :].bitcast(F32),
                                            ALU.subtract).then_inc(a_ready, 1)

                turned(0)
                for j in range(2):
                    nc.vector.scalar_tensor_tensor(k.gain2[:, :, j], k.mod[:, 4 * DC:5 * DC, j], 1.0, k.cols[:, C_N2:C_N2 + DC],
                                                   ALU.add, ALU.mult).then_inc(gain2_done, 1)
                for n in range(DC):
                    dve.wait_ge(wo_hi, n + 1)
                    nc.vector.tensor_tensor(wo[1][:, n, :], wor[n % NW], wo[0][:, n, :].bitcast(F32),
                                            ALU.subtract).then_inc(wo_ready, 1)
                dve.wait_ge(gate_done, 2)
                for t in range(T):
                    if t + 1 < T:
                        turned(t + 1)
                    dve.wait_ge(out_ready, t + 1)
                    for i in range(2):
                        cut = slice(i * 512, (i + 1) * 512)
                        if t:
                            dve.wait_ge(x2_ready, 2 * t + i - 1)
                        nc.vector.tensor_tensor(add[:, i, :], bank[2 + 2 * (t % 2) + i][:, :], gate[:, kind(t), cut],
                                                ALU.mult).then_inc(gated, 1)
                    if 0 <= t - 1 < BLK:
                        normed_again(nc, dve, k, t - 1)
                    if 0 <= t - 2 < BLK:
                        for q in range(2):
                            split_half(nc, dve, k, 2 * (t - 2) + q)

            @block.tensor
            def _(pe):
                for n in range(2):
                    spread_gate(nc, pe, k, 2, n, [bank[4 + 2 * n], bank[5 + 2 * n]], gate_ready)
                for t in range(T):
                    pe.wait_ge(a_ready, t + 1)
                    pe.wait_ge(m_ready, t + 1)
                    if t == 1:
                        pe.wait_ge(gate_done, 2)
                    if t >= 2:
                        pe.wait_ge(gated, 2 * t - 2)
                    b = [bank[2 + 2 * (t % 2) + i] for i in range(2)]
                    for c in range(DC):
                        if t == 0:
                            pe.wait_ge(wo_ready, c + 1)
                        src = aT if c < 4 else mT
                        for x, y in ((0, 0), (0, 1), (1, 0)):
                            first, last = c == 0 and (x, y) == (0, 0), c == DC - 1 and (x, y) == (1, 0)
                            for i in range(2):
                                op = nc.tensor.matmul(b[i][:, :], src[x][:, t % 2, c % 4, :],
                                                      wo[y][:, c, i * 512:(i + 1) * 512], start=first, stop=last)
                    op.then_inc(out_ready, 1)
                    if 0 <= t - 2 < BLK:
                        if t == 2:
                            pe.wait_ge(gate_done, 2)
                        else:
                            pe.wait_ge(k.hf_ready, 2 * (t - 2))
                        for q in range(2):
                            turn_half(nc, pe, k, 2 * (t - 2) + q, bank[6 + q])


def mlp_phase(nc, a, k):
    with ExitStack() as ctx:
        sb, sem = memory(nc, ctx), signals(nc, ctx)
        bank = k.bank
        k.h2.append([sb(f"h2{x}1", [P, DC, BN], F32R) for x in "hl"])
        raw = [[sb(f"w{m}raw{s}", [P, D]) for s in range(4)] for m in (1, 2)]
        w = [[[sb(f"w{m}{x}{s}", [P, D], F32R) for x in "hl"] for s in range(2)] for m in (1, 2)]
        relu = [sb(f"relu{s}", [P, BN]) for s in range(2)]
        sq = [sb(f"sq{s}", [P, BN]) for s in range(2)]
        rT = [[sb(f"rT{x}{s}", [P, BN], F32R) for x in "hl"] for s in range(2)]
        add = sb("add2", [P, 2, 512])
        fnorm = sb("fnorm", [P, D])
        gate = sb("gate2", [P, 2, D])
        gate_ready, gate_done = sem("gate2_ready"), sem("gate2_done")
        loaded = [[sem(f"w{m}_loaded{s}") for s in range(4)] for m in (1, 2)]
        w_hi = [sem("w1_hi"), sem("w2_hi")]
        w_ready = [sem("w1_ready"), sem("w2_ready")]
        fn_loaded = sem("fn_loaded")
        hid_done, relu_done, sq_done, r_hi, r_ready = sem("hid_done"), sem("relu_done"), sem("sq_done"), sem("r_hi"), sem("r_ready")
        down_done, out_gated, out_added = sem("down_done"), sem("out_gated"), sem("out_added")
        y_sq, y_eps, y_rs, y_ready = sem("y_sq"), sem("y_eps"), sem("y_rs"), sem("y_ready")
        stored = [sem(f"y_stored{s}") for s in range(2)]
        kind = lambda t: int(t == CTX)
        HALVES, PEEL = 2 * BLK, 2
        assert 4 * PEEL > HALVES

        with nc.Block() as block:

            @block.sync
            def _(sp):
                def load(g, f, j):
                    for m in range(2):
                        sp.dma_start(raw[m][j][:, :], a[("w1", "w2")[m]][f]).then_inc(loaded[m][j], 16)

                for m, j in ((0, 0), (0, 1), (1, 0), (0, 2), (1, 1), (0, 3), (1, 2), (1, 3)):
                    sp.dma_start(raw[m][j][:, :], a[("w1", "w2")[m]][j]).then_inc(loaded[m][j], 16)
                sp.dma_start(fnorm[:], a["final_norm_row"]).then_inc(fn_loaded, 16)
                for b in range(NB):
                    with sp.Fori(1 if b == 0 else 0, FC // 4) as i:
                        for j in range(4):
                            sp.wait_ge(w_ready[0], 4 * i + (FC * b + j - 3))
                            sp.wait_ge(w_ready[1], 4 * i + (FC * b + j - 3))
                            load(None, 4 * i + j, j)

            @block.gpsimd
            def _(pool):
                for b in range(NB):
                    tiles = range(BLK * b, BLK * (b + 1))
                    for t in tiles:
                        for i in range(2):
                            n = 2 * t + i
                            cut = slice(i * 512, (i + 1) * 512)
                            pool.wait_ge(out_gated, n + 1)
                            nc.gpsimd.tensor_tensor(k.x[:, t, cut], k.x[:, t, cut], add[:, i, :], ALU.add).then_inc(out_added, 1)
                    for t in tiles:
                        pool.wait_ge(y_sq, t + 1)
                        nc.gpsimd.tensor_scalar(k.stat2[:, t, 1:2], k.stat2[:, t, 0:1], EPS, None, ALU.add).then_inc(y_eps, 1)
                        pool.wait_ge(y_eps, t + 1)
                        nc.gpsimd.tensor_tensor(k.stat2[:, t, 2:3], k.stat2[:, t, 1:2], k.nhalf[:, 0:1], ALU.pow).then_inc(y_rs, 1)
                    for t in tiles:
                        pool.wait_ge(y_ready, t + 1)
                        pool.dma_start(a["y"][t], k.x[:, t, :]).then_inc(stored[t % 2], 16)
                pool.wait_ge(stored[0], 16 * ((T + 1) // 2))
                pool.wait_ge(stored[1], 16 * (T // 2))

            @block.scalar
            def _(act):
                def split_hi(m, slot, rslot, use):
                    act.wait_ge(loaded[m][rslot], use)
                    nc.scalar.activation(w[m][slot][0][:, :], raw[m][rslot][:, :], ACT.Copy).then_inc(w_hi[m], 1)

                split_hi(0, 0, 0, 16)
                split_hi(0, 1, 1, 16)
                split_hi(1, 0, 0, 16)
                for n in range(2):
                    read_gate(nc, act, gate[:, n, :], bank[2 * n:2 * n + 2], gate_ready, gate_done, n)

                def step(b, i, j, first=False, half=None):
                    g = 4 * i + (FC * b + j)
                    s = j % 2
                    act.wait_ge(hid_done, g + 1)
                    nc.scalar.activation(relu[s][:, :], bank[6 + s][:, 0:BN], ACT.Relu).then_inc(relu_done, 1)
                    if half is not None:
                        modulate_half(nc, act, k, half, bank[7 - s])
                    split_hi(0, s, (j + 2) % 4, 16 * i + 16 * ((FC // 4) * b + (j + 2) // 4 + 1))
                    act.wait_ge(sq_done, g + 1)
                    if b or j or not first:
                        act.wait_ge(down_done, g)
                    nc.scalar.activation(rT[s][0][:, :], sq[s][:, :], ACT.Copy).then_inc(r_hi, 1)
                    split_hi(1, 1 - s, (j + 1) % 4, 16 * i + 16 * ((FC // 4) * b + (j + 1) // 4 + 1))

                def last_step(g):
                    s = g % 2
                    act.wait_ge(hid_done, g + 1)
                    nc.scalar.activation(relu[s][:, :], bank[6 + s][:, 0:BN], ACT.Relu).then_inc(relu_done, 1)
                    act.wait_ge(sq_done, g + 1)
                    act.wait_ge(down_done, g)
                    nc.scalar.activation(rT[s][0][:, :], sq[s][:, :], ACT.Copy).then_inc(r_hi, 1)
                    if g + 1 < NB * FC:
                        split_hi(1, 1 - s, (g + 1) % 4, 16 * ((g + 1) // 4 + 1))

                def squares(b):
                    for t in range(BLK * b, BLK * (b + 1)):
                        act.wait_ge(out_added, 2 * t + 2)
                        if t:
                            act.wait_ge(y_sq, t)
                        nc.scalar.activation(k.junk[:, :], k.x[:, t, :], ACT.Square, scale=1.0 / 32.0,
                                             accum_out=k.stat2[:, t, 0:1]).then_inc(y_sq, 1)

                for b in range(NB):
                    final = b == NB - 1
                    for j in range(4):
                        step(b, 0, j, first=b == 0)
                        if b and j == 1:
                            squares(b - 1)
                    with act.Fori(1, FC // 4 - (1 if final else PEEL)) as i:
                        for j in range(4):
                            step(b, i, j)
                    if final:
                        for j in range(2):
                            step(b, FC // 4 - 1, j)
                        for g in range(NB * FC - 2, NB * FC):
                            last_step(g)
                    else:
                        for n in range(4 * PEEL):
                            step(b, FC // 4 - PEEL + n // 4, n % 4, half=HALVES * (b + 1) + n if n < HALVES else None)
                squares(NB - 1)

            @block.vector
            def _(dve):
                def split_lo(m, slot, rslot, n):
                    dve.wait_ge(w_hi[m], n + 1)
                    nc.vector.tensor_tensor(w[m][slot][1][:, :], raw[m][rslot][:, :], w[m][slot][0][:, :].bitcast(F32),
                                            ALU.subtract).then_inc(w_ready[m], 1)

                def step(b, i, j, w1_too=True, w2_too=True):
                    g = 4 * i + (FC * b + j)
                    s = j % 2
                    dve.wait_ge(relu_done, g + 1)
                    nc.vector.tensor_tensor(sq[s][:, :], relu[s][:, :], relu[s][:, :], ALU.mult).then_inc(sq_done, 1)
                    if w1_too:
                        split_lo(0, s, (j + 2) % 4, g + 2)
                    dve.wait_ge(r_hi, g + 1)
                    nc.vector.tensor_tensor(rT[s][1][:, :], sq[s][:, :], rT[s][0][:, :].bitcast(F32), ALU.subtract).then_inc(r_ready, 1)
                    if w2_too:
                        split_lo(1, 1 - s, (j + 1) % 4, g + 1)

                def finish(b):
                    dve.wait_ge(down_done, FC * (b + 1))
                    for t in range(BLK * b, BLK * (b + 1)):
                        for i in range(2):
                            n = 2 * t + i
                            cut = slice(i * 512, (i + 1) * 512)
                            if n >= 2:
                                dve.wait_ge(out_added, n - 1)
                            nc.vector.tensor_tensor(add[:, i, :], bank[2 * (t % BLK) + i][:, :], gate[:, kind(t), cut],
                                                    ALU.mult).then_inc(out_gated, 1)

                def last_norm(b):
                    for t in range(BLK * b, BLK * (b + 1)):
                        dve.wait_ge(y_rs, t + 1)
                        nc.vector.scalar_tensor_tensor(k.x[:, t, :], k.x[:, t, :], k.stat2[:, t, 2:3], fnorm[:, :], ALU.mult,
                                                       ALU.mult).then_inc(y_ready, 1)

                split_lo(0, 0, 0, 0)
                split_lo(0, 1, 1, 1)
                split_lo(1, 0, 0, 0)
                for b in range(NB):
                    final = b == NB - 1
                    for j in range(4):
                        step(b, 0, j)
                    if b == 0:
                        dve.wait_ge(fn_loaded, 16)
                        dve.wait_ge(gate_done, 2)
                    else:
                        last_norm(b - 1)
                    with dve.Fori(1, FC // 4 - (1 if final else PEEL)) as i:
                        for j in range(4):
                            step(b, i, j)
                    if final:
                        for j in range(4):
                            step(b, FC // 4 - 1, j, w1_too=j < 2, w2_too=j < 3)
                    else:
                        for n in range(4 * PEEL):
                            if n % 2 == 0 and n < HALVES:
                                normed_again(nc, dve, k, BLK * (b + 1) + n // 2)
                            step(b, FC // 4 - PEEL + n // 4, n % 4)
                            if n < HALVES:
                                split_half(nc, dve, k, HALVES * (b + 1) + n)
                    finish(b)
                last_norm(NB - 1)

            @block.tensor
            def _(pe):
                def up(b, g, s, first=False):
                    pe.wait_ge(w_ready[0], g + 1)
                    if not first:
                        pe.wait_ge(relu_done, g - 1)
                    n = 0
                    for c in range(DC):
                        for x, y_ in ((0, 0), (0, 1), (1, 0)):
                            op = nc.tensor.matmul(bank[6 + s][:, 0:BN], w[0][s][x][:, c * P:(c + 1) * P], k.h2[b % 2][y_][:, c, :],
                                                  start=n == 0, stop=n == 3 * DC - 1)
                            n += 1
                    op.then_inc(hid_done, 1)

                def down(g, s, first=False, last=False):
                    pe.wait_ge(w_ready[1], g + 1)
                    pe.wait_ge(r_ready, g + 1)
                    for i in range(BLK):
                        for n, (x, y_) in enumerate(((0, 0), (0, 1), (1, 0))):
                            for half in range(2):
                                op = nc.tensor.matmul(bank[2 * i + half][:, :], rT[s][x][:, i * P:(i + 1) * P],
                                                      w[1][s][y_][:, half * 512:(half + 1) * 512],
                                                      start=first and n == 0, stop=last and n == 2, skip_group_check=True)
                    op.then_inc(down_done, 1)

                for n in range(2):
                    spread_gate(nc, pe, k, 5, n, bank[2 * n:2 * n + 2], gate_ready)
                for b in range(NB):
                    g0 = FC * b
                    pe.wait_ge(k.h_ready, HALVES * (b + 1))
                    if b:
                        pe.wait_ge(relu_done, g0)
                    up(b, g0, 0, first=True)
                    up(b, g0 + 1, 1, first=True)
                    if b:
                        pe.wait_ge(out_gated, 2 * BLK * b)
                    else:
                        pe.wait_ge(gate_done, 2)
                    down(g0, 0, first=True)
                    peel = 4 * PEEL if b + 1 < NB else 0
                    with pe.Fori(1, (FC - peel) // 2) as i:
                        up(b, 2 * i + g0, 0)
                        down(2 * i + (g0 - 1), 1)
                        up(b, 2 * i + (g0 + 1), 1)
                        down(2 * i + g0, 0)
                    for n in range(peel):
                        g, s = g0 + FC - peel + n, n % 2
                        half = HALVES * (b + 1) + n
                        if 0 < n <= HALVES:
                            pe.wait_ge(k.hf_ready, half)
                        up(b, g, s)
                        if n < HALVES:
                            pe.wait_ge(relu_done, g)
                            turn_half(nc, pe, k, half, bank[7 - s])
                        down(g - 1, 1 - s)
                    down(g0 + FC - 1, 1, last=True)


def rope_tables():
    inv = (1.0 / (np.float32(10000.0) ** (np.arange(8, dtype=np.float32) * np.float32(2.0) / np.float32(16.0)))).astype(np.float32)
    n = np.arange(LAT)
    pos = np.stack([n // GRID_W, n % GRID_W], 1).astype(np.float32)
    ang = (pos[:, :, None] * inv).astype(np.float32)
    cos, sin = np.cos(ang).astype(np.float32), np.sin(ang).astype(np.float32)
    cos = np.stack([cos, cos], 2).reshape(LAT, ROPE)
    sin = np.stack([-sin, sin], 2).reshape(LAT, ROPE)
    return cos, sin


def pool_tables():
    def cnt(t, w, n):
        return min(t + w // 2, n) - max(t - w // 2, 0)

    bands = np.zeros((P, BANDS), np.float32)
    inv = np.zeros((4, G, P), np.float32)
    for g, w in enumerate(WINDOWS):
        for v, (t0, n) in enumerate(((0, LAT), (P, LAT), (LAT - P, LAT), (0, P))):
            for t in range(P):
                m = bands[:, (4 * g + v) * P + t]
                m[max(t - w // 2, 0):min(t + w // 2, P)] = 1.0
                m[t] -= cnt(t0 + t, w, n)
                inv[v, g, t] = 1.0 / cnt(t0 + t, w, n)
        at = 4 * G * P + 2 * g * EDGE
        for t in range(EDGE):
            for s in range(P):
                if s - P >= t - w // 2:
                    bands[s, at + t] = 1.0
                if s + P < P - EDGE + t + w // 2:
                    bands[s, at + EDGE + t] = 1.0
    return bands, np.broadcast_to(inv.reshape(4, 1, G * P), (4, P, G * P))


def kernel(x_prompt, x_sample, cache_ckv, cache_krope, c, c_ctx, w_ada, b_ada, norm1, w_in, q_norm, w_qb,
           kv_norm, w_kvb, w_pool, pool_scale, w_o, norm2, w1, w2, final_norm):
    import concourse.bacc as bacc
    from concourse.bass_utils import run_bass_kernel_spmd

    def ar(v):
        return np.asarray(v)

    def feature_cols(v):
        return ar(v).reshape(-1, P).T

    swap = np.arange(ROPE).reshape(2, 2, 8)[:, ::-1].reshape(-1)
    wi = ar(w_in)[0]
    kr0 = QL + KVL
    wi = np.concatenate([wi[:, :kr0 + ROPE], wi[:, kr0:kr0 + ROPE][:, swap], wi[:, kr0 + ROPE:]], 1)
    wq = ar(w_qb)[0].reshape(2, P, H, QK)
    wq = np.concatenate([wq, wq[..., NOPE:][..., swap]], -1).transpose(2, 1, 0, 3).reshape(H, P, 2 * P)
    wkv = ar(w_kvb)[0].reshape(P, H, NOPE + VD)
    cos, sin = rope_tables()
    bands, inv = pool_tables()
    one, zero = np.ones((P, ROPE), np.float32), np.zeros((P, ROPE), np.float32)
    arrays = {
        "x": np.concatenate([ar(x_sample)[0], ar(x_prompt)[0]], 0).reshape(T, P, D),
        "cols": np.concatenate([feature_cols(v) for v in (c, c_ctx, b_ada, norm1, norm2, q_norm, kv_norm, pool_scale)], 1),
        "ident": np.eye(P, dtype=np.float32),
        "pick": np.tile(np.eye(2, dtype=np.float32), (2, 1)),
        "w_ada": ar(w_ada)[0].reshape(4, 2, P, 12, 512).transpose(3, 0, 2, 1, 4).reshape(ADA_BLOCKS, P, D),
        "w_in": wi.reshape(DC, P, INC),
        "w_head": np.concatenate([wq, wkv[:, :, :NOPE].transpose(1, 0, 2)], -1),
        "w_v": wkv[:, :, NOPE:].reshape(P, H * VD),
        "w_pool": ar(w_pool)[0].transpose(1, 0, 2).reshape(P, G * P),
        "bands": bands,
        "inv_count": inv,
        "ropek": np.stack([cos.reshape(LT, P, ROPE), sin.reshape(LT, P, ROPE)]).transpose(2, 0, 1, 3).reshape(P, -1),
        "ropeq": np.concatenate([np.concatenate([cos, one]).T, np.concatenate([sin, zero]).T], 0),
        "kv_norm_row": np.broadcast_to(ar(kv_norm)[0], (P, KVL)),
        "cache": np.concatenate([ar(cache_ckv)[0, 0], ar(cache_krope)[0, 0]], 1),
        "w_o": ar(w_o)[0].reshape(DC, P, D),
        "w1": ar(w1)[0].reshape(DC, P, FC, P).transpose(2, 1, 0, 3).reshape(FC, P, D),
        "w2": ar(w2)[0].reshape(FC, P, D),
        "final_norm_row": np.broadcast_to(ar(final_norm), (P, D)),
    }
    arrays = {n: np.ascontiguousarray(v) for n, v in arrays.items()}
    nc = bacc.Bacc("TRN2", target_bir_lowering=False, num_devices=1)
    aps = {n: nc.dram_tensor(f"in_{n}", v.shape, mybir.dt.from_np(v.dtype), kind="ExternalInput").ap() for n, v in arrays.items()}
    for n, shape in (("y", (T, P, D)), ("new_ckv", (P, KVL)), ("new_krope", (P, ROPE))):
        aps[n] = nc.dram_tensor(f"out_{n}", shape, F32, kind="ExternalOutput").ap()
    build(nc, aps)
    got = run_bass_kernel_spmd(nc, [{f"in_{n}": v for n, v in arrays.items()}], core_ids=[0]).results[0]
    y = got["out_y"]
    return (y[CTX][None], y[:LT].reshape(1, LAT, D), got["out_new_ckv"][None, None], got["out_new_krope"][None, None])
```
